# Optimizing a Trainium2 kernel written in Bass

```python
import math, functools
import jax, jax.numpy as jnp
from jax import lax
import numpy as np

D_MODEL = 1024
BATCH = 1
SEQ = 256
DEPTH = 1

GRID_W = 64
D_MIX = D_MODEL
HEAD_DIM = 64
N_Q_HEADS = 8
N_KV_HEADS = 2
GQA_GROUP = N_Q_HEADS // N_KV_HEADS
ATTN_W = N_Q_HEADS * HEAD_DIM
KV_W = N_KV_HEADS * HEAD_DIM
LRU_W = D_MIX - ATTN_W
LRU_BLOCKS = 8
LRU_BW = LRU_W // LRU_BLOCKS
LRU_C = 8.0
CONV_W = 4
CONV_PAD_L = 2
ROPE_THETA = 10000.0
ROPE_HALF = HEAD_DIM // 2
Q_BLOCK = 128
N_EXPERTS = 32
TOP_K = 4
D_FF = D_MODEL
SWIGLU_ALPHA = 1.702
SWIGLU_LIMIT = 7.0
MOE_BLOCK = 256
NORM_EPS = 1e-5
IN_W = ATTN_W + 2 * KV_W + 2 * LRU_W


def rms_norm(x, g, eps=NORM_EPS):
    xf = x.astype(jnp.float32)
    y = xf * lax.rsqrt(jnp.mean(xf * xf, axis=-1, keepdims=True) + eps)
    return (y * g.astype(jnp.float32)).astype(x.dtype)

def rope_1d(x, pos):
    m = x.shape[-1] // 2
    inv_freq = ROPE_THETA ** (-jnp.arange(m, dtype=jnp.float32) / m)
    ang = pos.astype(jnp.float32)[:, None] * inv_freq[None, :]
    cos = jnp.cos(ang)[None, :, None, :]
    sin = jnp.sin(ang)[None, :, None, :]
    xf = x.astype(jnp.float32)
    x1, x2 = xf[..., :m], xf[..., m:]
    out = jnp.concatenate([x1 * cos - x2 * sin, x2 * cos + x1 * sin], axis=-1)
    return out.astype(x.dtype)

def rope_axial_2d(x, rows, cols):
    return jnp.concatenate([rope_1d(x[..., :ROPE_HALF], rows),
                            rope_1d(x[..., ROPE_HALF:], cols)], axis=-1)

def block_attention(q, k, v):
    B, S = q.shape[0], q.shape[1]
    nblk = S // Q_BLOCK
    qb = q.reshape(B, nblk, Q_BLOCK, N_KV_HEADS, GQA_GROUP, HEAD_DIM)
    qb = jnp.moveaxis(qb, 1, 0)
    scale = HEAD_DIM ** -0.5

    def one_block(qi):
        s = jnp.einsum('bqkgd,bskd->bkgqs', qi, k).astype(jnp.float32) * scale
        p = jax.nn.softmax(s, axis=-1).astype(v.dtype)
        return jnp.einsum('bkgqs,bskd->bqkgd', p, v)

    o = lax.map(one_block, qb)
    return jnp.moveaxis(o, 0, 1).reshape(B, S, ATTN_W)

def centred_depthwise_conv(u, w, b):
    S = u.shape[1]
    up = jnp.pad(u, ((0, 0), (CONV_PAD_L, CONV_W - 1 - CONV_PAD_L), (0, 0)))
    acc = b
    for j in range(CONV_W):
        acc = acc + up[:, j:j + S, :] * w[j]
    return acc

def _lin_combine(c1, c2):
    a1, b1 = c1
    a2, b2 = c2
    return a1 * a2, a2 * b1 + b2

def rglru_direction(xc, wa, ba, wi, bi, lam, reverse):
    B, S, _ = xc.shape
    xb = xc.reshape(B, S, LRU_BLOCKS, LRU_BW)
    r = jax.nn.sigmoid((jnp.einsum('bsni,nij->bsnj', xb, wa).reshape(B, S, LRU_W) + ba).astype(jnp.float32))
    i = jax.nn.sigmoid((jnp.einsum('bsni,nij->bsnj', xb, wi).reshape(B, S, LRU_W) + bi).astype(jnp.float32))
    log_a = -LRU_C * r * jax.nn.softplus(-lam.astype(jnp.float32))
    a = jnp.exp(log_a)
    mult = jnp.sqrt(-jnp.expm1(2.0 * log_a))
    bterm = mult * i * xc.astype(jnp.float32)
    _, h = lax.associative_scan(_lin_combine, (a, bterm), reverse=reverse, axis=1)
    return h

def moe_ffn(xn, w_router, b_router, w_gate, b_gate, w_up, b_up, w_down, b_down):
    B, S, D = xn.shape
    T = B * S
    xf = xn.reshape(T, D)
    logits = (xf @ w_router + b_router).astype(jnp.float32)
    top_v, top_i = lax.top_k(logits, TOP_K)
    gates = jax.nn.softmax(top_v, axis=-1).astype(xn.dtype)

    TK = T * TOP_K
    flat_e = top_i.reshape(TK).astype(jnp.int32)
    flat_tok = jnp.arange(TK, dtype=jnp.int32) // TOP_K
    flat_g = gates.reshape(TK)
    order = jnp.argsort(flat_e, stable=True)
    sorted_e = flat_e[order]
    counts = jnp.bincount(flat_e, length=N_EXPERTS)
    padded = ((counts + MOE_BLOCK - 1) // MOE_BLOCK) * MOE_BLOCK
    start = jnp.cumsum(counts) - counts
    pend = jnp.cumsum(padded)
    pstart = pend - padded
    dest = pstart[sorted_e] + (jnp.arange(TK, dtype=jnp.int32) - start[sorted_e])

    n_rows = TK + N_EXPERTS * MOE_BLOCK
    n_blocks = n_rows // MOE_BLOCK
    row_tok = jnp.full((n_rows,), T, dtype=jnp.int32).at[dest].set(flat_tok[order])
    row_gate = jnp.zeros((n_rows,), dtype=xn.dtype).at[dest].set(flat_g[order])
    block_e = jnp.searchsorted(pend, jnp.arange(n_blocks) * MOE_BLOCK, side='right')
    block_e = jnp.minimum(block_e, N_EXPERTS - 1).astype(jnp.int32)

    xpad = jnp.concatenate([xf, jnp.zeros((1, D), xf.dtype)], axis=0)
    x_rows = xpad[row_tok].reshape(n_blocks, MOE_BLOCK, D)

    def expert_block(args):
        xb, e = args
        g = xb @ w_gate[e] + b_gate[e]
        u = xb @ w_up[e] + b_up[e]
        g = jnp.minimum(g, SWIGLU_LIMIT)
        u = jnp.clip(u, -SWIGLU_LIMIT, SWIGLU_LIMIT)
        glu = g * jax.nn.sigmoid(SWIGLU_ALPHA * g)
        return ((u + 1.0) * glu) @ w_down[e] + b_down[e]

    y_rows = lax.map(expert_block, (x_rows, block_e)).reshape(n_rows, D)
    y_rows = y_rows * row_gate[:, None]
    out = jax.ops.segment_sum(y_rows, row_tok, num_segments=T + 1)[:T]
    return out.reshape(B, S, D)

def first_inputs(seed: int = 0) -> dict:
    key = jax.random.key(seed)
    ks = jax.random.split(key, 32)
    f32 = jnp.float32
    L = DEPTH

    def nrm(k, shape, fan_in):
        return jax.random.normal(k, shape, f32) * (fan_in ** -0.5)

    def gain(k, shape):
        return 1.0 + 0.05 * jax.random.normal(k, shape, f32)

    def bias(k, shape, s=0.01):
        return s * jax.random.normal(k, shape, f32)

    u = jax.random.uniform(ks[10], (L, 2, LRU_W), f32, minval=0.9, maxval=0.999)
    sgm = u ** (1.0 / LRU_C)
    lru_lam = jnp.log(sgm) - jnp.log1p(-sgm)

    return {
        'x': jax.random.normal(ks[0], (BATCH, SEQ, D_MODEL), f32),
        'norm1_g': gain(ks[1], (L, D_MODEL)),
        'w_in': nrm(ks[2], (L, D_MODEL, IN_W), D_MODEL),
        'q_norm_g': gain(ks[3], (L, HEAD_DIM)),
        'k_norm_g': gain(ks[4], (L, HEAD_DIM)),
        'conv_w': nrm(ks[5], (L, CONV_W, LRU_W), CONV_W),
        'conv_b': bias(ks[6], (L, LRU_W)),
        'lru_wa': nrm(ks[7], (L, 2, LRU_BLOCKS, LRU_BW, LRU_BW), LRU_BW),
        'lru_ba': bias(ks[8], (L, 2, LRU_W), 0.1),
        'lru_wi': nrm(ks[9], (L, 2, LRU_BLOCKS, LRU_BW, LRU_BW), LRU_BW),
        'lru_bi': bias(ks[11], (L, 2, LRU_W), 0.1),
        'lru_lam': lru_lam,
        'attn_out_g': gain(ks[12], (L, ATTN_W)),
        'lru_out_g': gain(ks[13], (L, LRU_W)),
        'w_out': nrm(ks[14], (L, D_MIX, D_MODEL), D_MIX),
        'norm2_g': gain(ks[15], (L, D_MODEL)),
        'w_router': nrm(ks[16], (L, D_MODEL, N_EXPERTS), D_MODEL),
        'b_router': bias(ks[17], (L, N_EXPERTS)),
        'w_gate': nrm(ks[18], (L, N_EXPERTS, D_MODEL, D_FF), D_MODEL),
        'b_gate': bias(ks[19], (L, N_EXPERTS, D_FF)),
        'w_up': nrm(ks[20], (L, N_EXPERTS, D_MODEL, D_FF), D_MODEL),
        'b_up': bias(ks[21], (L, N_EXPERTS, D_FF)),
        'w_down': nrm(ks[22], (L, N_EXPERTS, D_FF, D_MODEL), D_FF),
        'b_down': bias(ks[23], (L, N_EXPERTS, D_MODEL)),
        'final_g': gain(ks[24], (D_MODEL,)),
    }

def first_block(x, norm1_g, w_in, q_norm_g, k_norm_g, conv_w, conv_b, lru_wa, lru_ba,
              lru_wi, lru_bi, lru_lam, attn_out_g, lru_out_g, w_out, norm2_g,
              w_router, b_router, w_gate, b_gate, w_up, b_up, w_down, b_down, final_g):
    B, S, _ = x.shape
    n_rows_grid = S // GRID_W
    rows = jnp.broadcast_to(jnp.arange(n_rows_grid)[:, None], (n_rows_grid, GRID_W)).reshape(S)
    cols = jnp.broadcast_to(jnp.arange(GRID_W)[None, :], (n_rows_grid, GRID_W)).reshape(S)

    for l in range(DEPTH):
        xn = rms_norm(x, norm1_g[l])
        h_in = xn @ w_in[l]
        o0, o1, o2, o3 = ATTN_W, ATTN_W + KV_W, ATTN_W + 2 * KV_W, ATTN_W + 2 * KV_W + LRU_W
        q = h_in[..., :o0].reshape(B, S, N_Q_HEADS, HEAD_DIM)
        k = h_in[..., o0:o1].reshape(B, S, N_KV_HEADS, HEAD_DIM)
        v = h_in[..., o1:o2].reshape(B, S, N_KV_HEADS, HEAD_DIM)
        lru_x = h_in[..., o2:o3]
        lru_gate = h_in[..., o3:]

        q = rope_axial_2d(rms_norm(q, q_norm_g[l], 1e-6), rows, cols)
        k = rope_axial_2d(rms_norm(k, k_norm_g[l], 1e-6), rows, cols)
        attn = block_attention(q, k, v)

        xc = centred_depthwise_conv(lru_x, conv_w[l], conv_b[l])
        h_f = rglru_direction(xc, lru_wa[l, 0], lru_ba[l, 0], lru_wi[l, 0], lru_bi[l, 0],
                              lru_lam[l, 0], False)
        h_b = rglru_direction(xc, lru_wa[l, 1], lru_ba[l, 1], lru_wi[l, 1], lru_bi[l, 1],
                              lru_lam[l, 1], True)
        lru = ((h_f + h_b).astype(x.dtype)) * jax.nn.gelu(lru_gate)

        mixed = jnp.concatenate([rms_norm(attn, attn_out_g[l]),
                                 rms_norm(lru, lru_out_g[l])], axis=-1)
        x = x + mixed @ w_out[l]

        x = x + moe_ffn(rms_norm(x, norm2_g[l]), w_router[l], b_router[l], w_gate[l],
                        b_gate[l], w_up[l], b_up[l], w_down[l], b_down[l])

    return rms_norm(x, final_g)


DEPTH_2 = 2

MEM_LEN = 256
N_EVEN = (DEPTH_2 + 1) // 2
N_ODD = DEPTH_2 // 2
EPS = 1e-6

A_HEADS = 4
A_WIDTH = D_MODEL // 2
HEAD_DIM_2 = A_WIDTH // A_HEADS
IDX_HEADS = 16
IDX_DIM = 64
TOPK_MAX = 256
ROPE_THETA_2 = 500000.0

POOL_WINDOWS = (2, 4, 8, 16)
B_WIDTH = D_MODEL - A_WIDTH
POOL_GROUP = B_WIDTH // len(POOL_WINDOWS)

AB_SIZES = (A_WIDTH, A_WIDTH, A_WIDTH, B_WIDTH, IDX_HEADS * IDX_DIM, IDX_HEADS, IDX_DIM)
IN_AB = sum(AB_SIZES)
AB_SPLITS = [int(s) for s in np.cumsum(AB_SIZES)[:-1]]

D_CONV = D_MODEL
CONV_WIDTH = 31

C_HEADS = 4
C_HEAD_DIM = D_MODEL // C_HEADS

D_FF_2 = -(-8 * D_MODEL // (3 * 256)) * 256


def rmsnorm(x, g):
    xf = x.astype(jnp.float32)
    y = xf * lax.rsqrt(jnp.mean(xf * xf, axis=-1, keepdims=True) + EPS)
    return (y * g.astype(jnp.float32)).astype(x.dtype)

def layernorm(x, g, b):
    xf = x.astype(jnp.float32)
    mu = jnp.mean(xf, axis=-1, keepdims=True)
    var = jnp.mean(jnp.square(xf - mu), axis=-1, keepdims=True)
    y = (xf - mu) * lax.rsqrt(var + EPS)
    return (y * g.astype(jnp.float32) + b.astype(jnp.float32)).astype(x.dtype)

def rope_partial(x, pos):
    d = x.shape[-1]
    rot = d // 4
    half = rot // 2
    inv = ROPE_THETA_2 ** (-jnp.arange(half, dtype=jnp.float32) * 2.0 / rot)
    ang = pos.astype(jnp.float32)[:, None] * inv[None, :]
    cos = jnp.cos(ang)[:, None, :]
    sin = jnp.sin(ang)[:, None, :]
    xf = x.astype(jnp.float32)
    x1, x2, rest = xf[..., :half], xf[..., half:rot], xf[..., rot:]
    out = jnp.concatenate([x1 * cos - x2 * sin, x2 * cos + x1 * sin, rest], axis=-1)
    return out.astype(x.dtype)

def dsa_attention(q, k, v, iq, iw, ik):
    bsz, t_len = q.shape[0], q.shape[1]
    topk = min(TOPK_MAX, t_len // 4)
    n_blocks = t_len // Q_BLOCK
    key_pos = jnp.arange(t_len)
    bidx = jnp.arange(bsz)[:, None, None]
    scale = HEAD_DIM_2 ** -0.5

    def block(i):
        start = i * Q_BLOCK
        qb = lax.dynamic_slice_in_dim(q, start, Q_BLOCK, axis=1)
        iqb = lax.dynamic_slice_in_dim(iq, start, Q_BLOCK, axis=1)
        iwb = lax.dynamic_slice_in_dim(iw, start, Q_BLOCK, axis=1)
        qpos = start + jnp.arange(Q_BLOCK)
        s = jnp.einsum('bqhd,bsd->bqhs', iqb, ik).astype(jnp.float32)
        scores = jnp.einsum('bqhs,bqh->bqs', jax.nn.relu(s), iwb.astype(jnp.float32))
        causal = key_pos[None, :] <= qpos[:, None]
        scores = jnp.where(causal[None], scores, -jnp.inf)
        _, idx = lax.top_k(scores, topk)
        valid = idx <= qpos[None, :, None]
        ks = k[bidx, idx]
        vs = v[bidx, idx]
        logits = jnp.einsum('bqhd,bqkhd->bhqk', qb, ks).astype(jnp.float32) * scale
        logits = jnp.where(valid[:, None], logits, -jnp.inf)
        p = jax.nn.softmax(logits, axis=-1).astype(v.dtype)
        return jnp.einsum('bhqk,bqkhd->bqhd', p, vs)

    out = lax.map(block, jnp.arange(n_blocks))
    return jnp.transpose(out, (1, 0, 2, 3, 4)).reshape(q.shape)

def multiscale_pool(u, pool_w):
    t_len = u.shape[1]
    uf = u.astype(jnp.float32)
    cs = jnp.cumsum(uf, axis=1)
    t = jnp.arange(t_len)
    outs = []
    for g, w in enumerate(POOL_WINDOWS):
        sl = slice(g * POOL_GROUP, (g + 1) * POOL_GROUP)
        c = cs[..., sl]
        shifted = jnp.pad(c, ((0, 0), (w, 0), (0, 0)))[:, :t_len]
        cnt = jnp.minimum(t + 1, w).astype(jnp.float32)[None, :, None]
        outs.append((c - shifted) / cnt - uf[..., sl])
    pooled = jnp.stack(outs, axis=2).astype(u.dtype)
    y = jnp.einsum('btgc,gcd->btgd', pooled, pool_w)
    return y.reshape(u.shape)

def mixer_ab(xn, w_in, q_gain, k_gain, pool_w, pool_scale, w_out):
    bsz, t_len, _ = xn.shape
    proj = xn @ w_in
    q, k, v, u, iq, iw, ik = jnp.split(proj, AB_SPLITS, axis=-1)
    pos = jnp.arange(t_len)
    q = rope_partial(rmsnorm(q.reshape(bsz, t_len, A_HEADS, HEAD_DIM_2), q_gain), pos)
    k = rope_partial(rmsnorm(k.reshape(bsz, t_len, A_HEADS, HEAD_DIM_2), k_gain), pos)
    v = v.reshape(bsz, t_len, A_HEADS, HEAD_DIM_2)
    iq = rope_partial(iq.reshape(bsz, t_len, IDX_HEADS, IDX_DIM), pos)
    ik = rope_partial(ik.reshape(bsz, t_len, 1, IDX_DIM), pos)[:, :, 0]
    iw = iw * (IDX_HEADS ** -0.5 * IDX_DIM ** -0.5)
    a = dsa_attention(q, k, v, iq, iw, ik).reshape(bsz, t_len, A_WIDTH)
    b = multiscale_pool(u, pool_w) * pool_scale
    return jnp.concatenate([a, b], axis=-1) @ w_out

def conv_module(xn, w_in, b_in, dw_w, dw_b, ln_g, ln_b, w_out):
    h = xn @ w_in + b_in
    a, gate = jnp.split(h, 2, axis=-1)
    h = a * jax.nn.sigmoid(gate)
    h = lax.conv_general_dilated(
        h, dw_w[:, None, :], window_strides=(1,), padding=[(CONV_WIDTH - 1, 0)],
        dimension_numbers=('NWC', 'WIO', 'NWC'), feature_group_count=D_CONV) + dw_b
    h = jax.nn.silu(layernorm(h, ln_g, ln_b))
    return h @ w_out

def cross_attn(hn, memn, wq, wk, wv, q_gain, k_gain, wo):
    bsz, t_len, _ = hn.shape
    m_len = memn.shape[1]
    q = rmsnorm((hn @ wq).reshape(bsz, t_len, C_HEADS, C_HEAD_DIM), q_gain)
    k = rmsnorm((memn @ wk).reshape(bsz, m_len, C_HEADS, C_HEAD_DIM), k_gain)
    v = (memn @ wv).reshape(bsz, m_len, C_HEADS, C_HEAD_DIM)
    logits = jnp.einsum('bthd,bmhd->bhtm', q, k).astype(jnp.float32) * C_HEAD_DIM ** -0.5
    p = jax.nn.softmax(logits, axis=-1).astype(v.dtype)
    o = jnp.einsum('bhtm,bmhd->bthd', p, v).reshape(bsz, t_len, D_MODEL)
    return o @ wo

def swiglu(xn, w_gate, w_up, w_down):
    return (jax.nn.silu(xn @ w_gate) * (xn @ w_up)) @ w_down

def second_inputs(seed: int = 0) -> dict:
    key = jax.random.key(seed)
    ks = iter(jax.random.split(key, 40))

    def dense(shape, fan_in):
        return jax.random.normal(next(ks), shape, jnp.float32) * fan_in ** -0.5

    def gain(shape):
        return 1.0 + 0.05 * jax.random.normal(next(ks), shape, jnp.float32)

    def bias(shape):
        return 0.02 * jax.random.normal(next(ks), shape, jnp.float32)

    return {
        'x': jax.random.normal(next(ks), (BATCH, SEQ, D_MODEL), jnp.float32),
        'mem': jax.random.normal(next(ks), (BATCH, MEM_LEN, D_MODEL), jnp.float32),
        'norm_mix': gain((DEPTH_2, D_MODEL)),
        'norm_cross': gain((DEPTH_2, D_MODEL)),
        'norm_mem': gain((DEPTH_2, D_MODEL)),
        'norm_ffn': gain((DEPTH_2, D_MODEL)),
        'w_in_ab': dense((N_EVEN, D_MODEL, IN_AB), D_MODEL),
        'a_q_norm': gain((N_EVEN, HEAD_DIM_2)),
        'a_k_norm': gain((N_EVEN, HEAD_DIM_2)),
        'pool_w': dense((N_EVEN, len(POOL_WINDOWS), POOL_GROUP, POOL_GROUP), POOL_GROUP),
        'pool_scale': gain((N_EVEN, B_WIDTH)),
        'w_out_ab': dense((N_EVEN, D_MODEL, D_MODEL), D_MODEL),
        'conv_w_in': dense((N_ODD, D_MODEL, 2 * D_CONV), D_MODEL),
        'conv_b_in': bias((N_ODD, 2 * D_CONV)),
        'conv_dw_w': dense((N_ODD, CONV_WIDTH, D_CONV), CONV_WIDTH),
        'conv_dw_b': bias((N_ODD, D_CONV)),
        'conv_ln_g': gain((N_ODD, D_CONV)),
        'conv_ln_b': bias((N_ODD, D_CONV)),
        'conv_w_out': dense((N_ODD, D_CONV, D_MODEL), D_CONV),
        'cross_wq': dense((DEPTH_2, D_MODEL, D_MODEL), D_MODEL),
        'cross_wk': dense((DEPTH_2, D_MODEL, D_MODEL), D_MODEL),
        'cross_wv': dense((DEPTH_2, D_MODEL, D_MODEL), D_MODEL),
        'cross_q_norm': gain((DEPTH_2, C_HEAD_DIM)),
        'cross_k_norm': gain((DEPTH_2, C_HEAD_DIM)),
        'cross_wo': dense((DEPTH_2, D_MODEL, D_MODEL), D_MODEL),
        'ffn_w_gate': dense((DEPTH_2, D_MODEL, D_FF_2), D_MODEL),
        'ffn_w_up': dense((DEPTH_2, D_MODEL, D_FF_2), D_MODEL),
        'ffn_w_down': dense((DEPTH_2, D_FF_2, D_MODEL), D_FF_2),
    }

def second_block(x, mem, norm_mix, norm_cross, norm_mem, norm_ffn, w_in_ab, a_q_norm, a_k_norm,
              pool_w, pool_scale, w_out_ab, conv_w_in, conv_b_in, conv_dw_w, conv_dw_b,
              conv_ln_g, conv_ln_b, conv_w_out, cross_wq, cross_wk, cross_wv, cross_q_norm,
              cross_k_norm, cross_wo, ffn_w_gate, ffn_w_up, ffn_w_down):
    h = x
    for l in range(DEPTH_2):
        xn = rmsnorm(h, norm_mix[l])
        if l % 2 == 0:
            e = l // 2
            h = h + mixer_ab(xn, w_in_ab[e], a_q_norm[e], a_k_norm[e], pool_w[e],
                             pool_scale[e], w_out_ab[e])
        else:
            o = l // 2
            h = h + conv_module(xn, conv_w_in[o], conv_b_in[o], conv_dw_w[o], conv_dw_b[o],
                                conv_ln_g[o], conv_ln_b[o], conv_w_out[o])
        h = h + cross_attn(rmsnorm(h, norm_cross[l]), rmsnorm(mem, norm_mem[l]),
                           cross_wq[l], cross_wk[l], cross_wv[l], cross_q_norm[l],
                           cross_k_norm[l], cross_wo[l])
        h = h + swiglu(rmsnorm(h, norm_ffn[l]), ffn_w_gate[l], ffn_w_up[l], ffn_w_down[l])
    return h


def setup_inputs(seed=0):
    out = dict(first_inputs(seed))
    for name, value in second_inputs(seed + 1).items():
        if name != "x":
            out[name + "_2"] = value
    return out


def reference(
    x, norm1_g, w_in, q_norm_g, k_norm_g, conv_w, conv_b, lru_wa, lru_ba, lru_wi, lru_bi,
    lru_lam, attn_out_g, lru_out_g, w_out, norm2_g, w_router, b_router, w_gate, b_gate, w_up,
    b_up, w_down, b_down, final_g, mem_2, norm_mix_2, norm_cross_2, norm_mem_2, norm_ffn_2,
    w_in_ab_2, a_q_norm_2, a_k_norm_2, pool_w_2, pool_scale_2, w_out_ab_2, conv_w_in_2,
    conv_b_in_2, conv_dw_w_2, conv_dw_b_2, conv_ln_g_2, conv_ln_b_2, conv_w_out_2, cross_wq_2,
    cross_wk_2, cross_wv_2, cross_q_norm_2, cross_k_norm_2, cross_wo_2, ffn_w_gate_2,
    ffn_w_up_2, ffn_w_down_2,
):
    x = first_block(
        x, norm1_g, w_in, q_norm_g, k_norm_g, conv_w, conv_b, lru_wa, lru_ba, lru_wi, lru_bi,
        lru_lam, attn_out_g, lru_out_g, w_out, norm2_g, w_router, b_router, w_gate, b_gate,
        w_up, b_up, w_down, b_down, final_g,
    )
    return second_block(
        x, mem_2, norm_mix_2, norm_cross_2, norm_mem_2, norm_ffn_2, w_in_ab_2, a_q_norm_2,
        a_k_norm_2, pool_w_2, pool_scale_2, w_out_ab_2, conv_w_in_2, conv_b_in_2, conv_dw_w_2,
        conv_dw_b_2, conv_ln_g_2, conv_ln_b_2, conv_w_out_2, cross_wq_2, cross_wk_2, cross_wv_2,
        cross_q_norm_2, cross_k_norm_2, cross_wo_2, ffn_w_gate_2, ffn_w_up_2, ffn_w_down_2,
    )


_drawn_inputs = setup_inputs


def setup_inputs(seed=0):
    import zlib

    import numpy as np

    out = dict(_drawn_inputs(seed))
    spreads = {}
    factors = {'b_gate': 7.039,
     'b_up': 8.0,
     'b_down': 6.932,
     'norm_cross_2': 8.0,
     'norm_mem_2': 5.876,
     'a_q_norm_2': 8.0,
     'a_k_norm_2': 8.0,
     'conv_b_in_2': 5.544,
     'conv_dw_b_2': 3.117,
     'conv_ln_b_2': 6.406,
     'cross_q_norm_2': 8.0,
     'cross_k_norm_2': 8.0}
    for name, (base, spread) in spreads.items():
        noise = np.random.default_rng([zlib.crc32(name.encode()), seed]).standard_normal(out[name].shape)
        drawn = base * np.exp(spread * noise) if base else spread * noise
        out[name] = __import__('jax').numpy.asarray(drawn.astype(out[name].dtype))
    for name, factor in factors.items():
        out[name] = (out[name] * factor).astype(out[name].dtype)
    return out
```

```python
from contextlib import ExitStack

import numpy as np

import concourse.bass as bass
from concourse import mybir

F32 = mybir.dt.float32
I32 = mybir.dt.int32
ALU = mybir.AluOpType
ACT = mybir.ActivationFunctionType
AX = mybir.AxisListType.X

P = 128
T = 256
D = 1024
C = D // P
UNIT = 2048
RING = 12
E = 32
SLOT = 64
BLOCKS = T // SLOT
FF2 = 2816
NG = FF2 // 256
TAPS = 31
ROUNDS = 64 // 8
FAR = -3.0e38
TAKEN = -3.4e38

PLAN = [("lru_x", 2), ("q", 2), ("kv", 1), ("lru_gate", 2), ("lru_w", 1), ("w_out", 4), ("moe", 12 * E),
        ("iq", 4), ("ikiw", 1), ("dq", 2), ("dk", 2), ("dv", 2), ("u", 2), ("pool", 1), ("ab_out", 4),
        ("ck0", 4), ("cv0", 4), ("cq0", 4), ("co0", 4), ("ffn0", 3 * NG),
        ("conv_in", 8), ("conv_out", 4),
        ("ck1", 4), ("cv1", 4), ("cq1", 4), ("co1", 4), ("ffn1", 3 * NG)]
AT = {}
N_UNITS = 0
for _name, _n in PLAN:
    AT[_name] = N_UNITS
    N_UNITS += _n
assert AT["moe"] % RING == 0 and RING == 12

VECS = [("norm1", 8), ("norm2", 8), ("final", 8), ("mix0", 8), ("mix1", 8), ("cross0", 8), ("cross1", 8),
        ("mem0", 8), ("mem1", 8), ("ffn0", 8), ("ffn1", 8), ("gq", 1), ("gk", 1), ("conv_w", 16),
        ("conv_b", 4), ("lru_b", 16), ("lam", 8), ("attn_g", 4), ("lru_g", 4), ("aq", 1), ("ak", 1),
        ("pool_scale", 4), ("cin_b", 16), ("dw", 8 * TAPS), ("dw_b", 8), ("ln_g", 8), ("ln_b", 8),
        ("cqg0", 2), ("cqg1", 2), ("ckg0", 2), ("ckg1", 2), ("eps5", 1), ("eps6", 1)]
VAT = {}
NV = 0
for _name, _n in VECS:
    VAT[_name] = NV
    NV += _n

TABLES = [("cos1", T), ("sin1", T), ("cos2", T), ("sin2", T), ("cos3", T), ("sin3", T), ("rot1", P),
          ("rot2", P), ("rot3", P), ("ident", P), ("ones", P), ("heads", P), ("before", P), ("iota", T),
          ("far", 2 * T), ("rcount", 64)]
TAT = {}
NT = 0
for _name, _n in TABLES:
    TAT[_name] = NT
    NT += _n


RES = {1: 0, 4: 1, 5: 2, 6: 3, 7: 4, 8: 5}


def ffn_gate_unit(g):
    return 3 * g - 1 if g else 0


class Chain:

    def __init__(self, eng, sem, offset=0):
        self.eng, self.sem, self.offset, self.n = eng, sem, offset, 0

    def mark(self, ins):
        ins.then_inc(self.sem, 1)
        self.n += 1

    def settle(self):
        self.eng.wait_ge(self.sem, self.offset + self.n)

    def link(self, ins):
        self.mark(ins)
        self.settle()


def build(nc, x, mem, stream, vecs, tables, moe_b, b_down, w_router, b_router, out):
    with ExitStack() as ctx:
        def sb(name, shape, dt=F32):
            return ctx.enter_context(nc.sbuf_tensor(name, shape, dt))

        def sem(name):
            return ctx.enter_context(nc.semaphore(name))

        ring = sb("ring", [P, RING, UNIT])
        xT = sb("xT", [P, C, T])
        xn = sb("xn", [P, C, T])
        sq = sb("sq", [P, C, T])
        B = sb("B", [P, 12560])
        vec = sb("vec", [P, NV])
        tab = sb("tab", [P, NT])
        mbias = sb("mbias", [P, E * 16])
        wr = sb("wr", [P, C, E])
        br = sb("br", [P, E])
        tsq = sb("tsq", [P, 2, 512])
        tv = sb("tv", [P, 2, 512])
        prob = sb("prob", [P, 2, 2, T])
        pT = sb("pT", [P, 2, 2, T])
        std = sb("std", [P, 512])
        rinv = sb("rinv", [P, 512])
        small = sb("small", [P, 32])
        mx = sb("mx", [P, 2])
        rs = sb("rs", [P, 2])
        lam3 = sb("lam3", [P, 24])
        m8b = sb("m8b", [P, 2, 8])
        flag = sb("flag", [P, 1], I32)
        PS = [ctx.enter_context(nc.psum_tensor(f"bank{i}", [P, 512], F32)) for i in range(8)]

        def V(name, i=0, n=1):
            return vec[:, VAT[name] + i:VAT[name] + i + n]

        def tb(name):
            return tab[:, TAT[name]:TAT[name] + dict(TABLES)[name]]

        def reg(a, *shape, rows=P):
            n = int(np.prod(shape))
            v = B[0:rows, a:a + n]
            if len(shape) == 2:
                return v.rearrange("p (a b) -> p a b", a=shape[0])
            if len(shape) == 3:
                return v.rearrange("p (a b c) -> p a b c", a=shape[0], b=shape[1])
            return v

        def two(bank):
            return PS[bank][:, :].rearrange("p (a t) -> p a t", a=2)

        def over(ap, n):
            return ap.unsqueeze(1).broadcast_to((P, n, ap.shape[-1]))

        def along(ap, n):
            return ap.unsqueeze(2).broadcast_to((ap.shape[0], ap.shape[1], n))

        lxp = reg(0, 4, 260)
        gtmp = reg(0, 4, T)
        xc = reg(1040, 4, T)
        lgate = reg(2064, 4, T)
        rr = reg(3088, 8, T)
        ii = reg(5136, 8, T)
        th = reg(7184, 8, T)
        qg = reg(9232, 5, T)
        at1 = reg(10512, 4, T)
        vt1 = reg(11536, 2, P)
        kz = reg(11792, 2, T)
        xtok = reg(0, 2, D)
        xs = [reg(2048 + 512 * s, C, SLOT) for s in range(2)]
        hT = reg(3072, C, SLOT)
        gu = [reg(3584 + 512 * s, 8, SLOT) for s in range(2)]
        sig = [reg(4608 + 256 * s, 4, SLOT) for s in range(2)]
        sel = [reg(5120 + 128 * s, 2, SLOT) for s in range(2)]
        selg = [reg(5376 + 128 * s, 2, SLOT) for s in range(2)]
        selgT = [reg(5632 + 256 * s, T, rows=SLOT) for s in range(2)]
        yT = reg(6144, C, SLOT)
        ytok = reg(6656, D, rows=SLOT)
        G = reg(7680, 2, E + 1)
        key = reg(7760, 2, E + 1)
        lg = reg(7840, 2, 40)
        lg2 = reg(7920, 2, 40)
        m8 = reg(8000, 2, 8)
        msk = reg(8016, 2, E)
        exr = reg(8080, 2, E)
        gs = reg(8144, 4)
        cnt = reg(8150, E)
        GT = reg(8192, T, rows=E)
        bd = reg(8448, D, rows=E)
        iqr = reg(0, 8, T)
        iz = reg(2048, 2, T)
        iw = reg(2560, 2, 16)
        dqk = reg(2592, 8, T)
        dv = reg(4640, 2, 512)
        up = reg(5664, 4, 272)
        w1 = reg(6752, 4, 272)
        w2 = reg(7840, 4, 272)
        mix = reg(9680, 8, T)
        iqt = reg(9680, 2, T)
        rl = [reg(9680 + 512 * s, 2, T) for s in range(2)]
        sc = reg(11728, 2, T)
        pen = reg(8928, 2, T)
        memT = [reg(0, 8, T), reg(10240, 8, T)]
        memn = reg(2048, 8, T)
        ckn = reg(4096, 8, T)
        cvt = reg(6144, 2, D)
        cqn = reg(8192, 8, T)
        co = reg(10240, 8, T)
        rmem = reg(12304, T)
        fh = [reg(512 * s, 2, T) for s in range(2)]
        fs = [reg(1024 + 512 * s, 2, T) for s in range(2)]
        hp = reg(0, 8, 286)
        hc = reg(2304, 8, T)
        yc = reg(4352, 8, T)
        csg = reg(6400, 2, T)
        NDIAG = 6
        diag = reg(7000, NDIAG, P)

        landed = [sem(f"landed{s}") for s in range(RING)]
        names = """x_loaded consts_loaded router_loaded mem_loaded bd_loaded pads_ready units_done
            sq_ready stat_mm std_ready xn_ready res_ready dve_chain act_chain
            lam_exp lx_ready xc_ready qraw_ready qsq_ready vk_ready lgate_ready hstat_mm hstd_ready rot_mm
            rot_read qn_ready lru_mm lru_ev r_ready lgsq_ready ginner_ready gsig_ready m_ready mult_ready lru_ready
            score_mm nmax_ready exp_done probs_ready pT_mm pT_ready o_mm o_ready
            osq_ready ostat_mm ostd_ready mixed_ready
            rout_mm lg_ready gex_ready mask_ready cnt_mm flag_ready tok_mm tok_ready acc_mm
            gt_mm gt_ready moe_mm xmoe_ready
            iq_ready iqrot_mm iqrot_read iqn_ready iw_ready iscore_mm relu_ready relu_used
            dqk_ready dsq_ready dstat_mm dstd_ready drot_mm dqn_ready dv_ready u_ready pooled_ready pool_mix
            msq_ready mstat_mm mstd_ready memn_ready
            ck_raw cksq_ready ckstat_mm ckstd_ready ckn_ready cv_ready
            f_sig f_h conv_sig hp_ready diag_ready dwc_mm hc_pe hc_dve lnsum_mm lnd_ready lnsq_ready lnvar_mm
            lnstd_ready lnz_ready lnsig_ready yc_ready out_stored""".split()
        S = {n: sem(n) for n in names}
        moe_sem_names = """sel_ready selT_mm selT_ready xs_mm xs_ready early_a early_b early_d sig_in sig_ready
            h_ready y_ready tr_mm ylo_ready yhi_ready scat_mm chain""".split()
        M = {path: {n: sem(f"{path}_{n}") for n in moe_sem_names} for path in ("one", "all")}

        class Path:
            def __init__(self, name):
                self.name = name
                self.s = M[name]
                self.passes = 2 if name == "one" else BLOCKS
                self.iters = E // 2 if name == "one" else E

            def number(self, i, q):
                return i * self.passes + q

            def expert(self, i, q):
                return i * 2 + q if self.name == "one" else i

            def following(self, i, q):
                if self.name == "one":
                    return i * 2 + q + 1, 0
                return (i, q + 1) if q + 1 < BLOCKS else (i + 1, 0)

            def releases(self, q):
                return self.name == "one" or q == BLOCKS - 1

            def await_part(self, eng, i, q, part, units):
                if self.releases(q):
                    eng.wait_ge(S["units_done"], self.expert(i, q) * 12 + (AT["moe"] + units))
                else:
                    eng.wait_ge(self.s[f"early_{part}"], i * (BLOCKS - 1) + (q + 1))

        PATHS = (Path("one"), Path("all"))

        block = ctx.enter_context(nc.Block())

        @block.sync
        def _(sp):
            sp.dma_start(xT[:], x).then_inc(S["x_loaded"], 16)
            for dst, src in ((vec, vecs), (tab, tables)):
                sp.dma_start(dst[:], src).then_inc(S["consts_loaded"], 16)
            for s in range(RING):
                sp.dma_start(ring[:, s, :], stream[s]).then_inc(landed[s], 16)
            for dst, src in ((wr, w_router), (br, b_router), (mbias, moe_b)):
                sp.dma_start(dst[:], src).then_inc(S["router_loaded"], 16)
            turns = N_UNITS // RING
            with sp.Fori(1, turns) as i:
                for s in range(RING):
                    sp.wait_ge(S["units_done"], i * RING + (s - RING + 1))
                    sp.dma_start(ring[:, s, :], stream[i * RING + s]).then_inc(landed[s], 16)
            for u in range(turns * RING, N_UNITS):
                sp.wait_ge(S["units_done"], u - RING + 1)
                sp.dma_start(ring[:, u % RING, :], stream[u]).then_inc(landed[u % RING], 16)
            for j in range(4):
                sp.wait_ge(S["res_ready"], 4 * 6 + j + 1)
                sp.dma_start(out[:, 2 * j:2 * j + 2, :], xT[:, 2 * j:2 * j + 2, :]).then_inc(S["out_stored"], 16)
            sp.wait_ge(S["out_stored"], 64)

        @block.gpsimd
        def _(pool):
            pool.memset(lxp[:, :, 0:2], 0.0).then_inc(S["pads_ready"], 1)
            pool.memset(lxp[:, :, 258:260], 0.0).then_inc(S["pads_ready"], 1)
            pool.memset(kz[:, :, :], 0.0).then_inc(S["pads_ready"], 1)
            pool.wait_ge(S["res_ready"], 4)
            pool.dma_start(bd[:, :], b_down).then_inc(S["bd_loaded"], 16)
            pool.memset(G[:, :, E:E + 1], 0.0).then_inc(S["pads_ready"], 1)
            pool.memset(key[:, :, E:E + 1], -1.0).then_inc(S["pads_ready"], 1)
            pool.memset(lg[:, :, E:E + 4], 3.0e38).then_inc(S["pads_ready"], 1)
            pool.wait_ge(S["xmoe_ready"], 4)
            pool.memset(iz[:, :, :], 0.0).then_inc(S["pads_ready"], 1)
            pool.memset(up[:, :, 0:16], 0.0).then_inc(S["pads_ready"], 1)
            pool.wait_ge(S["o_ready"], 12)
            pool.dma_start(memT[0][:, :, :], mem).then_inc(S["mem_loaded"], 16)
            pool.wait_ge(S["res_ready"], 4 * 4)
            pool.memset(hp[:, :, 0:30], 0.0).then_inc(S["pads_ready"], 1)
            pool.dma_start(memT[1][:, :, :], mem).then_inc(S["mem_loaded"], 16)

        @block.tensor
        def _(pe):
            def tile(u, t, n=P):
                return ring[:, u % RING, t * P:t * P + n]

            def await_unit(u):
                pe.wait_ge(landed[u % RING], 16 * (u // RING + 1))

            def stationary(u, dst, rhs, ready=None):
                await_unit(u)
                for m in range(2):
                    for k in range(C):
                        if ready is not None and m == 0:
                            pe.wait_ge(ready[0], ready[1] + k + 1)
                        mm = pe.matmul(dst[:, m, :], tile(u, m * C + k), rhs[:, k, :], start=(k == 0),
                                       stop=(k == C - 1))
                mm.then_inc(S["units_done"], 1)

            def stat_pair(n, j):
                pe.wait_ge(S["sq_ready"], 4 * n + j + 1)
                for c in (2 * j, 2 * j + 1):
                    mm = pe.matmul(PS[4][:, 0:T], tb("ones"), sq[:, c, :], start=(c == 0), stop=(c == C - 1))
                if j == 3:
                    mm.then_inc(S["stat_mm"], 1)

            def output_linear(first, rhs, n, ready=None):
                for j in range(4):
                    stationary(first + j, two(j), rhs, ready if j == 0 else None)
                    if j and n is not None:
                        stat_pair(n, j - 1)
                if n is not None:
                    stat_pair(n, 3)

            def heads(first, count, score, output):
                def scores(a):
                    if a - first >= 2:
                        pe.wait_ge(S["exp_done"], a - 1)
                    score(a, two(2 + a % 2)).then_inc(S["score_mm"], 1)

                def outputs(a):
                    pe.wait_ge(S["probs_ready"], a + 1)
                    if a >= 2:
                        pe.wait_ge(S["pT_ready"], a - 1)
                    bank = two(6 + a % 2)
                    for kb in range(2):
                        for b in range(2):
                            mm = pe.transpose(bank[:, kb, b * P:(b + 1) * P],
                                              prob[:, a % 2, b, kb * P:(kb + 1) * P], tb("ident"))
                    mm.then_inc(S["pT_mm"], 1)
                    pe.wait_ge(S["pT_ready"], a + 1)
                    if a >= 2:
                        pe.wait_ge(S["o_ready"], a - 1)
                    output(a, two(4 + a % 2)).then_inc(S["o_mm"], 1)

                scores(first)
                for a in range(first, first + count):
                    if a + 1 < first + count:
                        scores(a + 1)
                    outputs(a)

            pe.wait_ge(S["consts_loaded"], 32)
            for j in range(4):
                stat_pair(0, j)
            stationary(AT["lru_x"], two(0), xn, (S["xn_ready"], 0))
            stationary(AT["lru_x"] + 1, two(1), xn)
            stationary(AT["q"], two(2), xn)
            stationary(AT["q"] + 1, two(3), xn)
            u = AT["kv"]
            await_unit(u)
            for k in range(C):
                pe.matmul(PS[5][:, 0:T], tile(u, k), xn[:, k, :], start=(k == 0), stop=(k == C - 1))
            for b in range(2):
                for k in range(C):
                    mm = pe.matmul(PS[5][:, T + b * P:T + (b + 1) * P], xn[:, k, b * P:(b + 1) * P],
                                   tile(u, C + k), start=(k == 0), stop=(k == C - 1))
            mm.then_inc(S["units_done"], 1)
            for j in range(2):
                pe.wait_ge(S["lx_ready"], j + 1)
                stationary(AT["lru_gate"] + j, two(j), xn)
            for j in range(2):
                pe.wait_ge(S["qsq_ready"], j + 1)
                pe.matmul(PS[6 + j][:, :], tb("heads"), tsq[:, j, :], start=True, stop=True)\
                    .then_inc(S["hstat_mm"], 1)
                pe.wait_ge(S["qraw_ready"], j + 1)
                pe.matmul(two(2 + j), tb("rot1"), qg[:, 2 * j:2 * j + 2, :], start=True, stop=True)\
                    .then_inc(S["rot_mm"], 1)
            pe.wait_ge(S["qsq_ready"], 3)
            pe.matmul(PS[4][:, 0:T], tb("heads"), tsq[:, 0, 0:T], start=True, stop=True)\
                .then_inc(S["hstat_mm"], 1)
            pe.wait_ge(S["vk_ready"], 1)
            pe.matmul(PS[4][:, T:2 * T], tb("rot1"), qg[:, 4, :], start=True, stop=True)\
                .then_inc(S["rot_mm"], 1)
            u = AT["lru_w"]
            await_unit(u)
            pe.wait_ge(S["xc_ready"], 4)
            for n in range(8):
                if n < 2:
                    pe.wait_ge(S["lgate_ready"], n + 1)
                else:
                    pe.wait_ge(S["lru_ev"], n - 1)
                for c in range(2):
                    mm = pe.matmul(two(n % 2)[:, c, :], tile(u, 2 * n + c), xc[:, 2 * (n % 2) + c, :],
                                   start=True, stop=True)
                mm.then_inc(S["lru_mm"] if n < 7 else S["units_done"], 1)

            def score1(a, bank):
                pe.wait_ge(S["qn_ready"], 3)
                for b in range(2):
                    mm = pe.matmul(bank[:, b, :], qg[:, a % 4, b * P:(b + 1) * P], kz[:, a // 4, :],
                                   start=True, stop=True)
                return mm

            def output1(a, bank):
                for kb in range(2):
                    mm = pe.matmul(bank[:, 0, :], vt1[:, kb, :], pT[:, a % 2, kb, :], start=(kb == 0),
                                   stop=(kb == 1))
                return mm

            heads(0, 8, score1, output1)
            for g in range(2):
                pe.wait_ge(S["osq_ready"], g + 1)
                for c in range(4):
                    mm = pe.matmul(two(0)[:, g, :], tb("ones"), sq[:, 4 * g + c, :], start=(c == 0),
                                   stop=(c == 3))
                mm.then_inc(S["ostat_mm"], 1)
            pe.wait_ge(S["mixed_ready"], 8)
            output_linear(AT["w_out"], xn, 1)

            for tk in range(2):
                for k in range(C):
                    pe.wait_ge(S["xn_ready"], 8 + k + 1)
                    if tk == 0 and k == 0:
                        pe.wait_ge(S["router_loaded"], 48)
                    mm = pe.matmul(PS[5][:, tk * E:(tk + 1) * E], xn[:, k, tk * P:(tk + 1) * P], wr[:, k, :],
                                   start=(k == 0), stop=(k == C - 1))
            mm.then_inc(S["rout_mm"], 1)
            for g in range(4):
                bank = PS[6 + g % 2]
                if g >= 2:
                    pe.wait_ge(S["tok_ready"], g - 1)
                for c in range(4):
                    mm = pe.transpose(bank[:, c * P:(c + 1) * P],
                                      xn[:, 4 * (g % 2) + c, (g // 2) * P:(g // 2 + 1) * P], tb("ident"))
                mm.then_inc(S["tok_mm"], 1)
            for c in range(C):
                mm = pe.matmul(PS[c // 2][:, (c % 2) * T:(c % 2 + 1) * T], tb("ident"), xT[:, c, :],
                               start=(c % 2 == 0), stop=False, skip_group_check=True)
            pe.wait_ge(S["mask_ready"], 1)
            cp = PS[5][:, 64:64 + 3 * E].rearrange("p (a e) -> p a e", a=3)
            pe.matmul(cp[:, 0, :], tb("before"), msk[:, 0, :], start=True, stop=True)
            for g, w in ((1, "before"), (2, "ones")):
                pe.matmul(cp[:, g, :], tb("ones"), msk[:, 0, :], start=True, stop=False)
                mm = pe.matmul(cp[:, g, :], tb(w), msk[:, 1, :], start=False, stop=True)
            mm.then_inc(S["cnt_mm"], 1)
            pe.wait_ge(S["lg_ready"], 3)
            for tk in range(2):
                mm = pe.transpose(PS[4][0:E, tk * P:(tk + 1) * P], G[:, tk, 0:E], tb("ident"))
            mm.then_inc(S["gt_mm"], 1)

            def select_T(path, n, s):
                pe.wait_ge(path.s["sel_ready"], n + 1)
                for tk in range(2):
                    mm = pe.matmul(PS[6][0:SLOT, tk * P:(tk + 1) * P], selg[s][:, tk, :], tb("ident"),
                                   start=True, stop=True)
                mm.then_inc(path.s["selT_mm"], 1)

            def gather(path, n, s):
                pe.wait_ge(path.s["selT_ready"], n + 1)
                for c in range(C):
                    for tk in range(2):
                        mm = pe.matmul(PS[6][:, c * SLOT:(c + 1) * SLOT], xtok[:, tk, c * P:(c + 1) * P],
                                       sel[s][:, tk, :], start=(tk == 0), stop=(tk == 1))
                mm.then_inc(path.s["xs_mm"], 1)

            def experts(path):
                pe.sem_inc(path.s["scat_mm"], 1)
                select_T(path, 0, 0)
                gather(path, 0, 0)
                with pe.Fori(0, path.iters) as i:
                    for q in range(path.passes):
                        n, s = path.number(i, q), q % 2
                        e = path.expert(i, q)
                        frees = path.releases(q)
                        pe.wait_ge(path.s["xs_ready"], n + 1)
                        for half in range(2):
                            pe.wait_ge(path.s["yhi_ready" if half else "ylo_ready"], n + 1)
                            for kind in range(2):
                                for pair in range(2):
                                    j = 4 * half + 2 * kind + pair
                                    pe.wait_ge(landed[j], e * 16 + 16 * (AT["moe"] // RING + 1))
                                    for m in range(2):
                                        at = (4 * kind + 2 * pair + m) * SLOT
                                        for k in range(C):
                                            mm = pe.matmul(PS[4 + half][:, at:at + SLOT], tile(j, m * C + k),
                                                           xs[s][:, k, :], start=(k == 0), stop=(k == C - 1))
                                    if frees:
                                        mm.then_inc(S["units_done"], 1)
                            if not frees:
                                mm.then_inc(path.s["early_b" if half else "early_a"], 1)
                            if half == 0:
                                select_T(path, n + 1, 1 - s)
                        gather(path, n + 1, 1 - s)
                        for d in range(4):
                            j = 8 + d
                            pe.wait_ge(landed[j], e * 16 + 16 * (AT["moe"] // RING + 1))
                            if d % 2 == 0:
                                pe.wait_ge(path.s["h_ready"], n * 2 + (d // 2 + 1))
                            if d == 0:
                                pe.wait_ge(path.s["y_ready"], n + 1)
                            for kk in range(2):
                                for m in range(C):
                                    mm = pe.matmul(PS[7][:, m * SLOT:(m + 1) * SLOT], tile(j, kk * C + m),
                                                   hT[:, 2 * d + kk, :], start=(d == kk == m == 0),
                                                   stop=(d == 3 and kk == 1), skip_group_check=True)
                            if frees:
                                mm.then_inc(S["units_done"], 1)
                        if not frees:
                            mm.then_inc(path.s["early_d"], 1)
                        pe.wait_ge(path.s["y_ready"], n + 2)
                        for m in range(C):
                            mm = pe.matmul(PS[4 + m // 4][0:SLOT, (m % 4) * P:(m % 4 + 1) * P], yT[:, m, :],
                                           tb("ident"), start=True, stop=True)
                        mm.then_inc(path.s["tr_mm"], 1)
                        pe.wait_ge(path.s["ylo_ready"], n + 2)
                        pe.wait_ge(path.s["yhi_ready"], n + 2)
                        for c in range(C):
                            mm = pe.matmul(PS[c // 2][:, (c % 2) * T:(c % 2 + 1) * T],
                                           ytok[:, c * P:(c + 1) * P], selgT[s][:, :], start=False, stop=False,
                                           skip_group_check=True)
                        mm.then_inc(path.s["scat_mm"], 1)

            pe.wait_ge(S["flag_ready"], 1)
            pe.wait_ge(S["tok_ready"], 4)
            pe.wait_ge(S["gt_ready"], 1)
            most = pe.value_load(flag[0:1, 0:1], min_val=0, max_val=T)
            with pe.If(most < SLOT + 1):
                experts(PATHS[0])
            with pe.Else():
                experts(PATHS[1])
            pe.wait_ge(S["bd_loaded"], 16)
            for c in range(C):
                mm = pe.matmul(PS[c // 2][:, (c % 2) * T:(c % 2 + 1) * T], bd[:, c * P:(c + 1) * P], GT[:, :],
                               start=False, stop=True, skip_group_check=True)
                if c % 2:
                    mm.then_inc(S["moe_mm"], 1)

            for n in (2, 3):
                for j in range(4):
                    stat_pair(n, j)

            for j in range(4):
                stationary(AT["iq"] + j, two(j), xn, (S["xn_ready"], 24) if j == 0 else None)
            u = AT["ikiw"]
            await_unit(u)
            for k in range(C):
                pe.matmul(PS[5][:, 0:T], tile(u, k), xn[:, k, :], start=(k == 0), stop=(k == C - 1))
            for b in range(2):
                for k in range(C):
                    mm = pe.matmul(PS[5][:, T + 16 * b:T + 16 * b + 16], xn[:, k, b * P:(b + 1) * P],
                                   ring[:, u % RING, C * P + 16 * k:C * P + 16 * k + 16],
                                   start=(k == 0), stop=(k == C - 1))
            mm.then_inc(S["units_done"], 1)
            for j in range(5):
                pe.wait_ge(S["iq_ready"], j + 1)
                if j >= 2:
                    pe.wait_ge(S["iqrot_read"], j - 1)
                if j < 4:
                    pe.matmul(two(6 + j % 2), tb("rot3"), iqr[:, 2 * j:2 * j + 2, :], start=True, stop=True)\
                        .then_inc(S["iqrot_mm"], 1)
                else:
                    pe.matmul(PS[6][:, 0:T], tb("rot3"), tv[:, 0, 0:T], start=True, stop=True)\
                        .then_inc(S["iqrot_mm"], 1)
            def index_scores(h):
                pe.wait_ge(S["iqn_ready"], 5)
                if h >= 2:
                    pe.wait_ge(S["relu_ready"], h - 1)
                for b in range(2):
                    mm = pe.matmul(two(h % 2)[:, b, :], iqr[:, h // 2, b * P:(b + 1) * P], iz[:, h % 2, :],
                                   start=True, stop=True)
                mm.then_inc(S["iscore_mm"], 1)

            for j in range(4):
                if j >= 2:
                    pe.wait_ge(S["dqk_ready"], j - 1)
                stationary((AT["dq"] + j), two(2 + j % 2), xn)
                for h in range(4 * j, 4 * j + 4):
                    index_scores(h)
                pe.wait_ge(S["dsq_ready"], j + 1)
                if j:
                    pe.wait_ge(S["dqn_ready"], j)
                pe.matmul(PS[4][:, :], tb("ones"), tsq[:, j % 2, :], start=True, stop=True)\
                    .then_inc(S["dstat_mm"], 1)
                pe.wait_ge(S["dqk_ready"], j + 1)
                pe.matmul(two(5), tb("rot2"), dqk[:, 2 * j:2 * j + 2, :], start=True, stop=True)\
                    .then_inc(S["drot_mm"], 1)
            for w in range(2):
                u = AT["dv"] + w
                await_unit(u)
                for kk in range(4):
                    for b in range(2):
                        k = 4 * w + kk
                        mm = pe.matmul(PS[6 + b][:, :], xn[:, k, b * P:(b + 1) * P],
                                       ring[:, u % RING, 512 * kk:512 * kk + 512],
                                       start=(k == 0), stop=(k == C - 1))
                mm.then_inc(S["units_done"], 1)
            pe.wait_ge(S["relu_ready"], 16)
            for j in range(2):
                stationary(AT["u"] + j, two(j), xn)
            u = AT["pool"]
            await_unit(u)
            pe.wait_ge(S["pooled_ready"], 4)
            for g in range(4):
                mm = pe.matmul(two(g // 2)[:, g % 2, :], tile(u, g), w1[:, g, 0:T], start=True, stop=True)
            mm.then_inc(S["units_done"], 1)

            def score2(a, bank):
                pe.wait_ge(S["dqn_ready"], 4)
                h = a - 8
                for b in range(2):
                    mm = pe.matmul(bank[:, b, :], dqk[:, h, b * P:(b + 1) * P], dqk[:, 4 + h, :],
                                   start=True, stop=True)
                return mm

            def output2(a, bank):
                h = a - 8
                for kb in range(2):
                    mm = pe.matmul(bank[:, 0, :], dv[:, kb, h * P:(h + 1) * P], pT[:, a % 2, kb, :],
                                   start=(kb == 0), stop=(kb == 1))
                return mm

            pe.wait_ge(S["dv_ready"], 2)
            heads(8, 4, score2, output2)
            pe.wait_ge(S["pool_mix"], 4)
            pe.wait_ge(S["o_ready"], 12)
            output_linear(AT["ab_out"], mix, 4)

            def cross(l):
                ck, cv, cq, c_o = (AT[f"{x}{l}"] for x in ("ck", "cv", "cq", "co"))
                if l == 0:
                    for j in range(4):
                        pe.wait_ge(S["msq_ready"], j + 1)
                        for c in (2 * j, 2 * j + 1):
                            mm = pe.matmul(PS[5][:, 0:T], tb("ones"), sq[:, c, :], start=(c == 0),
                                           stop=(c == C - 1))
                    mm.then_inc(S["mstat_mm"], 1)
                for side, first, rhs, ready in ((0, ck, memn, (S["memn_ready"], 8 * l)),
                                                (1, cq, xn, (S["xn_ready"], 8 * (4 + 3 * l)))):
                    base = 8 * l + 4 * side
                    for j in range(4):
                        if j >= 2 or side:
                            pe.wait_ge(S["ck_raw"], base + j - 1 if j >= 2 else base)
                        stationary(first + j, two(2 + j % 2), rhs, ready if j == 0 else None)
                        if j:
                            head_sum(base + j - 1)
                    head_sum(base + 3)
                    if side == 0:
                        for w in range(4):
                            u = cv + w
                            await_unit(u)
                            for kk in range(2):
                                k = 2 * w + kk
                                for b in range(2):
                                    for hf in range(2):
                                        bank = (0, 1, 6, 7)[2 * b + hf]
                                        mm = pe.matmul(PS[bank][:, :], memn[:, k, b * P:(b + 1) * P],
                                                       ring[:, u % RING,
                                                            D * kk + 512 * hf:D * kk + 512 * hf + 512],
                                                       start=(k == 0), stop=(k == C - 1))
                            mm.then_inc(S["units_done"], 1)

                def score(a, bank):
                    h = (a - 12) % 4
                    pe.wait_ge(S["ckn_ready"], 8 * l + 8)
                    for b in range(2):
                        for c in range(2):
                            mm = pe.matmul(bank[:, b, :], cqn[:, 2 * h + c, b * P:(b + 1) * P],
                                           ckn[:, 2 * h + c, :], start=(c == 0), stop=(c == 1))
                    return mm

                def output(a, bank):
                    h = (a - 12) % 4
                    for c in range(2):
                        for kb in range(2):
                            mm = pe.matmul(bank[:, c, :], cvt[:, kb, 256 * h + c * P:256 * h + (c + 1) * P],
                                           pT[:, a % 2, kb, :], start=(kb == 0), stop=(kb == 1))
                    return mm

                pe.wait_ge(S["cv_ready"], 4 * (l + 1))
                heads(12 + 4 * l, 4, score, output)
                pe.wait_ge(S["o_ready"], 16 + 4 * l)
                output_linear(c_o, co, 5 + 3 * l)

            def head_sum(p):
                pe.wait_ge(S["cksq_ready"], p + 1)
                if p:
                    pe.wait_ge(S["ckstd_ready"], p)
                for c in range(2):
                    mm = pe.matmul(PS[5][:, T:2 * T], tb("ones"), tsq[:, p % 2, c * T:(c + 1) * T],
                                   start=(c == 0), stop=(c == 1))
                mm.then_inc(S["ckstat_mm"], 1)

            def ffn(l):
                first, n = AT[f"ffn{l}"], 8 * (5 + 3 * l)
                at = [first]
                for g in range(NG):
                    for kind in range(2):
                        bank = 4 + 2 * (g % 2) + kind
                        if g >= 2:
                            pe.wait_ge(S["f_h"], NG * l + g - 1)
                        stationary(at[0], two(bank), xn, (S["xn_ready"], n) if g == kind == 0 else None)
                        at[0] += 1
                    if g:
                        down(l, g - 1, at)
                down(l, NG - 1, at)
                if l == 0:
                    for j in range(4):
                        stat_pair(6, j)

            def down(l, g, at):
                u = at[0]
                at[0] += 1
                await_unit(u)
                pe.wait_ge(S["f_h"], NG * l + g + 1)
                for m in range(C):
                    for kk in range(2):
                        mm = pe.matmul(PS[m // 2][:, (m % 2) * T:(m % 2 + 1) * T], tile(u, kk * C + m),
                                       fh[g % 2][:, kk, :], start=(g == 0 and kk == 0 and m % 2 == 0),
                                       stop=(g == NG - 1 and kk == 1), skip_group_check=True)
                mm.then_inc(S["units_done"], 1)

            cross(0)
            ffn(0)
            for j in range(8):
                if j >= 4:
                    pe.wait_ge(S["hp_ready"], j - 3)
                stationary(AT["conv_in"] + j, two(j % 4), xn, (S["xn_ready"], 48) if j == 0 else None)
            for c in range(4):
                pe.wait_ge(S["hp_ready"], c + 1)
                for t in range(TAPS):
                    pe.wait_ge(S["diag_ready"], c * TAPS + t + 1)
                    pe.matmul(PS[4 + c][:, 0:T], diag[:, (c * TAPS + t) % NDIAG, :],
                              hp[:, c, t:t + T], start=(t == 0), stop=(t == TAPS - 1))\
                        .then_inc(S["dwc_mm"], 1)
            for c in range(C):
                if c < 4:
                    pe.wait_ge(S["hc_pe"], c + 1)
                else:
                    pe.wait_ge(S["hc_dve"], c - 3)
                mm = pe.matmul(PS[0][:, 0:T], tb("ones"), hc[:, c, :], start=(c == 0), stop=(c == C - 1))
            mm.then_inc(S["lnsum_mm"], 1)
            for j in range(4):
                pe.wait_ge(S["lnsq_ready"], j + 1)
                for c in (2 * j, 2 * j + 1):
                    mm = pe.matmul(PS[1][:, 0:T], tb("ones"), sq[:, c, :], start=(c == 0), stop=(c == C - 1))
            mm.then_inc(S["lnvar_mm"], 1)
            output_linear(AT["conv_out"], yc, 7, (S["yc_ready"], 0))
            cross(1)
            ffn(1)
            assert AT["ffn1"] + 3 * NG == N_UNITS

        @block.scalar
        def _(act):
            chain = Chain(act, S["act_chain"])

            def f(out_, in_, fn, **kw):
                return act.activation(out_, in_, fn, **kw)

            def squares(n, j, sem_=None, value=None, src=None):
                if n == 0:
                    act.wait_ge(S["x_loaded"], 16)
                elif n == 3:
                    act.wait_ge(S["xn_ready"], 16 + 2 * j + 2)
                elif n == 2:
                    act.wait_ge(S["xmoe_ready"], j + 1)
                else:
                    act.wait_ge(S["res_ready"], 4 * RES[n] + j + 1)
                f(sq[:, 2 * j:2 * j + 2, :], xT[:, 2 * j:2 * j + 2, :], ACT.Square).then_inc(S["sq_ready"], 1)

            def deviation(n, eps):
                act.wait_ge(S["stat_mm"], n + 1)
                f(std[:, 0:T], PS[4][:, 0:T], ACT.Sqrt, scale=1.0 / D, bias=V(eps)).then_inc(S["std_ready"], 1)

            def norm(n, eps="eps6"):
                for j in range(4):
                    squares(n, j)
                deviation(n, eps)

            def heads(first, count, scale, src, evacuate):
                def exps(a):
                    act.wait_ge(S["nmax_ready"], a + 1)
                    if a >= 2:
                        act.wait_ge(S["pT_mm"], a - 1)
                        act.wait_ge(S["probs_ready"], a - 1)
                    for b in range(2):
                        e_ = f(prob[:, a % 2, b, :], src(a)[:, b, :], ACT.Exp, scale=scale,
                               bias=small[:, 2 * (a % 2) + b:2 * (a % 2) + b + 1],
                               accum_out=small[:, 4 + 2 * (a % 2) + b:5 + 2 * (a % 2) + b])
                    e_.then_inc(S["exp_done"], 1)

                exps(first)
                for a in range(first, first + count):
                    if a + 1 < first + count:
                        exps(a + 1)
                    act.wait_ge(S["pT_mm"], a + 1)
                    if a >= 2:
                        act.wait_ge(S["o_mm"], a - 1)
                    f(pT[:, a % 2, :, :], two(6 + a % 2), ACT.Copy).then_inc(S["pT_ready"], 1)
                    act.wait_ge(S["o_mm"], a + 1)
                    evacuate(a, two(4 + a % 2)).then_inc(S["o_ready"], 1)

            act.wait_ge(S["consts_loaded"], 32)
            norm(0, "eps5")
            act.wait_ge(S["pads_ready"], 3)
            act.wait_ge(S["lam_exp"], 1)
            chain.mark(f(small[:, 16:24], small[:, 16:24], ACT.Exp))
            for j in range(2):
                act.wait_ge(S["units_done"], j + 1)
                f(lxp[:, 2 * j:2 * j + 2, 2:2 + T], two(j), ACT.Copy).then_inc(S["lx_ready"], 1)
            for j in range(2):
                act.wait_ge(S["units_done"], AT["q"] + j + 1)
                f(tsq[:, j, :], PS[2 + j][:, :], ACT.Square).then_inc(S["qsq_ready"], 1)
                f(qg[:, 2 * j:2 * j + 2, :], two(2 + j), ACT.Identity, scale=V("gq"))\
                    .then_inc(S["qraw_ready"], 1)
            act.wait_ge(S["units_done"], AT["kv"] + 1)
            act.wait_ge(S["hstat_mm"], 1)
            f(tsq[:, 0, 0:T], PS[5][:, 0:T], ACT.Square).then_inc(S["qsq_ready"], 1)
            f(vt1[:, :, :], PS[5][:, T:2 * T].rearrange("p (a b) -> p a b", a=2), ACT.Copy)
            f(qg[:, 4, :], PS[5][:, 0:T], ACT.Identity, scale=V("gk")).then_inc(S["vk_ready"], 1)
            for j in range(2):
                act.wait_ge(S["units_done"], AT["lru_gate"] + j + 1)
                f(lgate[:, 2 * j:2 * j + 2, :], two(j), ACT.Copy).then_inc(S["lgate_ready"], 1)
            act.wait_ge(S["rot_mm"], 3)
            f(std[:, 0:T], PS[4][:, 0:T], ACT.Sqrt, scale=1.0 / 64, bias=V("eps6")).then_inc(S["hstd_ready"], 1)
            for j in range(2):
                act.wait_ge(S["qn_ready"], j + 1)
                f(std[:, :], PS[6 + j][:, :], ACT.Sqrt, scale=1.0 / 64, bias=V("eps6"))\
                    .then_inc(S["hstd_ready"], 1)
            for n in range(8):
                d, kind, j = n // 4, (n // 2) % 2, n % 2
                if n < 7:
                    act.wait_ge(S["lru_mm"], n + 1)
                else:
                    act.wait_ge(S["units_done"], AT["lru_w"] + 1)
                for c in range(2):
                    ch = 2 * j + c
                    last = f((ii if kind else rr)[:, 4 * d + ch, :], two(n % 2)[:, c, :], ACT.Sigmoid,
                             bias=V("lru_b", 8 * kind + 4 * d + ch))
                last.then_inc(S["lru_ev"], 1)
            act.wait_ge(S["r_ready"], 1)
            act.wait_ge(S["lru_ev"], 8)
            for n in range(8):
                f(th[:, n, :], rr[:, n, :], ACT.Tanh, scale=small[:, 24 + n:25 + n])
            chain.mark(f(gtmp[:, :, :], lgate[:, :, :], ACT.Square))
            chain.settle()
            for n in range(8):
                last = f(rr[:, n, :], rr[:, n, :], ACT.Exp, scale=small[:, 8 + n:9 + n])
            last.then_inc(S["lgsq_ready"], 1)
            act.wait_ge(S["m_ready"], 1)
            f(th[:, :, :], th[:, :, :], ACT.Sqrt).then_inc(S["mult_ready"], 1)
            act.wait_ge(S["ginner_ready"], 1)
            f(gtmp[:, :, :], gtmp[:, :, :], ACT.Sigmoid, scale=2.0 * float(np.sqrt(2.0 / np.pi)))\
                .then_inc(S["gsig_ready"], 1)
            heads(0, 8, 0.125, lambda a: two(2 + a % 2),
                  lambda a, bank: f(at1[64 * (a // 4):64 * (a // 4) + 64, a % 4, :],
                                    bank[64 * (a // 4):64 * (a // 4) + 64, 0, :], ACT.Copy))
            act.wait_ge(S["o_ready"], 8)
            f(sq[:, 0:4, :], at1[:, :, :], ACT.Square).then_inc(S["osq_ready"], 1)
            act.wait_ge(S["lru_ready"], 1)
            f(sq[:, 4:8, :], xc[:, :, :], ACT.Square).then_inc(S["osq_ready"], 1)
            act.wait_ge(S["ostat_mm"], 2)
            f(std[:, :], PS[0][:, :], ACT.Sqrt, scale=1.0 / 512, bias=V("eps5")).then_inc(S["ostd_ready"], 1)
            norm(1, "eps5")

            for g in range(4):
                act.wait_ge(S["tok_mm"], g + 1)
                f(xtok[:, g // 2, 512 * (g % 2):512 * (g % 2) + 512], PS[6 + g % 2][:, :], ACT.Copy)\
                    .then_inc(S["tok_ready"], 1)
            act.wait_ge(S["lg_ready"], 2)
            for tk in range(2):
                last = f(exr[:, tk, :], lg[:, tk, 0:E], ACT.Exp, bias=gs[:, tk:tk + 1])
            last.then_inc(S["gex_ready"], 1)
            act.wait_ge(S["gt_mm"], 1)
            f(GT[:, :], PS[4][0:E, 0:T], ACT.Copy).then_inc(S["gt_ready"], 1)

            def prepare_T(path, n, s):
                act.wait_ge(path.s["selT_mm"], n + 1)
                f(selgT[s][:, :], PS[6][0:SLOT, 0:T], ACT.Copy).then_inc(path.s["selT_ready"], 1)

            def prepare_x(path, n, s):
                act.wait_ge(path.s["xs_mm"], n + 1)
                f(xs[s][:, :, :], PS[6][:, :].rearrange("p (c n) -> p c n", c=C), ACT.Copy)\
                    .then_inc(path.s["xs_ready"], 1)

            def experts(path):
                act.sem_inc(path.s["y_ready"], 1)
                act.sem_inc(path.s["ylo_ready"], 1)
                prepare_T(path, 0, 0)
                prepare_x(path, 0, 0)
                with act.Fori(0, path.iters) as i:
                    for q in range(path.passes):
                        n, s = path.number(i, q), q % 2

                        def swish(half):
                            act.wait_ge(path.s["sig_in"], n * 2 + (half + 1))
                            f(sig[half][:, :, :], gu[half][:, 0:4, :], ACT.Sigmoid, scale=1.702)\
                                .then_inc(path.s["sig_ready"], 1)

                        act.wait_ge(path.s["scat_mm"], n + 1)
                        prepare_T(path, n + 1, 1 - s)
                        swish(0)
                        prepare_x(path, n + 1, 1 - s)
                        swish(1)
                        path.await_part(act, i, q, "d", 12)
                        f(yT[:, :, :], PS[7][:, :].rearrange("p (c n) -> p c n", c=C), ACT.Copy)\
                            .then_inc(path.s["y_ready"], 1)
                        act.wait_ge(path.s["tr_mm"], n + 1)
                        f(ytok[:, 0:512], PS[4][0:SLOT, :], ACT.Copy).then_inc(path.s["ylo_ready"], 1)

            act.wait_ge(S["flag_ready"], 1)
            most = act.value_load(flag[0:1, 0:1], min_val=0, max_val=T)
            with act.If(most < SLOT + 1):
                experts(PATHS[0])
            with act.Else():
                experts(PATHS[1])
            for j in range(4):
                act.wait_ge(S["moe_mm"], j + 1)
                f(xT[:, 2 * j:2 * j + 2, :], two(j), ACT.Copy).then_inc(S["xmoe_ready"], 1)
            norm(2, "eps5")
            norm(3)

            act.wait_ge(S["pads_ready"], 8)
            for j in range(4):
                act.wait_ge(S["units_done"], AT["iq"] + j + 1)
                f(iqr[:, 2 * j:2 * j + 2, :], two(j), ACT.Copy).then_inc(S["iq_ready"], 1)
            act.wait_ge(S["units_done"], AT["ikiw"] + 1)
            f(tv[:, 0, 0:T], PS[5][:, 0:T], ACT.Copy).then_inc(S["iq_ready"], 1)
            f(iw[:, :, :], PS[5][:, T:T + 32].rearrange("p (a b) -> p a b", a=2), ACT.Copy, scale=1.0 / 32)\
                .then_inc(S["iw_ready"], 1)
            def relu(h):
                act.wait_ge(S["iscore_mm"], h + 1)
                if h >= 2:
                    act.wait_ge(S["relu_used"], h - 1)
                f(rl[h % 2][:, :, :], two(h % 2), ACT.Relu).then_inc(S["relu_ready"], 1)

            for j in range(4):
                act.wait_ge(S["units_done"], AT["dq"] + j + 1)
                if j >= 2:
                    act.wait_ge(S["dstat_mm"], j - 1)
                if j == 0:
                    act.wait_ge(S["iqn_ready"], 4)
                f(tsq[:, j % 2, :], PS[2 + j % 2][:, :], ACT.Square).then_inc(S["dsq_ready"], 1)
                f(dqk[:, 2 * j:2 * j + 2, :], two(2 + j % 2), ACT.Identity, scale=V("aq" if j < 2 else "ak"))\
                    .then_inc(S["dqk_ready"], 1)
                for h in range(4 * j, 4 * j + 4):
                    relu(h)
                act.wait_ge(S["dstat_mm"], j + 1)
                if j:
                    act.wait_ge(S["dqn_ready"], j)
                f(std[:, :], PS[4][:, :], ACT.Sqrt, scale=1.0 / P, bias=V("eps6")).then_inc(S["dstd_ready"], 1)
            act.wait_ge(S["units_done"], AT["dv"] + 2)
            for b in range(2):
                f(dv[:, b, :], PS[6 + b][:, :], ACT.Copy).then_inc(S["dv_ready"], 1)
            for j in range(2):
                act.wait_ge(S["units_done"], AT["u"] + j + 1)
                f(up[:, 2 * j:2 * j + 2, 16:272], two(j), ACT.Copy).then_inc(S["u_ready"], 1)
            act.wait_ge(S["relu_used"], 16)
            act.wait_ge(S["units_done"], AT["pool"] + 1)
            for g in range(4):
                f(mix[:, 4 + g, :], two(g // 2)[:, g % 2, :], ACT.Identity, scale=V("pool_scale", g))\
                    .then_inc(S["pool_mix"], 1)
            heads(8, 4, 1.0, lambda a: tv[:, a % 2, :].rearrange("p (b t) -> p b t", b=2),
                  lambda a, bank: f(mix[:, a - 8, :], bank[:, 0, :], ACT.Copy))

            def cross(l):
                if l == 0:
                    act.wait_ge(S["stat_mm"], 5)
                    act.wait_ge(S["mem_loaded"], 16)
                    for j in range(4):
                        f(sq[:, 2 * j:2 * j + 2, :], memT[0][:, 2 * j:2 * j + 2, :], ACT.Square)\
                            .then_inc(S["msq_ready"], 1)
                    act.wait_ge(S["mstat_mm"], 1)
                    f(rmem, PS[5][:, 0:T], ACT.Sqrt, scale=1.0 / D, bias=V("eps6")).then_inc(S["mstd_ready"], 1)
                for side, name, first, dst in ((0, "ckg", AT[f"ck{l}"], ckn), (1, "cqg", AT[f"cq{l}"], cqn)):
                    for j in range(4):
                        p = 8 * l + 4 * side + j
                        act.wait_ge(S["units_done"], first + j + 1)
                        if p >= 2:
                            act.wait_ge(S["ckstat_mm"], p - 1)
                        f(tsq[:, p % 2, :], PS[2 + j % 2][:, :], ACT.Square).then_inc(S["cksq_ready"], 1)
                        for c in range(2):
                            last = f(dst[:, 2 * j + c, :], two(2 + j % 2)[:, c, :], ACT.Identity,
                                     scale=V(f"{name}{l}", c))
                        last.then_inc(S["ck_raw"], 1)
                        act.wait_ge(S["ckstat_mm"], p + 1)
                        if p:
                            act.wait_ge(S["ckn_ready"], p)
                        f(std[:, T:2 * T], PS[5][:, T:2 * T], ACT.Sqrt, scale=1.0 / T, bias=V("eps6"))\
                            .then_inc(S["ckstd_ready"], 1)
                    if side == 0:
                        act.wait_ge(S["units_done"], AT[f"cv{l}"] + 4)
                        for b in range(2):
                            for hf in range(2):
                                f(cvt[:, b, 512 * hf:512 * hf + 512], PS[(0, 1, 6, 7)[2 * b + hf]][:, :],
                                  ACT.Copy).then_inc(S["cv_ready"], 1)
                heads(12 + 4 * l, 4, 1.0 / 16, lambda a: two(2 + a % 2),
                      lambda a, bank: f(co[:, 2 * ((a - 12) % 4):2 * ((a - 12) % 4) + 2, :], bank, ACT.Copy))

            def ffn(l):
                for g in range(NG):
                    act.wait_ge(S["units_done"], AT[f"ffn{l}"] + ffn_gate_unit(g) + 1)
                    f(fs[g % 2][:, :, :], two(4 + 2 * (g % 2)), ACT.Sigmoid).then_inc(S["f_sig"], 1)

            norm(4)
            cross(0)
            norm(5)
            ffn(0)
            norm(6)
            for j in range(8):
                act.wait_ge(S["units_done"], AT["conv_in"] + j + 1)
                if j >= 2:
                    act.wait_ge(S["hp_ready"], j - 1)
                f(csg[:, j % 2, :], two(j % 4)[:, 1, :], ACT.Sigmoid, bias=V("cin_b", 8 + j))\
                    .then_inc(S["conv_sig"], 1)
            for c in range(4):
                for t in range(TAPS):
                    n = c * TAPS + t
                    if n >= NDIAG:
                        act.wait_ge(S["dwc_mm"], n - NDIAG + 1)
                    f(diag[:, n % NDIAG, :], tb("ident"), ACT.Copy, scale=V("dw", n))\
                        .then_inc(S["diag_ready"], 1)
                act.wait_ge(S["dwc_mm"], (c + 1) * TAPS)
                f(hc[:, c, :], PS[4 + c][:, 0:T], ACT.Identity, bias=V("dw_b", c))\
                    .then_inc(S["hc_pe"], 1)
            for j in range(4):
                act.wait_ge(S["lnd_ready"], j + 1)
                f(sq[:, 2 * j:2 * j + 2, :], hc[:, 2 * j:2 * j + 2, :], ACT.Square).then_inc(S["lnsq_ready"], 1)
            act.wait_ge(S["lnvar_mm"], 1)
            f(std[:, 0:T], PS[1][:, 0:T], ACT.Sqrt, scale=1.0 / D, bias=V("eps6")).then_inc(S["lnstd_ready"], 1)
            for c in range(C):
                act.wait_ge(S["lnz_ready"], c + 1)
                f(sq[:, c, :], hc[:, c, :], ACT.Sigmoid, bias=V("ln_b", c)).then_inc(S["lnsig_ready"], 1)
            norm(7)
            cross(1)
            norm(8)
            ffn(1)

        @block.vector
        def _(dve):
            chain = Chain(dve, S["dve_chain"])
            link, mark, settle = chain.link, chain.mark, chain.settle
            tt, ts, stt = dve.tensor_tensor, dve.tensor_scalar, dve.scalar_tensor_tensor

            def norm(n, gain, dst):
                dve.wait_ge(S["std_ready"], n + 1)
                link(dve.reciprocal(rinv[:, 0:T], std[:, 0:T]))
                for k in range(C):
                    stt(dst[:, k, :], xT[:, k, :], V(gain, k), rinv[:, 0:T], ALU.mult, ALU.mult)\
                        .then_inc(S["xn_ready"], 1)

            def residual(first):
                for j in range(4):
                    dve.wait_ge(S["units_done"], first + j + 1)
                    tt(xT[:, 2 * j:2 * j + 2, :], two(j), xT[:, 2 * j:2 * j + 2, :], ALU.add)\
                        .then_inc(S["res_ready"], 1)

            def heads(first, count, scale, between=None, sparse=False):
                def maxima(a):
                    dve.wait_ge(S["score_mm"], a + 1)
                    bank = two(2 + a % 2)
                    if a - first >= 2:
                        dve.wait_ge(S["exp_done"], a - 1)
                    if a:
                        dve.wait_ge(S["nmax_ready"], a)
                    if sparse:
                        src = tv[:, a % 2, :].rearrange("p (b t) -> p b t", b=2)
                        link(stt(src, bank, scale, pen[:, :, :], ALU.mult, ALU.add))
                        bank = src
                    link(dve.tensor_reduce(mx[:, :], bank, AX, ALU.max))
                    ts(small[:, 2 * (a % 2):2 * (a % 2) + 2], mx[:, :], -1.0 if sparse else -scale, None, ALU.mult)\
                        .then_inc(S["nmax_ready"], 1)

                def divide(a):
                    dve.wait_ge(S["exp_done"], a + 1)
                    if a:
                        dve.wait_ge(S["probs_ready"], a)
                    o = 4 + 2 * (a % 2)
                    link(dve.reciprocal(rs[:, :], small[:, o:o + 2]))
                    tt(prob[:, a % 2, :, :], prob[:, a % 2, :, :], along(rs[:, :], T), ALU.mult)\
                        .then_inc(S["probs_ready"], 1)

                maxima(first)
                for a in range(first, first + count):
                    if a + 1 < first + count:
                        maxima(a + 1)
                    divide(a)
                    if between:
                        between(a)

            dve.wait_ge(S["consts_loaded"], 32)
            ea, rate_n, rate_p = small[:, 16:24], small[:, 8:16], small[:, 24:32]
            link(ts(rate_n, V("lam", 0, 8), -1.0, None, ALU.mult))
            ts(ea, V("lam", 0, 8), 0.0, None, ALU.max)
            link(ts(rate_p, rate_n, 0.0, None, ALU.max))
            link(tt(ea, ea, rate_p, ALU.add))
            ts(ea, ea, -1.0, None, ALU.mult).then_inc(S["lam_exp"], 1)
            norm(0, "norm1", xn)
            dve.wait_ge(S["act_chain"], 1)
            z, z2, ser = lam3[:, 0:8], lam3[:, 8:16], lam3[:, 16:24]
            link(ts(z, ea, 2.0, None, ALU.add))
            link(dve.reciprocal(z, z))
            link(tt(z, z, ea, ALU.mult))
            link(tt(z2, z, z, ALU.mult))
            link(ts(ser, z2, 1.0 / 19, 1.0 / 17, ALU.mult, ALU.add))
            for k in range(15, 0, -2):
                link(tt(ser, ser, z2, ALU.mult))
                link(ts(ser, ser, 1.0 / k, None, ALU.add))
            link(stt(ser, ser, 2.0, z, ALU.mult, ALU.mult))
            link(tt(ser, ser, rate_p, ALU.add))
            ts(rate_n, ser, -8.0, None, ALU.mult)
            ts(rate_p, ser, 8.0, None, ALU.mult).then_inc(S["r_ready"], 1)
            dve.wait_ge(S["pads_ready"], 3)
            for c in range(4):
                dve.wait_ge(S["lx_ready"], c // 2 + 1)
                link(ts(xc[:, c, :], lxp[:, c, 0:T], V("conv_w", 4 * c), V("conv_b", c), ALU.mult, ALU.add))
                for t in range(1, 4):
                    o = stt(xc[:, c, :], lxp[:, c, t:t + T], V("conv_w", 4 * c + t), xc[:, c, :],
                            ALU.mult, ALU.add)
                    if t < 3:
                        link(o)
                o.then_inc(S["xc_ready"], 1)

            def rotated(src, rot, n, dst, cos, sin):
                link(tt(tv[:, 0, 0:n * T].rearrange("p (a t) -> p a t", a=n), src, over(tb(cos), n), ALU.mult))
                link(tt(tv[:, 1, 0:n * T].rearrange("p (a t) -> p a t", a=n), rot, over(tb(sin), n), ALU.mult))
                return tt(dst, tv[:, 0, 0:n * T].rearrange("p (a t) -> p a t", a=n),
                          tv[:, 1, 0:n * T].rearrange("p (a t) -> p a t", a=n), ALU.add)

            dve.wait_ge(S["rot_mm"], 3)
            dve.wait_ge(S["hstd_ready"], 1)
            link(dve.reciprocal(rinv[:, 0:T], std[:, 0:T]))
            link(rotated(qg[:, 4:5, :], PS[4][:, T:2 * T].unsqueeze(1), 1, qg[:, 4:5, :], "cos1", "sin1"))
            mark(tt(kz[0:64, 0, :], qg[0:64, 4, :], rinv[0:64, 0:T], ALU.mult))
            tt(kz[64:128, 1, :], qg[64:128, 4, :], rinv[64:128, 0:T], ALU.mult).then_inc(S["qn_ready"], 1)
            for j in range(2):
                dve.wait_ge(S["hstd_ready"], j + 2)
                link(dve.reciprocal(rinv[:, :], std[:, :]))
                pair = qg[:, 2 * j:2 * j + 2, :]
                link(rotated(pair, two(2 + j), 2, pair, "cos1", "sin1"))
                tt(pair, pair, rinv[:, :].rearrange("p (a t) -> p a t", a=2), ALU.mult)\
                    .then_inc(S["qn_ready"], 1)

            dve.wait_ge(S["lgsq_ready"], 1)
            lg_, x_ = lgate[:, :, :], gtmp[:, :, :]
            link(tt(sq[:, :, :], rr[:, :, :], rr[:, :, :], ALU.mult))
            stt(th[:, :, :], sq[:, :, :], 1.0, th[:, :, :], ALU.add, ALU.mult).then_inc(S["m_ready"], 1)
            link(ts(x_, x_, 0.044715, 1.0, ALU.mult, ALU.add))
            tt(x_, x_, lg_, ALU.mult).then_inc(S["ginner_ready"], 1)
            bt = ii[:, :, :].rearrange("p (d c) t -> p d c t", d=2)
            link(tt(bt, bt, xc[:, :, :].unsqueeze(1).broadcast_to((P, 2, 4, T)), ALU.mult))
            dve.wait_ge(S["mult_ready"], 1)
            link(tt(ii[:, :, :], ii[:, :, :], th[:, :, :], ALU.mult))

            def lru_tail(a):
                if a < 4:
                    c = a
                    dve.tensor_tensor_scan(th[:, c, :], rr[:, c, :], ii[:, c, :], 0.0, ALU.mult, ALU.add)
                    mark(dve.tensor_tensor_scan(th[:, 4 + c, ::-1], rr[:, 4 + c, ::-1], ii[:, 4 + c, ::-1], 0.0,
                                                ALU.mult, ALU.add))
                if a == 4:
                    dve.wait_ge(S["gsig_ready"], 1)
                    mark(tt(lg_, lg_, x_, ALU.mult))
                    settle()
                    link(tt(xc[:, :, :], th[:, 0:4, :], th[:, 4:8, :], ALU.add))
                    tt(xc[:, :, :], xc[:, :, :], lg_, ALU.mult).then_inc(S["lru_ready"], 1)

            heads(0, 8, 0.125, between=lru_tail)
            dve.wait_ge(S["ostd_ready"], 1)
            link(dve.reciprocal(rinv[:, :], std[:, :]))
            for k in range(C):
                src, g = (at1, "attn_g") if k < 4 else (xc, "lru_g")
                stt(xn[:, k, :], src[:, k % 4, :], V(g, k % 4), rinv[:, T * (k // 4):T * (k // 4) + T],
                    ALU.mult, ALU.mult).then_inc(S["mixed_ready"], 1)
            residual(AT["w_out"])
            norm(1, "norm2", xn)

            dve.wait_ge(S["rout_mm"], 1)
            dve.wait_ge(S["pads_ready"], 6)
            tt(lg[:, :, 0:E], PS[5][:, 0:2 * E].rearrange("p (a e) -> p a e", a=2), over(br[:, :], 2), ALU.add)\
                .then_inc(S["lg_ready"], 1)
            dve.wait_ge(S["lg_ready"], 1)
            for tk in range(2):
                mark(dve.max(m8[:, tk, :], lg[:, tk, 0:E]))
            settle()
            ts(gs[:, 0:2].unsqueeze(2), m8[:, :, 0:1], -1.0, None, ALU.mult).then_inc(S["lg_ready"], 1)
            link(dve.memset(m8[:, :, 4:8], 3.0e38))
            for tk in range(2):
                mark(dve.match_replace(lg2[:, tk, 0:E + 4], m8[:, tk, :], lg[:, tk, 0:E + 4], FAR))
            settle()
            ts(msk[:, :, :], lg2[:, :, 0:E], 0.9 * FAR, None, ALU.is_le).then_inc(S["mask_ready"], 1)
            dve.wait_ge(S["mask_ready"], 1)
            dve.wait_ge(S["gex_ready"], 1)
            link(tt(exr[:, :, :], exr[:, :, :], msk[:, :, :], ALU.mult))
            link(dve.tensor_reduce(gs[:, 2:4], exr[:, :, :], AX, ALU.add))
            link(dve.reciprocal(gs[:, 2:4], gs[:, 2:4]))
            tt(G[:, :, 0:E], exr[:, :, :], along(gs[:, 2:4], E), ALU.mult).then_inc(S["lg_ready"], 1)
            dve.wait_ge(S["cnt_mm"], 1)
            cp = PS[5][:, 64:64 + 3 * E].rearrange("p (a e) -> p a e", a=3)
            link(stt(key[:, :, 0:E], cp[:, 0:2, :], 1.0, msk[:, :, :], ALU.add, ALU.mult))
            link(ts(key[:, :, 0:E], key[:, :, 0:E], -1.0, None, ALU.add))
            link(dve.tensor_reduce(cnt[:, 0:1], cp[:, 2, :], AX, ALU.max))
            dve.tensor_copy(flag[:, :], cnt[:, 0:1]).then_inc(S["flag_ready"], 1)

            def select(path, e, b, n, s, loop):
                io = tb("iota")[:, b * SLOT:(b + 1) * SLOT]
                for tk in range(2):
                    k_, g_ = key[:, tk, bass.ds(e, 1)], G[:, tk, bass.ds(e, 1)]
                    ts(sel[s][:, tk, :], io, k_, None, ALU.is_equal)
                    last = ts(selg[s][:, tk, :], io, k_, g_, ALU.is_equal, ALU.mult)
                last.then_inc(path.s["sel_ready"], 1)

            def experts(path):
                dve.sem_inc(path.s["yhi_ready"], 1)
                select(path, 0, 0, 0, 0, False)
                LINKS = 8
                with dve.Fori(0, path.iters) as i:
                    mlink = Chain(dve, path.s["chain"], i * (LINKS * path.passes))
                    for q in range(path.passes):
                        n, s = path.number(i, q), q % 2
                        e = path.expert(i, q)
                        ne, nb = path.following(i, q)
                        select(path, ne, nb, n + 1, 1 - s, True)
                        for half in range(2):
                            path.await_part(dve, i, q, "b" if half else "a", 8 if half else 4)
                            g8 = gu[half]
                            bias = mbias[:, bass.ds(e * 16 + 8 * half, 8)]
                            bk = PS[4 + half][:, :].rearrange("p (c n) -> p c n", c=8)
                            mlink.link(tt(g8[:, :, :], bk, along(bias, SLOT), ALU.add))
                            ts(g8[:, 0:4, :], g8[:, 0:4, :], 7.0, None, ALU.min)\
                                .then_inc(path.s["sig_in"], 1)
                            mlink.link(ts(g8[:, 4:8, :], g8[:, 4:8, :], 7.0, -7.0, ALU.min, ALU.max))
                            mlink.link(ts(g8[:, 4:8, :], g8[:, 4:8, :], 1.0, None, ALU.add))
                            mlink.link(tt(g8[:, 4:8, :], g8[:, 4:8, :], g8[:, 0:4, :], ALU.mult))
                            dve.wait_ge(path.s["sig_ready"], n * 2 + (half + 1))
                            if half == 0:
                                dve.wait_ge(path.s["y_ready"], n + 1)
                            tt(hT[:, 4 * half:4 * half + 4, :], g8[:, 4:8, :], sig[half][:, :, :], ALU.mult)\
                                .then_inc(path.s["h_ready"], 1)
                        dve.wait_ge(path.s["tr_mm"], n + 1)
                        dve.tensor_copy(ytok[:, 512:1024], PS[5][0:SLOT, :]).then_inc(path.s["yhi_ready"], 1)
                    assert mlink.n == LINKS * path.passes

            dve.wait_ge(S["flag_ready"], 1)
            dve.wait_ge(S["router_loaded"], 48)
            most = dve.value_load(flag[0:1, 0:1], min_val=0, max_val=T)
            with dve.If(most < SLOT + 1):
                experts(PATHS[0])
            with dve.Else():
                experts(PATHS[1])

            norm(2, "final", xT)
            norm(3, "mix0", xn)

            for j in range(5):
                dve.wait_ge(S["iqrot_mm"], j + 1)
                if j < 4:
                    pair = iqr[:, 2 * j:2 * j + 2, :]
                    cs = iqt
                    if j:
                        dve.wait_ge(S["iqn_ready"], j)
                    link(tt(cs[:, :, :], pair, over(tb("cos3"), 2), ALU.mult))
                    tt(tsq[:, 0, :].rearrange("p (a t) -> p a t", a=2), two(6 + j % 2), over(tb("sin3"), 2),
                       ALU.mult).then_inc(S["iqrot_read"], 1)
                    dve.wait_ge(S["iqrot_read"], j + 1)
                    tt(pair, cs[:, :, :], tsq[:, 0, :].rearrange("p (a t) -> p a t", a=2), ALU.add)\
                        .then_inc(S["iqn_ready"], 1)
                else:
                    dve.wait_ge(S["iqn_ready"], 4)
                    link(tt(iqt[:, 0, :], tv[:, 0, 0:T], tb("cos3"), ALU.mult))
                    tt(iqt[:, 1, :], PS[6][:, 0:T], tb("sin3"), ALU.mult).then_inc(S["iqrot_read"], 1)
                    dve.wait_ge(S["iqrot_read"], 5)
                    dve.wait_ge(S["pads_ready"], 8)
                    tt(iz[0:64, 0, :], iqt[0:64, 0, :], iqt[0:64, 1, :], ALU.add)
                    tt(iz[64:128, 1, :], iqt[64:128, 0, :], iqt[64:128, 1, :], ALU.add)\
                        .then_inc(S["iqn_ready"], 1)
            dve.wait_ge(S["iw_ready"], 1)

            def add_index(h):
                dve.wait_ge(S["relu_ready"], h + 1)
                for b in range(2):
                    if h == 0:
                        last = ts(sc[:, b, :], rl[0][:, b, :], iw[:, b, 0:1], None, ALU.mult)
                    else:
                        if b == 0:
                            dve.wait_ge(S["relu_used"], h)
                        last = stt(sc[:, b, :], rl[h % 2][:, b, :], iw[:, b, h:h + 1], sc[:, b, :],
                                   ALU.mult, ALU.add)
                last.then_inc(S["relu_used"], 1)

            for j in range(4):
                for h in range(4 * j, 4 * j + 4):
                    add_index(h)
                dve.wait_ge(S["drot_mm"], j + 1)
                dve.wait_ge(S["dstd_ready"], j + 1)
                link(dve.reciprocal(rinv[:, :], std[:, :]))
                pair = dqk[:, 2 * j:2 * j + 2, :]
                link(rotated(pair, two(5), 2, pair, "cos2", "sin2"))
                tt(pair, pair, rinv[:, :].rearrange("p (a t) -> p a t", a=2), ALU.mult)\
                    .then_inc(S["dqn_ready"], 1)
            dve.wait_ge(S["relu_used"], 16)
            link(tt(sc[:, :, :], sc[:, :, :], tb("far").rearrange("p (b t) -> p b t", b=2), ALU.add))
            dve.wait_ge(S["u_ready"], 2)
            link(tt(w1[:, :, 1:272], up[:, :, 1:272], up[:, :, 0:271], ALU.add))
            link(tt(w2[:, 1:4, 3:272], w1[:, 1:4, 3:272], w1[:, 1:4, 1:270], ALU.add))
            link(tt(w1[:, 2:4, 7:272], w2[:, 2:4, 7:272], w2[:, 2:4, 3:268], ALU.add))
            link(tt(w2[:, 3:4, 15:272], w1[:, 3:4, 15:272], w1[:, 3:4, 7:264], ALU.add))
            rc = tb("rcount").rearrange("p (g t) -> p g t", g=4)
            for g in range(4):
                w = w2 if g % 2 else w1
                mark(tt(iqt[:, 0, 16 * g:16 * g + 16], w[:, g, 16:32], rc[:, g, :], ALU.mult))
                link(stt(iqt[:, 1, :], w[:, g, 16:272], 0.5 ** (g + 1), up[:, g, 16:272], ALU.mult, ALU.subtract))
                mark(dve.tensor_copy(w1[:, g, 16:256], iqt[:, 1, 16:256]))
                tt(w1[:, g, 0:16], iqt[:, 0, 16 * g:16 * g + 16], up[:, g, 16:32], ALU.subtract)\
                    .then_inc(S["pooled_ready"], 1)
                dve.wait_ge(S["pooled_ready"], g + 1)
            for rnd in range(ROUNDS):
                for b in range(2):
                    mark(dve.max(m8b[:, b, :], sc[:, b, :]))
                settle()
                for b in range(2):
                    mark(dve.match_replace(sc[:, b, :], m8b[:, b, :], sc[:, b, :], TAKEN))
                settle()
            link(ts(pen[:, :, :], sc[:, :, :], 0.5 * (FAR + TAKEN), 1.0e30, ALU.is_le, ALU.mult))
            link(stt(pen[:, :, :], pen[:, :, :], -1.0e30, tb("far").rearrange("p (b t) -> p b t", b=2),
                     ALU.add, ALU.add))
            heads(8, 4, float(P) ** -0.5, sparse=True)
            residual(AT["ab_out"])

            def memory(l):
                if l == 0:
                    dve.wait_ge(S["mstd_ready"], 1)
                    link(dve.reciprocal(rmem, rmem))
                dve.wait_ge(S["mem_loaded"], 16 * (l + 1))
                for k in range(C):
                    stt(memn[:, k, :], memT[l][:, k, :], V(f"mem{l}", k), rmem, ALU.mult, ALU.mult)\
                        .then_inc(S["memn_ready"], 1)

            def cross_norms(l, side, dst):
                for j in range(4):
                    p = 8 * l + 4 * side + j
                    dve.wait_ge(S["ckstd_ready"], p + 1)
                    link(dve.reciprocal(rinv[:, T:2 * T], std[:, T:2 * T]))
                    pair = dst[:, 2 * j:2 * j + 2, :]
                    tt(pair, pair, over(rinv[:, T:2 * T], 2), ALU.mult).then_inc(S["ckn_ready"], 1)

            def cross(l):
                norm(4 + 3 * l, f"cross{l}", xn)
                memory(l)
                cross_norms(l, 0, ckn)
                cross_norms(l, 1, cqn)
                heads(12 + 4 * l, 4, 1.0 / 16)
                residual(AT[f"co{l}"])
                norm(5 + 3 * l, f"ffn{l}", xn)

            def ffn(l):
                for g in range(NG):
                    n = NG * l + g
                    dve.wait_ge(S["f_sig"], n + 1)
                    gb, ub = two(4 + 2 * (g % 2)), two(5 + 2 * (g % 2))
                    link(tt(fs[g % 2][:, :, :], gb, fs[g % 2][:, :, :], ALU.mult))
                    dve.wait_ge(S["units_done"], AT[f"ffn{l}"] + ffn_gate_unit(g) + 2)
                    tt(fh[g % 2][:, :, :], ub, fs[g % 2][:, :, :], ALU.mult).then_inc(S["f_h"], 1)
                dve.wait_ge(S["units_done"], AT[f"ffn{l}"] + 3 * NG)
                for j in range(4):
                    tt(xT[:, 2 * j:2 * j + 2, :], two(j), xT[:, 2 * j:2 * j + 2, :], ALU.add)\
                        .then_inc(S["res_ready"], 1)

            cross(0)
            ffn(0)
            norm(6, "mix1", xn)
            dve.wait_ge(S["pads_ready"], 9)
            for j in range(8):
                dve.wait_ge(S["conv_sig"], j + 1)
                stt(hp[:, j, 30:30 + T], two(j % 4)[:, 0, :], V("cin_b", j), csg[:, j % 2, :], ALU.add, ALU.mult)\
                    .then_inc(S["hp_ready"], 1)
            dve.wait_ge(S["hp_ready"], 8)
            for t in range(TAPS):
                for c in range(4, C):
                    w = V("dw", c * TAPS + t)
                    if t == 0:
                        mark(ts(hc[:, c, :], hp[:, c, 0:T], w, V("dw_b", c), ALU.mult, ALU.add))
                    elif t < TAPS - 1:
                        dve.wait_ge(S["dve_chain"], chain.n - 3)
                        mark(stt(hc[:, c, :], hp[:, c, t:t + T], w, hc[:, c, :], ALU.mult, ALU.add))
                    else:
                        settle()
                        stt(hc[:, c, :], hp[:, c, t:t + T], w, hc[:, c, :], ALU.mult, ALU.add)\
                            .then_inc(S["hc_dve"], 1)
            dve.wait_ge(S["lnsum_mm"], 1)
            dve.wait_ge(S["hc_dve"], 4)
            dve.wait_ge(S["hc_pe"], 4)
            link(ts(rinv[:, 0:T], PS[0][:, 0:T], 1.0 / D, None, ALU.mult))
            for j in range(4):
                pair = hc[:, 2 * j:2 * j + 2, :]
                tt(pair, pair, over(rinv[:, 0:T], 2), ALU.subtract).then_inc(S["lnd_ready"], 1)
            dve.wait_ge(S["lnstd_ready"], 1)
            link(dve.reciprocal(rinv[:, 0:T], std[:, 0:T]))
            for c in range(C):
                stt(hc[:, c, :], hc[:, c, :], V("ln_g", c), rinv[:, 0:T], ALU.mult, ALU.mult)\
                    .then_inc(S["lnz_ready"], 1)
            for c in range(C):
                dve.wait_ge(S["lnsig_ready"], c + 1)
                stt(yc[:, c, :], hc[:, c, :], V("ln_b", c), sq[:, c, :], ALU.add, ALU.mult)\
                    .then_inc(S["yc_ready"], 1)
            residual(AT["conv_out"])
            cross(1)
            ffn(1)



def columns(v):
    return v.reshape(-1, P).T


def stationary_units(w):
    n = w.shape[1] // 256
    return w.reshape(C, P, n, 2, P).transpose(2, 1, 3, 0, 4).reshape(n, P, UNIT)


def row_units(w):
    kk = UNIT // w.shape[1]
    n = w.shape[0] // (P * kk)
    return w.reshape(n, kk, P, w.shape[1]).transpose(0, 2, 1, 3).reshape(n, P, UNIT)


def lay_out_stream(a):
    s = np.zeros((N_UNITS, P, UNIT), np.float32)

    def put(name, units):
        s[AT[name]:AT[name] + len(units)] = units

    w = a["w_in"][0]
    put("lru_x", stationary_units(w[:, 768:1280]))
    put("q", stationary_units(w[:, 0:512].reshape(D, 2, 4, 64).transpose(0, 2, 1, 3).reshape(D, 512)))
    put("kv", stationary_units(w[:, 512:768]))
    put("lru_gate", stationary_units(w[:, 1280:1792]))
    gates = s[AT["lru_w"]].reshape(P, 2, 2, 4, P)
    for kind, name in enumerate(("lru_wa", "lru_wi")):
        for d in range(2):
            for c in range(4):
                for h in range(2):
                    r = slice(64 * h, 64 * h + 64)
                    gates[r, d, kind, c, r] = a[name][0, d, 2 * c + h]
    w = a["w_out"][0]
    w = np.concatenate([w[:512].reshape(2, 4, 64, D).transpose(1, 0, 2, 3).reshape(512, D), w[512:]])
    put("w_out", stationary_units(w))
    moe = s[AT["moe"]:AT["moe"] + 12 * E].reshape(E, 12, P, UNIT)
    for e in range(E):
        g, u = (stationary_units(a[n][0, e]) for n in ("w_gate", "w_up"))
        for half in range(2):
            moe[e, 4 * half:4 * half + 2] = g[2 * half:2 * half + 2]
            moe[e, 4 * half + 2:4 * half + 4] = u[2 * half:2 * half + 2]
        moe[e, 8:12] = row_units(a["w_down"][0, e])
    w = a["w_in_ab_2"][0]
    put("dq", stationary_units(w[:, 0:512]))
    put("dk", stationary_units(w[:, 512:1024]))
    put("dv", row_units(w[:, 1024:1536]))
    put("u", stationary_units(w[:, 1536:2048]))
    put("iq", stationary_units(w[:, 2048:3072]))
    one = s[AT["ikiw"]]
    ik = w[:, 3088:3152]
    one[:, 0:D] = np.concatenate([ik, ik], 1).reshape(C, P, P).transpose(1, 0, 2).reshape(P, D)
    one[:, D:D + 16 * C] = w[:, 3072:3088].reshape(C, P, 16).transpose(1, 0, 2).reshape(P, 16 * C)
    s[AT["pool"]][:, 0:4 * P] = a["pool_w_2"][0].transpose(1, 0, 2).reshape(P, 4 * P)
    put("ab_out", stationary_units(a["w_out_ab_2"][0]))
    put("conv_in", stationary_units(a["conv_w_in_2"][0].reshape(D, 2, C, P).transpose(0, 2, 1, 3)
                                    .reshape(D, 2 * D)))
    put("conv_out", stationary_units(a["conv_w_out_2"][0]))
    for l in range(2):
        put(f"ck{l}", stationary_units(a["cross_wk_2"][l]))
        put(f"cv{l}", row_units(a["cross_wv_2"][l]))
        put(f"cq{l}", stationary_units(a["cross_wq_2"][l]))
        put(f"co{l}", stationary_units(a["cross_wo_2"][l]))
        f = s[AT[f"ffn{l}"]:AT[f"ffn{l}"] + 3 * NG]
        g, u = (stationary_units(a[n][l]) for n in ("ffn_w_gate_2", "ffn_w_up_2"))
        d = row_units(a["ffn_w_down_2"][l])
        for i in range(NG):
            f[ffn_gate_unit(i)] = g[i]
            f[ffn_gate_unit(i) + 1] = u[i]
            f[min(3 * i + 4, 3 * NG - 1)] = d[i]
    return s


def lay_out_vectors(a):
    v = np.zeros((P, NV), np.float32)

    def put(name, m):
        v[:, VAT[name]:VAT[name] + m.shape[1]] = m

    for name, value in (("norm1", a["norm1_g"][0]), ("norm2", a["norm2_g"][0]), ("final", a["final_g"]),
                        ("mix0", a["norm_mix_2"][0]), ("mix1", a["norm_mix_2"][1]),
                        ("cross0", a["norm_cross_2"][0]), ("cross1", a["norm_cross_2"][1]),
                        ("mem0", a["norm_mem_2"][0]), ("mem1", a["norm_mem_2"][1]),
                        ("ffn0", a["norm_ffn_2"][0]), ("ffn1", a["norm_ffn_2"][1]),
                        ("gq", np.concatenate([a["q_norm_g"][0]] * 2)),
                        ("gk", np.concatenate([a["k_norm_g"][0]] * 2)),
                        ("conv_b", a["conv_b"][0]), ("lam", a["lru_lam"][0]),
                        ("lru_b", np.concatenate([a["lru_ba"][0].ravel(), a["lru_bi"][0].ravel()])),
                        ("attn_g", a["attn_out_g"][0].reshape(2, 4, 64).transpose(1, 0, 2)),
                        ("lru_g", a["lru_out_g"][0]), ("aq", a["a_q_norm_2"][0]), ("ak", a["a_k_norm_2"][0]),
                        ("pool_scale", a["pool_scale_2"][0]), ("cin_b", a["conv_b_in_2"][0]),
                        ("dw_b", a["conv_dw_b_2"][0]), ("ln_g", a["conv_ln_g_2"][0]),
                        ("ln_b", a["conv_ln_b_2"][0]), ("cqg0", a["cross_q_norm_2"][0]),
                        ("cqg1", a["cross_q_norm_2"][1]), ("ckg0", a["cross_k_norm_2"][0]),
                        ("ckg1", a["cross_k_norm_2"][1])):
        put(name, columns(value))
    put("conv_w", a["conv_w"][0].reshape(4, 4, P).transpose(2, 1, 0).reshape(P, 16))
    put("dw", a["conv_dw_w_2"][0].reshape(TAPS, C, P).transpose(2, 1, 0).reshape(P, C * TAPS))
    v[:, VAT["eps5"]] = 1e-5
    v[:, VAT["eps6"]] = 1e-6
    return v


def rotary(heads_at, half, inv, positions):
    cos, sin, rot = np.ones((P, T), np.float32), np.zeros((P, T), np.float32), np.zeros((P, P), np.float32)
    for start, pos in zip(heads_at, positions):
        ang = inv[:, None].astype(np.float32) * pos[None, :].astype(np.float32)
        for i in range(half):
            lo, hi = start + i, start + half + i
            cos[lo] = cos[hi] = np.cos(ang[i])
            sin[lo] = sin[hi] = np.sin(ang[i])
            rot[hi, lo] = -1.0
            rot[lo, hi] = 1.0
    return cos, sin, rot


def lay_out_tables():
    t = np.zeros((P, NT), np.float32)

    def put(name, m):
        t[:, TAT[name]:TAT[name] + m.shape[1]] = m

    tok = np.arange(T)
    f = np.float32
    axial = f(10000.0) ** (-np.arange(16, dtype=f) / f(16))
    inv2 = f(500000.0) ** (-np.arange(16, dtype=f) * f(2.0) / f(32))
    inv3 = f(500000.0) ** (-np.arange(8, dtype=f) * f(2.0) / f(16))
    for n, (cos, sin, rot) in enumerate((rotary((0, 32, 64, 96), 16, axial, (tok // 64, tok % 64) * 2),
                                         rotary((0,), 16, inv2, (tok,)),
                                         rotary((0, 64), 8, inv3, (tok, tok))), 1):
        put(f"cos{n}", cos)
        put(f"sin{n}", sin)
        put(f"rot{n}", rot)
    i = np.arange(P)
    put("ident", np.eye(P, dtype=f))
    put("ones", np.ones((P, P), f))
    put("heads", (i[:, None] // 64 == i[None, :] // 64).astype(f))
    put("before", (i[:, None] < i[None, :]).astype(f))
    put("iota", np.broadcast_to(tok.astype(f), (P, T)))
    q = i[:, None, None] + P * np.arange(2)[None, :, None]
    put("far", np.where(tok[None, None, :] > q, f(FAR), f(0)).reshape(P, 2 * T))
    w = 2 ** np.arange(1, 5)[:, None]
    put("rcount", np.broadcast_to((f(1) / np.minimum(np.arange(16)[None, :] + 1, w).astype(f)).reshape(1, 64),
                                  (P, 64)))
    return t


def token_chunks(m):
    return np.ascontiguousarray(m[0].T.reshape(C, P, T).transpose(1, 0, 2))


def kernel(**inputs):
    import concourse.bacc as _bacc
    from concourse.bass_utils import run_bass_kernel_spmd as _run

    a = {k: np.asarray(v) for k, v in inputs.items()}
    gate, up = (a[n][0].reshape(E, 2, 4, P) for n in ("b_gate", "b_up"))
    arrays = {
        "x": token_chunks(a["x"]),
        "mem": token_chunks(a["mem_2"]),
        "stream": lay_out_stream(a),
        "vecs": lay_out_vectors(a),
        "tables": lay_out_tables(),
        "moe_b": np.ascontiguousarray(np.stack([gate, up], 2).transpose(4, 0, 1, 2, 3).reshape(P, E * 16)),
        "b_down": np.ascontiguousarray(a["b_down"][0]),
        "w_router": np.ascontiguousarray(a["w_router"][0].reshape(C, P, E).transpose(1, 0, 2)),
        "b_router": np.ascontiguousarray(np.broadcast_to(a["b_router"][0], (P, E))),
    }
    nc = _bacc.Bacc("TRN2", target_bir_lowering=False, num_devices=1)
    args = [nc.dram_tensor(f"in_{n}", v.shape, mybir.dt.from_np(v.dtype), kind="ExternalInput").ap()
            for n, v in arrays.items()]
    out = nc.dram_tensor("out_y", (P, C, T), F32, kind="ExternalOutput").ap()
    build(nc, *args, out)
    r = _run(nc, [{f"in_{n}": v for n, v in arrays.items()}], core_ids=[0])
    y = r.results[0]["out_y"]
    return np.ascontiguousarray(y.transpose(1, 0, 2).reshape(D, T).T)[None]
```

```python
from contextlib import ExitStack

import numpy as np

import concourse.bass as bass
from concourse import mybir

F32 = mybir.dt.float32
I32 = mybir.dt.int32
ALU = mybir.AluOpType
ACT = mybir.ActivationFunctionType
AX = mybir.AxisListType.X

P = 128
T = 256
D = 1024
C = D // P
UNIT = 2048
RING = 12
E = 32
NARROW = 64
WIDE = 128
BLOCKS = T // WIDE
FF2 = 2816
NG = FF2 // 256
TAPS = 31
ROUNDS = 64 // 8
FAR = -3.0e38
TAKEN = -3.4e38

PLAN = [("lru_x", 2), ("q", 2), ("kv", 1), ("lru_gate", 2), ("lru_w", 1), ("w_out", 4), ("moe", 12 * E),
        ("iq", 4), ("ikiw", 1), ("dq", 2), ("dk", 2), ("dv", 2), ("u", 2), ("pool", 1), ("ab_out", 4),
        ("ck0", 4), ("cv0", 4), ("cq0", 4), ("co0", 4), ("ffn0", 3 * NG),
        ("conv_in", 8), ("conv_out", 4),
        ("ck1", 4), ("cv1", 4), ("cq1", 4), ("co1", 4), ("ffn1", 3 * NG)]
AT = {}
N_UNITS = 0
for _name, _n in PLAN:
    AT[_name] = N_UNITS
    N_UNITS += _n
assert AT["moe"] % RING == 0 and RING == 12

VECS = [("norm1", 8), ("norm2", 8), ("final", 8), ("mix0", 8), ("mix1", 8), ("cross0", 8), ("cross1", 8),
        ("mem0", 8), ("mem1", 8), ("ffn0", 8), ("ffn1", 8), ("gq", 1), ("gk", 1), ("conv_w", 16),
        ("conv_b", 4), ("lru_b", 16), ("lam", 8), ("attn_g", 4), ("lru_g", 4), ("aq", 1), ("ak", 1),
        ("pool_scale", 4), ("cin_b", 16), ("dw", 8 * TAPS), ("dw_b", 8), ("ln_g", 8), ("ln_b", 8),
        ("cqg0", 2), ("cqg1", 2), ("ckg0", 2), ("ckg1", 2), ("eps5", 1), ("eps6", 1)]
VAT = {}
NV = 0
for _name, _n in VECS:
    VAT[_name] = NV
    NV += _n

TABLES = [("cos1", T), ("sin1", T), ("cos2", T), ("sin2", T), ("cos3", T), ("sin3", T), ("rot1", P),
          ("rot2", P), ("rot3", P), ("ident", P), ("ones", P), ("heads", P), ("before", P), ("iota", T),
          ("far", 2 * T), ("rcount", 64)]
TAT = {}
NT = 0
for _name, _n in TABLES:
    TAT[_name] = NT
    NT += _n


RES = {1: 0, 4: 1, 5: 2, 6: 3, 7: 4, 8: 5}


def ffn_gate_unit(g):
    return 3 * g - 1 if g else 0


class Chain:

    def __init__(self, eng, sem, offset=0):
        self.eng, self.sem, self.offset, self.n = eng, sem, offset, 0

    def mark(self, ins):
        ins.then_inc(self.sem, 1)
        self.n += 1

    def settle(self):
        self.eng.wait_ge(self.sem, self.offset + self.n)

    def link(self, ins):
        self.mark(ins)
        self.settle()


def build(nc, x, mem, stream, vecs, tables, moe_b, b_down, w_router, b_router, out):
    with ExitStack() as ctx:
        def sb(name, shape, dt=F32):
            return ctx.enter_context(nc.sbuf_tensor(name, shape, dt))

        def sem(name):
            return ctx.enter_context(nc.semaphore(name))

        ring = sb("ring", [P, RING, UNIT])
        xT = sb("xT", [P, C, T])
        xn = sb("xn", [P, C, T])
        sq = sb("sq", [P, C, T])
        B = sb("B", [P, 12560])
        vec = sb("vec", [P, NV])
        tab = sb("tab", [P, NT])
        mbias = sb("mbias", [P, E * 16])
        wr = sb("wr", [P, C, E])
        br = sb("br", [P, E])
        tsq = sb("tsq", [P, 2, 512])
        tv = sb("tv", [P, 2, 512])
        prob = sb("prob", [P, 2, 2, T])
        pT = sb("pT", [P, 2, 2, T])
        std = sb("std", [P, 512])
        rinv = sb("rinv", [P, 512])
        small = sb("small", [P, 32])
        mx = sb("mx", [P, 2])
        rs = sb("rs", [P, 2])
        lam3 = sb("lam3", [P, 24])
        m8b = sb("m8b", [P, 2, 8])
        flag = sb("flag", [P, 1], I32)
        load = sb("load", [P, E], I32)
        PS = [ctx.enter_context(nc.psum_tensor(f"bank{i}", [P, 512], F32)) for i in range(8)]

        def V(name, i=0, n=1):
            return vec[:, VAT[name] + i:VAT[name] + i + n]

        def tb(name):
            return tab[:, TAT[name]:TAT[name] + dict(TABLES)[name]]

        def reg(a, *shape, rows=P):
            n = int(np.prod(shape))
            v = B[0:rows, a:a + n]
            if len(shape) == 2:
                return v.rearrange("p (a b) -> p a b", a=shape[0])
            if len(shape) == 3:
                return v.rearrange("p (a b c) -> p a b c", a=shape[0], b=shape[1])
            return v

        def two(bank):
            return PS[bank][:, :].rearrange("p (a t) -> p a t", a=2)

        def over(ap, n):
            return ap.unsqueeze(1).broadcast_to((P, n, ap.shape[-1]))

        def along(ap, n):
            return ap.unsqueeze(2).broadcast_to((ap.shape[0], ap.shape[1], n))

        lxp = reg(0, 4, 260)
        gtmp = reg(0, 4, T)
        xc = reg(1040, 4, T)
        lgate = reg(2064, 4, T)
        rr = reg(3088, 8, T)
        ii = reg(5136, 8, T)
        th = reg(7184, 8, T)
        qg = reg(9232, 5, T)
        at1 = reg(10512, 4, T)
        vt1 = reg(11536, 2, P)
        kz = reg(11792, 2, T)
        xtok = reg(0, 2, D)
        xs = reg(2048, C, WIDE)
        hT = [reg(3072 + 512 * w, 4, WIDE) for w in range(2)]
        gA = [reg(4096, 512), reg(10320, 512)]
        uA = [reg(4608, 512), reg(10832, 512)]
        ge = reg(5120, 512)
        ue = reg(5632, 512)
        sg = reg(6144, 512)
        yS = reg(6656, D)
        G = reg(7680, 2, E + 1)
        key = reg(7760, 2, E + 1)
        lg = reg(7840, 2, 40)
        lg2 = reg(7920, 2, 40)
        m8 = reg(8000, 2, 8)
        msk = reg(8016, 2, E)
        exr = reg(8080, 2, E)
        gs = reg(8144, 4)
        cnt = reg(8150, 2)
        GT = reg(8192, T, rows=E)
        bd = reg(8448, D, rows=E)
        sel = reg(9472, 2, WIDE)
        selg = reg(9728, 2, WIDE)
        selgT = reg(9984, T)
        key2 = reg(10240, 2, E + 1)
        iqr = reg(0, 8, T)
        iz = reg(2048, 2, T)
        iw = reg(2560, 2, 16)
        dqk = reg(2592, 8, T)
        dv = reg(4640, 2, 512)
        up = reg(5664, 4, 272)
        w1 = reg(6752, 4, 272)
        w2 = reg(7840, 4, 272)
        mix = reg(9680, 8, T)
        iqt = reg(9680, 2, T)
        rl = [reg(9680 + 512 * s, 2, T) for s in range(2)]
        sc = reg(11728, 2, T)
        pen = reg(8928, 2, T)
        memT = [reg(0, 8, T), reg(10240, 8, T)]
        memn = reg(2048, 8, T)
        ckn = reg(4096, 8, T)
        cvt = reg(6144, 2, D)
        cqn = reg(8192, 8, T)
        co = reg(10240, 8, T)
        rmem = reg(12304, T)
        fh = [reg(512 * s, 2, T) for s in range(2)]
        fs = [reg(1024 + 512 * s, 2, T) for s in range(2)]
        hp = reg(0, 8, 286)
        hc = reg(2304, 8, T)
        yc = reg(4352, 8, T)
        csg = reg(6400, 2, T)
        NDIAG = 6
        diag = reg(7000, NDIAG, P)

        landed = [sem(f"landed{s}") for s in range(RING)]
        names = """x_loaded consts_loaded router_loaded mem_loaded bd_loaded pads_ready units_done
            sq_ready stat_mm std_ready xn_ready res_ready dve_chain act_chain
            lam_exp lx_ready xc_ready qraw_ready qsq_ready vk_ready lgate_ready hstat_mm hstd_ready rot_mm
            rot_read qn_ready lru_mm lru_ev r_ready lgsq_ready ginner_ready gsig_ready m_ready mult_ready lru_ready
            score_mm nmax_ready exp_done probs_ready pT_mm pT_ready o_mm o_ready
            osq_ready ostat_mm ostd_ready mixed_ready
            rout_mm lg_ready gex_ready mask_ready cnt_mm flag_ready tok_mm tok_ready acc_mm
            gt_mm gt_ready moe_mm xmoe_ready
            iq_ready iqrot_mm iqrot_read iqn_ready iw_ready iscore_mm relu_ready relu_used
            dqk_ready dsq_ready dstat_mm dstd_ready drot_mm dqn_ready dv_ready u_ready pooled_ready pool_mix
            msq_ready mstat_mm mstd_ready memn_ready
            ck_raw cksq_ready ckstat_mm ckstd_ready ckn_ready cv_ready
            f_sig f_h conv_sig hp_ready diag_ready dwc_mm hc_pe hc_dve lnsum_mm lnd_ready lnsq_ready lnvar_mm
            lnstd_ready lnz_ready lnsig_ready yc_ready out_stored""".split()
        S = {n: sem(n) for n in names}
        moe_sem_names = """sel_ready selT_mm selT_ready xs_mm xs_ready y_mm y_ready scat_mm chain chain2 passed
            g_mm g_ready u_mm u_ready tg_mm tu_mm sig_in sig_ready h_ready
            g_mm2 g_ready2 u_mm2 u_ready2 tg_mm2 tu_mm2 sig_in2 sig_ready2 h_ready2""".split()
        M = {n: sem(f"moe_{n}") for n in moe_sem_names}
        ROUND = ("", "2")

        block = ctx.enter_context(nc.Block())

        @block.sync
        def _(sp):
            sp.dma_start(xT[:], x).then_inc(S["x_loaded"], 16)
            for dst, src in ((vec, vecs), (tab, tables)):
                sp.dma_start(dst[:], src).then_inc(S["consts_loaded"], 16)
            for s in range(RING):
                sp.dma_start(ring[:, s, :], stream[s]).then_inc(landed[s], 16)
            for dst, src in ((wr, w_router), (br, b_router), (mbias, moe_b)):
                sp.dma_start(dst[:], src).then_inc(S["router_loaded"], 16)
            turns = N_UNITS // RING
            with sp.Fori(1, turns) as i:
                for s in range(RING):
                    sp.wait_ge(S["units_done"], i * RING + (s - RING + 1))
                    sp.dma_start(ring[:, s, :], stream[i * RING + s]).then_inc(landed[s], 16)
            for u in range(turns * RING, N_UNITS):
                sp.wait_ge(S["units_done"], u - RING + 1)
                sp.dma_start(ring[:, u % RING, :], stream[u]).then_inc(landed[u % RING], 16)
            for j in range(4):
                sp.wait_ge(S["res_ready"], 4 * 6 + j + 1)
                sp.dma_start(out[:, 2 * j:2 * j + 2, :], xT[:, 2 * j:2 * j + 2, :]).then_inc(S["out_stored"], 16)
            sp.wait_ge(S["out_stored"], 64)

        @block.gpsimd
        def _(pool):
            pool.memset(lxp[:, :, 0:2], 0.0).then_inc(S["pads_ready"], 1)
            pool.memset(lxp[:, :, 258:260], 0.0).then_inc(S["pads_ready"], 1)
            pool.memset(kz[:, :, :], 0.0).then_inc(S["pads_ready"], 1)
            pool.wait_ge(S["res_ready"], 4)
            pool.dma_start(bd[:, :], b_down).then_inc(S["bd_loaded"], 16)
            pool.memset(G[:, :, E:E + 1], 0.0).then_inc(S["pads_ready"], 1)
            pool.memset(key[:, :, E:E + 1], -1.0)
            pool.memset(key2[:, :, E:E + 1], -1.0).then_inc(S["pads_ready"], 1)
            pool.memset(lg[:, :, E:E + 4], 3.0e38).then_inc(S["pads_ready"], 1)
            pool.wait_ge(S["xmoe_ready"], 4)
            pool.memset(iz[:, :, :], 0.0).then_inc(S["pads_ready"], 1)
            pool.memset(up[:, :, 0:16], 0.0).then_inc(S["pads_ready"], 1)
            pool.wait_ge(S["o_ready"], 12)
            pool.dma_start(memT[0][:, :, :], mem).then_inc(S["mem_loaded"], 16)
            pool.wait_ge(S["res_ready"], 4 * 4)
            pool.memset(hp[:, :, 0:30], 0.0).then_inc(S["pads_ready"], 1)
            pool.dma_start(memT[1][:, :, :], mem).then_inc(S["mem_loaded"], 16)

        @block.tensor
        def _(pe):
            def tile(u, t, n=P):
                return ring[:, u % RING, t * P:t * P + n]

            def await_unit(u):
                pe.wait_ge(landed[u % RING], 16 * (u // RING + 1))

            def stationary(u, dst, rhs, ready=None):
                await_unit(u)
                for m in range(2):
                    for k in range(C):
                        if ready is not None and m == 0:
                            pe.wait_ge(ready[0], ready[1] + k + 1)
                        mm = pe.matmul(dst[:, m, :], tile(u, m * C + k), rhs[:, k, :], start=(k == 0),
                                       stop=(k == C - 1))
                mm.then_inc(S["units_done"], 1)

            def stat_pair(n, j):
                pe.wait_ge(S["sq_ready"], 4 * n + j + 1)
                for c in (2 * j, 2 * j + 1):
                    mm = pe.matmul(PS[4][:, 0:T], tb("ones"), sq[:, c, :], start=(c == 0), stop=(c == C - 1))
                if j == 3:
                    mm.then_inc(S["stat_mm"], 1)

            def output_linear(first, rhs, n, ready=None):
                for j in range(4):
                    stationary(first + j, two(j), rhs, ready if j == 0 else None)
                    if j and n is not None:
                        stat_pair(n, j - 1)
                if n is not None:
                    stat_pair(n, 3)

            def heads(first, count, score, output):
                def scores(a):
                    if a - first >= 2:
                        pe.wait_ge(S["exp_done"], a - 1)
                    score(a, two(2 + a % 2)).then_inc(S["score_mm"], 1)

                def outputs(a):
                    pe.wait_ge(S["probs_ready"], a + 1)
                    if a >= 2:
                        pe.wait_ge(S["pT_ready"], a - 1)
                    bank = two(6 + a % 2)
                    for kb in range(2):
                        for b in range(2):
                            mm = pe.transpose(bank[:, kb, b * P:(b + 1) * P],
                                              prob[:, a % 2, b, kb * P:(kb + 1) * P], tb("ident"))
                    mm.then_inc(S["pT_mm"], 1)
                    pe.wait_ge(S["pT_ready"], a + 1)
                    if a >= 2:
                        pe.wait_ge(S["o_ready"], a - 1)
                    output(a, two(4 + a % 2)).then_inc(S["o_mm"], 1)

                scores(first)
                for a in range(first, first + count):
                    if a + 1 < first + count:
                        scores(a + 1)
                    outputs(a)

            pe.wait_ge(S["consts_loaded"], 32)
            for j in range(4):
                stat_pair(0, j)
            stationary(AT["lru_x"], two(0), xn, (S["xn_ready"], 0))
            stationary(AT["lru_x"] + 1, two(1), xn)
            stationary(AT["q"], two(2), xn)
            stationary(AT["q"] + 1, two(3), xn)
            u = AT["kv"]
            await_unit(u)
            for k in range(C):
                pe.matmul(PS[5][:, 0:T], tile(u, k), xn[:, k, :], start=(k == 0), stop=(k == C - 1))
            for b in range(2):
                for k in range(C):
                    mm = pe.matmul(PS[5][:, T + b * P:T + (b + 1) * P], xn[:, k, b * P:(b + 1) * P],
                                   tile(u, C + k), start=(k == 0), stop=(k == C - 1))
            mm.then_inc(S["units_done"], 1)
            for j in range(2):
                pe.wait_ge(S["lx_ready"], j + 1)
                stationary(AT["lru_gate"] + j, two(j), xn)
            for j in range(2):
                pe.wait_ge(S["qsq_ready"], j + 1)
                pe.matmul(PS[6 + j][:, :], tb("heads"), tsq[:, j, :], start=True, stop=True)\
                    .then_inc(S["hstat_mm"], 1)
                pe.wait_ge(S["qraw_ready"], j + 1)
                pe.matmul(two(2 + j), tb("rot1"), qg[:, 2 * j:2 * j + 2, :], start=True, stop=True)\
                    .then_inc(S["rot_mm"], 1)
            pe.wait_ge(S["qsq_ready"], 3)
            pe.matmul(PS[4][:, 0:T], tb("heads"), tsq[:, 0, 0:T], start=True, stop=True)\
                .then_inc(S["hstat_mm"], 1)
            pe.wait_ge(S["vk_ready"], 1)
            pe.matmul(PS[4][:, T:2 * T], tb("rot1"), qg[:, 4, :], start=True, stop=True)\
                .then_inc(S["rot_mm"], 1)
            u = AT["lru_w"]
            await_unit(u)
            pe.wait_ge(S["xc_ready"], 4)
            for n in range(8):
                if n < 2:
                    pe.wait_ge(S["lgate_ready"], n + 1)
                else:
                    pe.wait_ge(S["lru_ev"], n - 1)
                for c in range(2):
                    mm = pe.matmul(two(n % 2)[:, c, :], tile(u, 2 * n + c), xc[:, 2 * (n % 2) + c, :],
                                   start=True, stop=True)
                mm.then_inc(S["lru_mm"] if n < 7 else S["units_done"], 1)

            def score1(a, bank):
                pe.wait_ge(S["qn_ready"], 3)
                for b in range(2):
                    mm = pe.matmul(bank[:, b, :], qg[:, a % 4, b * P:(b + 1) * P], kz[:, a // 4, :],
                                   start=True, stop=True)
                return mm

            def output1(a, bank):
                for kb in range(2):
                    mm = pe.matmul(bank[:, 0, :], vt1[:, kb, :], pT[:, a % 2, kb, :], start=(kb == 0),
                                   stop=(kb == 1))
                return mm

            heads(0, 8, score1, output1)
            for g in range(2):
                pe.wait_ge(S["osq_ready"], g + 1)
                for c in range(4):
                    mm = pe.matmul(two(0)[:, g, :], tb("ones"), sq[:, 4 * g + c, :], start=(c == 0),
                                   stop=(c == 3))
                mm.then_inc(S["ostat_mm"], 1)
            pe.wait_ge(S["mixed_ready"], 8)
            output_linear(AT["w_out"], xn, 1)

            for tk in range(2):
                for k in range(C):
                    pe.wait_ge(S["xn_ready"], 8 + k + 1)
                    if tk == 0 and k == 0:
                        pe.wait_ge(S["router_loaded"], 48)
                    mm = pe.matmul(PS[5][:, tk * E:(tk + 1) * E], xn[:, k, tk * P:(tk + 1) * P], wr[:, k, :],
                                   start=(k == 0), stop=(k == C - 1))
            mm.then_inc(S["rout_mm"], 1)
            for g in range(4):
                bank = PS[6 + g % 2]
                if g >= 2:
                    pe.wait_ge(S["tok_ready"], g - 1)
                for c in range(4):
                    mm = pe.transpose(bank[:, c * P:(c + 1) * P],
                                      xn[:, 4 * (g % 2) + c, (g // 2) * P:(g // 2 + 1) * P], tb("ident"))
                mm.then_inc(S["tok_mm"], 1)
            for c in range(C):
                mm = pe.matmul(PS[c // 2][:, (c % 2) * T:(c % 2 + 1) * T], tb("ident"), xT[:, c, :],
                               start=(c % 2 == 0), stop=False, skip_group_check=True)
            pe.wait_ge(S["mask_ready"], 1)
            cp = PS[5][:, 64:64 + 3 * E].rearrange("p (a e) -> p a e", a=3)
            pe.matmul(cp[:, 0, :], tb("before"), msk[:, 0, :], start=True, stop=True)
            for g, w in ((1, "before"), (2, "ones")):
                pe.matmul(cp[:, g, :], tb("ones"), msk[:, 0, :], start=True, stop=False)
                mm = pe.matmul(cp[:, g, :], tb(w), msk[:, 1, :], start=False, stop=True)
            mm.then_inc(S["cnt_mm"], 1)
            pe.wait_ge(S["lg_ready"], 3)
            for tk in range(2):
                mm = pe.transpose(PS[4][0:E, tk * P:(tk + 1) * P], G[:, tk, 0:E], tb("ident"))
            mm.then_inc(S["gt_mm"], 1)

            def select_T(n):
                pe.wait_ge(M["sel_ready"], n + 1)
                for tk in range(2):
                    mm = pe.matmul(PS[7][:, tk * P:(tk + 1) * P], selg[:, tk, :], tb("ident"), start=True,
                                   stop=True)
                mm.then_inc(M["selT_mm"], 1)

            def gather(n):
                pe.wait_ge(M["sel_ready"], n + 1)
                for c in range(C):
                    for tk in range(2):
                        mm = pe.matmul(PS[4 + c // 4][:, (c % 4) * WIDE:(c % 4 + 1) * WIDE],
                                       xtok[:, tk, c * P:(c + 1) * P], sel[:, tk, :], start=(tk == 0),
                                       stop=(tk == 1))
                mm.then_inc(M["xs_mm"], 1)

            def await_expert_unit(e, j):
                pe.wait_ge(landed[j], e * 16 + 16 * (AT["moe"] // RING + 1))

            def turn(n, w, kind):
                pe.wait_ge(M[("g_ready", "u_ready")[kind] + ROUND[w]], n + 1)
                for c in range(4):
                    mm = pe.transpose(PS[6 + kind][:, c * P:(c + 1) * P],
                                      (gA, uA)[kind][w][:, c * P:(c + 1) * P], tb("ident"))
                mm.then_inc(M[("tg_mm", "tu_mm")[kind] + ROUND[w]], 1)

            def narrow_pass(n, e):
                mm = None
                for kind in range(2):
                    for j in range(4 * kind, 4 * kind + 4):
                        await_expert_unit(e, j)
                        for kk in range(2):
                            k = 2 * (j % 4) + kk
                            for h in range(2):
                                mm = pe.matmul(PS[4 + kind][NARROW * h:NARROW * (h + 1), :],
                                               xs[:, k, NARROW * h:NARROW * (h + 1)],
                                               ring[:, j, D * kk + 512 * h:D * kk + 512 * (h + 1)],
                                               start=(k == 0), stop=(k == C - 1))
                                if j and kk == h == 0:
                                    mm.then_inc(S["units_done"], 1)
                    mm.then_inc(M[("g_mm", "u_mm")[kind]], 1)
                turn(n, 0, 0)
                pe.wait_ge(M["selT_ready"], n + 1)
                turn(n, 0, 1)
                gather(n + 1)
                pe.wait_ge(M["h_ready"], n + 1)
                for j in range(8, 12):
                    await_expert_unit(e, j)
                    for kk in range(2):
                        f = 2 * (j - 8) + kk
                        for h in range(2):
                            mm = pe.matmul(PS[6][NARROW * h:NARROW * (h + 1), :],
                                           hT[0][:, f % 4, NARROW * (f // 4):NARROW * (f // 4 + 1)],
                                           ring[:, j, D * kk + 512 * h:D * kk + 512 * (h + 1)],
                                           start=(f == 0), stop=(f == C - 1))
                            if kk == h == 0:
                                mm.then_inc(S["units_done"], 1)
                mm.then_inc(M["y_mm"], 1)
                pe.wait_ge(M["y_ready"], n + 1)
                for c in (0, 4, 1, 5, 2, 6, 3, 7):
                    rows = slice(NARROW * (c // 4), NARROW * (c // 4 + 1))
                    mm = pe.matmul(PS[c // 2][:, (c % 2) * T:(c % 2 + 1) * T],
                                   yS[rows, (c % 4) * P:(c % 4 + 1) * P], selgT[rows, :], start=False,
                                   stop=False, skip_group_check=True)
                    if c == 0:
                        mm.then_inc(S["units_done"], 1)
                mm.then_inc(M["scat_mm"], 1)
                select_T(n + 1)
                for name in ("g_mm2", "u_mm2", "tg_mm2", "tu_mm2"):
                    pe.sem_inc(M[name], 1)

            def wide_pass(n, e, frees):
                mm = None
                for w in range(2):
                    for kind in range(2):
                        if w:
                            pe.wait_ge(M[("g_ready", "u_ready")[kind]], n + 1)
                        for j in range(4 * kind, 4 * kind + 4):
                            if w == 0:
                                await_expert_unit(e, j)
                            for kk in range(2):
                                k = 2 * (j % 4) + kk
                                mm = pe.matmul(PS[4 + kind][:, :], xs[:, k, :],
                                               ring[:, j, D * kk + 512 * w:D * kk + 512 * (w + 1)],
                                               start=(k == 0), stop=(k == C - 1))
                                if frees and w and j and kk == 0:
                                    mm.then_inc(S["units_done"], 1)
                        mm.then_inc(M[("g_mm", "u_mm")[kind] + ROUND[w]], 1)
                    if w:
                        pe.wait_ge(M["h_ready"], n + 1)
                    turn(n, w, 0)
                    if w == 0:
                        pe.wait_ge(M["selT_ready"], n + 1)
                    turn(n, w, 1)
                gather(n + 1)
                pe.wait_ge(M["h_ready2"], n + 1)
                for j in range(8, 12):
                    await_expert_unit(e, j)
                    for kk in range(2):
                        f = 2 * (j - 8) + kk
                        for h in range(2):
                            mm = pe.matmul(PS[6 + h][:, :], hT[f // 4][:, f % 4, :],
                                           ring[:, j, D * kk + 512 * h:D * kk + 512 * (h + 1)],
                                           start=(f == 0), stop=(f == C - 1))
                            if frees and kk == h == 0:
                                mm.then_inc(S["units_done"], 1)
                mm.then_inc(M["y_mm"], 1)
                pe.wait_ge(M["y_ready"], n + 1)
                for c in range(C):
                    mm = pe.matmul(PS[c // 2][:, (c % 2) * T:(c % 2 + 1) * T], yS[:, c * P:(c + 1) * P],
                                   selgT[:, :], start=False, stop=False, skip_group_check=True)
                    if frees and c == 0:
                        mm.then_inc(S["units_done"], 1)
                mm.then_inc(M["scat_mm"], 1)
                select_T(n + 1)

            def tokens_of(e):
                return pe.value_load(load[0:1, bass.ds(e, 1)], min_val=0, max_val=T)

            pe.wait_ge(S["flag_ready"], 1)
            pe.wait_ge(S["tok_ready"], 4)
            pe.wait_ge(S["gt_ready"], 1)
            most = pe.value_load(flag[0:1, 0:1], min_val=0, max_val=T)
            select_T(0)
            gather(0)
            with pe.If(most < WIDE + 1):
                with pe.Fori(0, E) as e:
                    pe.wait_ge(M["xs_ready"], e + 1)
                    with pe.If(tokens_of(e) < NARROW + 1):
                        narrow_pass(e, e)
                    with pe.Else():
                        wide_pass(e, e, True)
                    pe.nop()
            with pe.Else():
                with pe.Fori(0, E) as e:
                    for b in range(BLOCKS):
                        pe.wait_ge(M["xs_ready"], e * BLOCKS + b + 1)
                        wide_pass(e * BLOCKS + b, e, b == BLOCKS - 1)
            pe.wait_ge(S["bd_loaded"], 16)
            for c in range(C):
                mm = pe.matmul(PS[c // 2][:, (c % 2) * T:(c % 2 + 1) * T], bd[:, c * P:(c + 1) * P], GT[:, :],
                               start=False, stop=True, skip_group_check=True)
                if c % 2:
                    mm.then_inc(S["moe_mm"], 1)

            for n in (2, 3):
                for j in range(4):
                    stat_pair(n, j)

            for j in range(4):
                stationary(AT["iq"] + j, two(j), xn, (S["xn_ready"], 24) if j == 0 else None)
            u = AT["ikiw"]
            await_unit(u)
            for k in range(C):
                pe.matmul(PS[5][:, 0:T], tile(u, k), xn[:, k, :], start=(k == 0), stop=(k == C - 1))
            for b in range(2):
                for k in range(C):
                    mm = pe.matmul(PS[5][:, T + 16 * b:T + 16 * b + 16], xn[:, k, b * P:(b + 1) * P],
                                   ring[:, u % RING, C * P + 16 * k:C * P + 16 * k + 16],
                                   start=(k == 0), stop=(k == C - 1))
            mm.then_inc(S["units_done"], 1)
            for j in range(5):
                pe.wait_ge(S["iq_ready"], j + 1)
                if j >= 2:
                    pe.wait_ge(S["iqrot_read"], j - 1)
                if j < 4:
                    pe.matmul(two(6 + j % 2), tb("rot3"), iqr[:, 2 * j:2 * j + 2, :], start=True, stop=True)\
                        .then_inc(S["iqrot_mm"], 1)
                else:
                    pe.matmul(PS[6][:, 0:T], tb("rot3"), tv[:, 0, 0:T], start=True, stop=True)\
                        .then_inc(S["iqrot_mm"], 1)
            def index_scores(h):
                pe.wait_ge(S["iqn_ready"], 5)
                if h >= 2:
                    pe.wait_ge(S["relu_ready"], h - 1)
                for b in range(2):
                    mm = pe.matmul(two(h % 2)[:, b, :], iqr[:, h // 2, b * P:(b + 1) * P], iz[:, h % 2, :],
                                   start=True, stop=True)
                mm.then_inc(S["iscore_mm"], 1)

            for j in range(4):
                if j >= 2:
                    pe.wait_ge(S["dqk_ready"], j - 1)
                stationary((AT["dq"] + j), two(2 + j % 2), xn)
                for h in range(4 * j, 4 * j + 4):
                    index_scores(h)
                pe.wait_ge(S["dsq_ready"], j + 1)
                if j:
                    pe.wait_ge(S["dqn_ready"], j)
                pe.matmul(PS[4][:, :], tb("ones"), tsq[:, j % 2, :], start=True, stop=True)\
                    .then_inc(S["dstat_mm"], 1)
                pe.wait_ge(S["dqk_ready"], j + 1)
                pe.matmul(two(5), tb("rot2"), dqk[:, 2 * j:2 * j + 2, :], start=True, stop=True)\
                    .then_inc(S["drot_mm"], 1)
            for w in range(2):
                u = AT["dv"] + w
                await_unit(u)
                for kk in range(4):
                    for b in range(2):
                        k = 4 * w + kk
                        mm = pe.matmul(PS[6 + b][:, :], xn[:, k, b * P:(b + 1) * P],
                                       ring[:, u % RING, 512 * kk:512 * kk + 512],
                                       start=(k == 0), stop=(k == C - 1))
                mm.then_inc(S["units_done"], 1)
            pe.wait_ge(S["relu_ready"], 16)
            for j in range(2):
                stationary(AT["u"] + j, two(j), xn)
            u = AT["pool"]
            await_unit(u)
            pe.wait_ge(S["pooled_ready"], 4)
            for g in range(4):
                mm = pe.matmul(two(g // 2)[:, g % 2, :], tile(u, g), w1[:, g, 0:T], start=True, stop=True)
            mm.then_inc(S["units_done"], 1)

            def score2(a, bank):
                pe.wait_ge(S["dqn_ready"], 4)
                h = a - 8
                for b in range(2):
                    mm = pe.matmul(bank[:, b, :], dqk[:, h, b * P:(b + 1) * P], dqk[:, 4 + h, :],
                                   start=True, stop=True)
                return mm

            def output2(a, bank):
                h = a - 8
                for kb in range(2):
                    mm = pe.matmul(bank[:, 0, :], dv[:, kb, h * P:(h + 1) * P], pT[:, a % 2, kb, :],
                                   start=(kb == 0), stop=(kb == 1))
                return mm

            pe.wait_ge(S["dv_ready"], 2)
            heads(8, 4, score2, output2)
            pe.wait_ge(S["pool_mix"], 4)
            pe.wait_ge(S["o_ready"], 12)
            output_linear(AT["ab_out"], mix, 4)

            def cross(l):
                ck, cv, cq, c_o = (AT[f"{x}{l}"] for x in ("ck", "cv", "cq", "co"))
                if l == 0:
                    for j in range(4):
                        pe.wait_ge(S["msq_ready"], j + 1)
                        for c in (2 * j, 2 * j + 1):
                            mm = pe.matmul(PS[5][:, 0:T], tb("ones"), sq[:, c, :], start=(c == 0),
                                           stop=(c == C - 1))
                    mm.then_inc(S["mstat_mm"], 1)
                for side, first, rhs, ready in ((0, ck, memn, (S["memn_ready"], 8 * l)),
                                                (1, cq, xn, (S["xn_ready"], 8 * (4 + 3 * l)))):
                    base = 8 * l + 4 * side
                    for j in range(4):
                        if j >= 2 or side:
                            pe.wait_ge(S["ck_raw"], base + j - 1 if j >= 2 else base)
                        stationary(first + j, two(2 + j % 2), rhs, ready if j == 0 else None)
                        if j:
                            head_sum(base + j - 1)
                    head_sum(base + 3)
                    if side == 0:
                        for w in range(4):
                            u = cv + w
                            await_unit(u)
                            for kk in range(2):
                                k = 2 * w + kk
                                for b in range(2):
                                    for hf in range(2):
                                        bank = (0, 1, 6, 7)[2 * b + hf]
                                        mm = pe.matmul(PS[bank][:, :], memn[:, k, b * P:(b + 1) * P],
                                                       ring[:, u % RING,
                                                            D * kk + 512 * hf:D * kk + 512 * hf + 512],
                                                       start=(k == 0), stop=(k == C - 1))
                            mm.then_inc(S["units_done"], 1)

                def score(a, bank):
                    h = (a - 12) % 4
                    pe.wait_ge(S["ckn_ready"], 8 * l + 8)
                    for b in range(2):
                        for c in range(2):
                            mm = pe.matmul(bank[:, b, :], cqn[:, 2 * h + c, b * P:(b + 1) * P],
                                           ckn[:, 2 * h + c, :], start=(c == 0), stop=(c == 1))
                    return mm

                def output(a, bank):
                    h = (a - 12) % 4
                    for c in range(2):
                        for kb in range(2):
                            mm = pe.matmul(bank[:, c, :], cvt[:, kb, 256 * h + c * P:256 * h + (c + 1) * P],
                                           pT[:, a % 2, kb, :], start=(kb == 0), stop=(kb == 1))
                    return mm

                pe.wait_ge(S["cv_ready"], 4 * (l + 1))
                heads(12 + 4 * l, 4, score, output)
                pe.wait_ge(S["o_ready"], 16 + 4 * l)
                output_linear(c_o, co, 5 + 3 * l)

            def head_sum(p):
                pe.wait_ge(S["cksq_ready"], p + 1)
                if p:
                    pe.wait_ge(S["ckstd_ready"], p)
                for c in range(2):
                    mm = pe.matmul(PS[5][:, T:2 * T], tb("ones"), tsq[:, p % 2, c * T:(c + 1) * T],
                                   start=(c == 0), stop=(c == 1))
                mm.then_inc(S["ckstat_mm"], 1)

            def ffn(l):
                first, n = AT[f"ffn{l}"], 8 * (5 + 3 * l)
                at = [first]
                for g in range(NG):
                    for kind in range(2):
                        bank = 4 + 2 * (g % 2) + kind
                        if g >= 2:
                            pe.wait_ge(S["f_h"], NG * l + g - 1)
                        stationary(at[0], two(bank), xn, (S["xn_ready"], n) if g == kind == 0 else None)
                        at[0] += 1
                    if g:
                        down(l, g - 1, at)
                down(l, NG - 1, at)
                if l == 0:
                    for j in range(4):
                        stat_pair(6, j)

            def down(l, g, at):
                u = at[0]
                at[0] += 1
                await_unit(u)
                pe.wait_ge(S["f_h"], NG * l + g + 1)
                for m in range(C):
                    for kk in range(2):
                        mm = pe.matmul(PS[m // 2][:, (m % 2) * T:(m % 2 + 1) * T], tile(u, kk * C + m),
                                       fh[g % 2][:, kk, :], start=(g == 0 and kk == 0 and m % 2 == 0),
                                       stop=(g == NG - 1 and kk == 1), skip_group_check=True)
                mm.then_inc(S["units_done"], 1)

            cross(0)
            ffn(0)
            for j in range(8):
                if j >= 4:
                    pe.wait_ge(S["hp_ready"], j - 3)
                stationary(AT["conv_in"] + j, two(j % 4), xn, (S["xn_ready"], 48) if j == 0 else None)
            for c in range(4):
                pe.wait_ge(S["hp_ready"], c + 1)
                for t in range(TAPS):
                    pe.wait_ge(S["diag_ready"], c * TAPS + t + 1)
                    pe.matmul(PS[4 + c][:, 0:T], diag[:, (c * TAPS + t) % NDIAG, :],
                              hp[:, c, t:t + T], start=(t == 0), stop=(t == TAPS - 1))\
                        .then_inc(S["dwc_mm"], 1)
            for c in range(C):
                if c < 4:
                    pe.wait_ge(S["hc_pe"], c + 1)
                else:
                    pe.wait_ge(S["hc_dve"], c - 3)
                mm = pe.matmul(PS[0][:, 0:T], tb("ones"), hc[:, c, :], start=(c == 0), stop=(c == C - 1))
            mm.then_inc(S["lnsum_mm"], 1)
            for j in range(4):
                pe.wait_ge(S["lnsq_ready"], j + 1)
                for c in (2 * j, 2 * j + 1):
                    mm = pe.matmul(PS[1][:, 0:T], tb("ones"), sq[:, c, :], start=(c == 0), stop=(c == C - 1))
            mm.then_inc(S["lnvar_mm"], 1)
            output_linear(AT["conv_out"], yc, 7, (S["yc_ready"], 0))
            cross(1)
            ffn(1)
            assert AT["ffn1"] + 3 * NG == N_UNITS

        @block.scalar
        def _(act):
            chain = Chain(act, S["act_chain"])

            def f(out_, in_, fn, **kw):
                return act.activation(out_, in_, fn, **kw)

            def squares(n, j, sem_=None, value=None, src=None):
                if n == 0:
                    act.wait_ge(S["x_loaded"], 16)
                elif n == 3:
                    act.wait_ge(S["xn_ready"], 16 + 2 * j + 2)
                elif n == 2:
                    act.wait_ge(S["xmoe_ready"], j + 1)
                else:
                    act.wait_ge(S["res_ready"], 4 * RES[n] + j + 1)
                f(sq[:, 2 * j:2 * j + 2, :], xT[:, 2 * j:2 * j + 2, :], ACT.Square).then_inc(S["sq_ready"], 1)

            def deviation(n, eps):
                act.wait_ge(S["stat_mm"], n + 1)
                f(std[:, 0:T], PS[4][:, 0:T], ACT.Sqrt, scale=1.0 / D, bias=V(eps)).then_inc(S["std_ready"], 1)

            def norm(n, eps="eps6"):
                for j in range(4):
                    squares(n, j)
                deviation(n, eps)

            def heads(first, count, scale, src, evacuate):
                def exps(a):
                    act.wait_ge(S["nmax_ready"], a + 1)
                    if a >= 2:
                        act.wait_ge(S["pT_mm"], a - 1)
                        act.wait_ge(S["probs_ready"], a - 1)
                    for b in range(2):
                        e_ = f(prob[:, a % 2, b, :], src(a)[:, b, :], ACT.Exp, scale=scale,
                               bias=small[:, 2 * (a % 2) + b:2 * (a % 2) + b + 1],
                               accum_out=small[:, 4 + 2 * (a % 2) + b:5 + 2 * (a % 2) + b])
                    e_.then_inc(S["exp_done"], 1)

                exps(first)
                for a in range(first, first + count):
                    if a + 1 < first + count:
                        exps(a + 1)
                    act.wait_ge(S["pT_mm"], a + 1)
                    if a >= 2:
                        act.wait_ge(S["o_mm"], a - 1)
                    f(pT[:, a % 2, :, :], two(6 + a % 2), ACT.Copy).then_inc(S["pT_ready"], 1)
                    act.wait_ge(S["o_mm"], a + 1)
                    evacuate(a, two(4 + a % 2)).then_inc(S["o_ready"], 1)

            act.wait_ge(S["consts_loaded"], 32)
            norm(0, "eps5")
            act.wait_ge(S["pads_ready"], 3)
            act.wait_ge(S["lam_exp"], 1)
            chain.mark(f(small[:, 16:24], small[:, 16:24], ACT.Exp))
            for j in range(2):
                act.wait_ge(S["units_done"], j + 1)
                f(lxp[:, 2 * j:2 * j + 2, 2:2 + T], two(j), ACT.Copy).then_inc(S["lx_ready"], 1)
            for j in range(2):
                act.wait_ge(S["units_done"], AT["q"] + j + 1)
                f(tsq[:, j, :], PS[2 + j][:, :], ACT.Square).then_inc(S["qsq_ready"], 1)
                f(qg[:, 2 * j:2 * j + 2, :], two(2 + j), ACT.Identity, scale=V("gq"))\
                    .then_inc(S["qraw_ready"], 1)
            act.wait_ge(S["units_done"], AT["kv"] + 1)
            act.wait_ge(S["hstat_mm"], 1)
            f(tsq[:, 0, 0:T], PS[5][:, 0:T], ACT.Square).then_inc(S["qsq_ready"], 1)
            f(vt1[:, :, :], PS[5][:, T:2 * T].rearrange("p (a b) -> p a b", a=2), ACT.Copy)
            f(qg[:, 4, :], PS[5][:, 0:T], ACT.Identity, scale=V("gk")).then_inc(S["vk_ready"], 1)
            for j in range(2):
                act.wait_ge(S["units_done"], AT["lru_gate"] + j + 1)
                f(lgate[:, 2 * j:2 * j + 2, :], two(j), ACT.Copy).then_inc(S["lgate_ready"], 1)
            act.wait_ge(S["rot_mm"], 3)
            f(std[:, 0:T], PS[4][:, 0:T], ACT.Sqrt, scale=1.0 / 64, bias=V("eps6")).then_inc(S["hstd_ready"], 1)
            for j in range(2):
                act.wait_ge(S["qn_ready"], j + 1)
                f(std[:, :], PS[6 + j][:, :], ACT.Sqrt, scale=1.0 / 64, bias=V("eps6"))\
                    .then_inc(S["hstd_ready"], 1)
            for n in range(8):
                d, kind, j = n // 4, (n // 2) % 2, n % 2
                if n < 7:
                    act.wait_ge(S["lru_mm"], n + 1)
                else:
                    act.wait_ge(S["units_done"], AT["lru_w"] + 1)
                for c in range(2):
                    ch = 2 * j + c
                    last = f((ii if kind else rr)[:, 4 * d + ch, :], two(n % 2)[:, c, :], ACT.Sigmoid,
                             bias=V("lru_b", 8 * kind + 4 * d + ch))
                last.then_inc(S["lru_ev"], 1)
            act.wait_ge(S["r_ready"], 1)
            act.wait_ge(S["lru_ev"], 8)
            for n in range(8):
                f(th[:, n, :], rr[:, n, :], ACT.Tanh, scale=small[:, 24 + n:25 + n])
            chain.mark(f(gtmp[:, :, :], lgate[:, :, :], ACT.Square))
            chain.settle()
            for n in range(8):
                last = f(rr[:, n, :], rr[:, n, :], ACT.Exp, scale=small[:, 8 + n:9 + n])
            last.then_inc(S["lgsq_ready"], 1)
            act.wait_ge(S["m_ready"], 1)
            f(th[:, :, :], th[:, :, :], ACT.Sqrt).then_inc(S["mult_ready"], 1)
            act.wait_ge(S["ginner_ready"], 1)
            f(gtmp[:, :, :], gtmp[:, :, :], ACT.Sigmoid, scale=2.0 * float(np.sqrt(2.0 / np.pi)))\
                .then_inc(S["gsig_ready"], 1)
            heads(0, 8, 0.125, lambda a: two(2 + a % 2),
                  lambda a, bank: f(at1[64 * (a // 4):64 * (a // 4) + 64, a % 4, :],
                                    bank[64 * (a // 4):64 * (a // 4) + 64, 0, :], ACT.Copy))
            act.wait_ge(S["o_ready"], 8)
            f(sq[:, 0:4, :], at1[:, :, :], ACT.Square).then_inc(S["osq_ready"], 1)
            act.wait_ge(S["lru_ready"], 1)
            f(sq[:, 4:8, :], xc[:, :, :], ACT.Square).then_inc(S["osq_ready"], 1)
            act.wait_ge(S["ostat_mm"], 2)
            f(std[:, :], PS[0][:, :], ACT.Sqrt, scale=1.0 / 512, bias=V("eps5")).then_inc(S["ostd_ready"], 1)
            norm(1, "eps5")

            for g in range(4):
                act.wait_ge(S["tok_mm"], g + 1)
                f(xtok[:, g // 2, 512 * (g % 2):512 * (g % 2) + 512], PS[6 + g % 2][:, :], ACT.Copy)\
                    .then_inc(S["tok_ready"], 1)
            act.wait_ge(S["lg_ready"], 2)
            for tk in range(2):
                last = f(exr[:, tk, :], lg[:, tk, 0:E], ACT.Exp, bias=gs[:, tk:tk + 1])
            last.then_inc(S["gex_ready"], 1)
            act.wait_ge(S["gt_mm"], 1)
            f(GT[:, :], PS[4][0:E, 0:T], ACT.Copy).then_inc(S["gt_ready"], 1)

            def copy_xs(n):
                act.wait_ge(M["xs_mm"], n + 1)
                for i in range(2):
                    last = f(xs[:, 4 * i:4 * i + 4, :], PS[4 + i][:, :].rearrange("p (c n) -> p c n", c=4),
                             ACT.Copy)
                last.then_inc(M["xs_ready"], 1)

            def selected(n):
                act.wait_ge(M["selT_mm"], n + 1)
                f(selgT, PS[7][:, 0:T], ACT.Copy).then_inc(M["selT_ready"], 1)

            def halves(n, w):
                r_ = ROUND[w]
                for kind in range(2):
                    name, dst = (("g", gA), ("u", uA))[kind]
                    act.wait_ge(M[f"{name}_mm{r_}"], n + 1)
                    f(dst[w], PS[4 + kind][:, :], ACT.Copy).then_inc(M[f"{name}_ready{r_}"], 1)
                act.wait_ge(M["sig_in" + r_], n + 1)
                f(sg, ge, ACT.Sigmoid, scale=1.702).then_inc(M["sig_ready" + r_], 1)

            def act_pass(n, wide):
                selected(n)
                halves(n, 0)
                if wide:
                    halves(n, 1)
                copy_xs(n + 1)
                act.wait_ge(M["y_mm"], n + 1)
                if wide:
                    f(yS[:, 0:512], PS[6][:, :], ACT.Copy)
                    f(yS[:, 512:D], PS[7][:, :], ACT.Copy).then_inc(M["y_ready"], 1)
                else:
                    f(yS[:, 0:512], PS[6][:, :], ACT.Copy).then_inc(M["y_ready"], 1)
                    for name in ("g_ready2", "u_ready2", "sig_ready2"):
                        act.sem_inc(M[name], 1)

            act.wait_ge(S["flag_ready"], 1)
            most = act.value_load(flag[0:1, 0:1], min_val=0, max_val=T)
            copy_xs(0)
            with act.If(most < WIDE + 1):
                with act.Fori(0, E) as e:
                    with act.If(act.value_load(load[0:1, bass.ds(e, 1)], min_val=0, max_val=T) < NARROW + 1):
                        act_pass(e, False)
                    with act.Else():
                        act_pass(e, True)
                    act.nop()
            with act.Else():
                with act.Fori(0, E) as e:
                    for b in range(BLOCKS):
                        act_pass(e * BLOCKS + b, True)
            for j in range(4):
                act.wait_ge(S["moe_mm"], j + 1)
                f(xT[:, 2 * j:2 * j + 2, :], two(j), ACT.Copy).then_inc(S["xmoe_ready"], 1)
            norm(2, "eps5")
            norm(3)

            act.wait_ge(S["pads_ready"], 8)
            for j in range(4):
                act.wait_ge(S["units_done"], AT["iq"] + j + 1)
                f(iqr[:, 2 * j:2 * j + 2, :], two(j), ACT.Copy).then_inc(S["iq_ready"], 1)
            act.wait_ge(S["units_done"], AT["ikiw"] + 1)
            f(tv[:, 0, 0:T], PS[5][:, 0:T], ACT.Copy).then_inc(S["iq_ready"], 1)
            f(iw[:, :, :], PS[5][:, T:T + 32].rearrange("p (a b) -> p a b", a=2), ACT.Copy, scale=1.0 / 32)\
                .then_inc(S["iw_ready"], 1)
            def relu(h):
                act.wait_ge(S["iscore_mm"], h + 1)
                if h >= 2:
                    act.wait_ge(S["relu_used"], h - 1)
                f(rl[h % 2][:, :, :], two(h % 2), ACT.Relu).then_inc(S["relu_ready"], 1)

            for j in range(4):
                act.wait_ge(S["units_done"], AT["dq"] + j + 1)
                if j >= 2:
                    act.wait_ge(S["dstat_mm"], j - 1)
                if j == 0:
                    act.wait_ge(S["iqn_ready"], 4)
                f(tsq[:, j % 2, :], PS[2 + j % 2][:, :], ACT.Square).then_inc(S["dsq_ready"], 1)
                f(dqk[:, 2 * j:2 * j + 2, :], two(2 + j % 2), ACT.Identity, scale=V("aq" if j < 2 else "ak"))\
                    .then_inc(S["dqk_ready"], 1)
                for h in range(4 * j, 4 * j + 4):
                    relu(h)
                act.wait_ge(S["dstat_mm"], j + 1)
                if j:
                    act.wait_ge(S["dqn_ready"], j)
                f(std[:, :], PS[4][:, :], ACT.Sqrt, scale=1.0 / P, bias=V("eps6")).then_inc(S["dstd_ready"], 1)
            act.wait_ge(S["units_done"], AT["dv"] + 2)
            for b in range(2):
                f(dv[:, b, :], PS[6 + b][:, :], ACT.Copy).then_inc(S["dv_ready"], 1)
            for j in range(2):
                act.wait_ge(S["units_done"], AT["u"] + j + 1)
                f(up[:, 2 * j:2 * j + 2, 16:272], two(j), ACT.Copy).then_inc(S["u_ready"], 1)
            act.wait_ge(S["relu_used"], 16)
            act.wait_ge(S["units_done"], AT["pool"] + 1)
            for g in range(4):
                f(mix[:, 4 + g, :], two(g // 2)[:, g % 2, :], ACT.Identity, scale=V("pool_scale", g))\
                    .then_inc(S["pool_mix"], 1)
            heads(8, 4, 1.0, lambda a: tv[:, a % 2, :].rearrange("p (b t) -> p b t", b=2),
                  lambda a, bank: f(mix[:, a - 8, :], bank[:, 0, :], ACT.Copy))

            def cross(l):
                if l == 0:
                    act.wait_ge(S["stat_mm"], 5)
                    act.wait_ge(S["mem_loaded"], 16)
                    for j in range(4):
                        f(sq[:, 2 * j:2 * j + 2, :], memT[0][:, 2 * j:2 * j + 2, :], ACT.Square)\
                            .then_inc(S["msq_ready"], 1)
                    act.wait_ge(S["mstat_mm"], 1)
                    f(rmem, PS[5][:, 0:T], ACT.Sqrt, scale=1.0 / D, bias=V("eps6")).then_inc(S["mstd_ready"], 1)
                for side, name, first, dst in ((0, "ckg", AT[f"ck{l}"], ckn), (1, "cqg", AT[f"cq{l}"], cqn)):
                    for j in range(4):
                        p = 8 * l + 4 * side + j
                        act.wait_ge(S["units_done"], first + j + 1)
                        if p >= 2:
                            act.wait_ge(S["ckstat_mm"], p - 1)
                        f(tsq[:, p % 2, :], PS[2 + j % 2][:, :], ACT.Square).then_inc(S["cksq_ready"], 1)
                        for c in range(2):
                            last = f(dst[:, 2 * j + c, :], two(2 + j % 2)[:, c, :], ACT.Identity,
                                     scale=V(f"{name}{l}", c))
                        last.then_inc(S["ck_raw"], 1)
                        act.wait_ge(S["ckstat_mm"], p + 1)
                        if p:
                            act.wait_ge(S["ckn_ready"], p)
                        f(std[:, T:2 * T], PS[5][:, T:2 * T], ACT.Sqrt, scale=1.0 / T, bias=V("eps6"))\
                            .then_inc(S["ckstd_ready"], 1)
                    if side == 0:
                        act.wait_ge(S["units_done"], AT[f"cv{l}"] + 4)
                        for b in range(2):
                            for hf in range(2):
                                f(cvt[:, b, 512 * hf:512 * hf + 512], PS[(0, 1, 6, 7)[2 * b + hf]][:, :],
                                  ACT.Copy).then_inc(S["cv_ready"], 1)
                heads(12 + 4 * l, 4, 1.0 / 16, lambda a: two(2 + a % 2),
                      lambda a, bank: f(co[:, 2 * ((a - 12) % 4):2 * ((a - 12) % 4) + 2, :], bank, ACT.Copy))

            def ffn(l):
                for g in range(NG):
                    act.wait_ge(S["units_done"], AT[f"ffn{l}"] + ffn_gate_unit(g) + 1)
                    f(fs[g % 2][:, :, :], two(4 + 2 * (g % 2)), ACT.Sigmoid).then_inc(S["f_sig"], 1)

            norm(4)
            cross(0)
            norm(5)
            ffn(0)
            norm(6)
            for j in range(8):
                act.wait_ge(S["units_done"], AT["conv_in"] + j + 1)
                if j >= 2:
                    act.wait_ge(S["hp_ready"], j - 1)
                f(csg[:, j % 2, :], two(j % 4)[:, 1, :], ACT.Sigmoid, bias=V("cin_b", 8 + j))\
                    .then_inc(S["conv_sig"], 1)
            for c in range(4):
                for t in range(TAPS):
                    n = c * TAPS + t
                    if n >= NDIAG:
                        act.wait_ge(S["dwc_mm"], n - NDIAG + 1)
                    f(diag[:, n % NDIAG, :], tb("ident"), ACT.Copy, scale=V("dw", n))\
                        .then_inc(S["diag_ready"], 1)
                act.wait_ge(S["dwc_mm"], (c + 1) * TAPS)
                f(hc[:, c, :], PS[4 + c][:, 0:T], ACT.Identity, bias=V("dw_b", c))\
                    .then_inc(S["hc_pe"], 1)
            for j in range(4):
                act.wait_ge(S["lnd_ready"], j + 1)
                f(sq[:, 2 * j:2 * j + 2, :], hc[:, 2 * j:2 * j + 2, :], ACT.Square).then_inc(S["lnsq_ready"], 1)
            act.wait_ge(S["lnvar_mm"], 1)
            f(std[:, 0:T], PS[1][:, 0:T], ACT.Sqrt, scale=1.0 / D, bias=V("eps6")).then_inc(S["lnstd_ready"], 1)
            for c in range(C):
                act.wait_ge(S["lnz_ready"], c + 1)
                f(sq[:, c, :], hc[:, c, :], ACT.Sigmoid, bias=V("ln_b", c)).then_inc(S["lnsig_ready"], 1)
            norm(7)
            cross(1)
            norm(8)
            ffn(1)

        @block.vector
        def _(dve):
            chain = Chain(dve, S["dve_chain"])
            link, mark, settle = chain.link, chain.mark, chain.settle
            tt, ts, stt = dve.tensor_tensor, dve.tensor_scalar, dve.scalar_tensor_tensor

            def norm(n, gain, dst):
                dve.wait_ge(S["std_ready"], n + 1)
                link(dve.reciprocal(rinv[:, 0:T], std[:, 0:T]))
                for k in range(C):
                    stt(dst[:, k, :], xT[:, k, :], V(gain, k), rinv[:, 0:T], ALU.mult, ALU.mult)\
                        .then_inc(S["xn_ready"], 1)

            def residual(first):
                for j in range(4):
                    dve.wait_ge(S["units_done"], first + j + 1)
                    tt(xT[:, 2 * j:2 * j + 2, :], two(j), xT[:, 2 * j:2 * j + 2, :], ALU.add)\
                        .then_inc(S["res_ready"], 1)

            def heads(first, count, scale, between=None, sparse=False):
                def maxima(a):
                    dve.wait_ge(S["score_mm"], a + 1)
                    bank = two(2 + a % 2)
                    if a - first >= 2:
                        dve.wait_ge(S["exp_done"], a - 1)
                    if a:
                        dve.wait_ge(S["nmax_ready"], a)
                    if sparse:
                        src = tv[:, a % 2, :].rearrange("p (b t) -> p b t", b=2)
                        link(stt(src, bank, scale, pen[:, :, :], ALU.mult, ALU.add))
                        bank = src
                    link(dve.tensor_reduce(mx[:, :], bank, AX, ALU.max))
                    ts(small[:, 2 * (a % 2):2 * (a % 2) + 2], mx[:, :], -1.0 if sparse else -scale, None, ALU.mult)\
                        .then_inc(S["nmax_ready"], 1)

                def divide(a):
                    dve.wait_ge(S["exp_done"], a + 1)
                    if a:
                        dve.wait_ge(S["probs_ready"], a)
                    o = 4 + 2 * (a % 2)
                    link(dve.reciprocal(rs[:, :], small[:, o:o + 2]))
                    tt(prob[:, a % 2, :, :], prob[:, a % 2, :, :], along(rs[:, :], T), ALU.mult)\
                        .then_inc(S["probs_ready"], 1)

                maxima(first)
                for a in range(first, first + count):
                    if a + 1 < first + count:
                        maxima(a + 1)
                    divide(a)
                    if between:
                        between(a)

            dve.wait_ge(S["consts_loaded"], 32)
            ea, rate_n, rate_p = small[:, 16:24], small[:, 8:16], small[:, 24:32]
            link(ts(rate_n, V("lam", 0, 8), -1.0, None, ALU.mult))
            ts(ea, V("lam", 0, 8), 0.0, None, ALU.max)
            link(ts(rate_p, rate_n, 0.0, None, ALU.max))
            link(tt(ea, ea, rate_p, ALU.add))
            ts(ea, ea, -1.0, None, ALU.mult).then_inc(S["lam_exp"], 1)
            norm(0, "norm1", xn)
            dve.wait_ge(S["act_chain"], 1)
            z, z2, ser = lam3[:, 0:8], lam3[:, 8:16], lam3[:, 16:24]
            link(ts(z, ea, 2.0, None, ALU.add))
            link(dve.reciprocal(z, z))
            link(tt(z, z, ea, ALU.mult))
            link(tt(z2, z, z, ALU.mult))
            link(ts(ser, z2, 1.0 / 19, 1.0 / 17, ALU.mult, ALU.add))
            for k in range(15, 0, -2):
                link(tt(ser, ser, z2, ALU.mult))
                link(ts(ser, ser, 1.0 / k, None, ALU.add))
            link(stt(ser, ser, 2.0, z, ALU.mult, ALU.mult))
            link(tt(ser, ser, rate_p, ALU.add))
            ts(rate_n, ser, -8.0, None, ALU.mult)
            ts(rate_p, ser, 8.0, None, ALU.mult).then_inc(S["r_ready"], 1)
            dve.wait_ge(S["pads_ready"], 3)
            for c in range(4):
                dve.wait_ge(S["lx_ready"], c // 2 + 1)
                link(ts(xc[:, c, :], lxp[:, c, 0:T], V("conv_w", 4 * c), V("conv_b", c), ALU.mult, ALU.add))
                for t in range(1, 4):
                    o = stt(xc[:, c, :], lxp[:, c, t:t + T], V("conv_w", 4 * c + t), xc[:, c, :],
                            ALU.mult, ALU.add)
                    if t < 3:
                        link(o)
                o.then_inc(S["xc_ready"], 1)

            def rotated(src, rot, n, dst, cos, sin):
                link(tt(tv[:, 0, 0:n * T].rearrange("p (a t) -> p a t", a=n), src, over(tb(cos), n), ALU.mult))
                link(tt(tv[:, 1, 0:n * T].rearrange("p (a t) -> p a t", a=n), rot, over(tb(sin), n), ALU.mult))
                return tt(dst, tv[:, 0, 0:n * T].rearrange("p (a t) -> p a t", a=n),
                          tv[:, 1, 0:n * T].rearrange("p (a t) -> p a t", a=n), ALU.add)

            dve.wait_ge(S["rot_mm"], 3)
            dve.wait_ge(S["hstd_ready"], 1)
            link(dve.reciprocal(rinv[:, 0:T], std[:, 0:T]))
            link(rotated(qg[:, 4:5, :], PS[4][:, T:2 * T].unsqueeze(1), 1, qg[:, 4:5, :], "cos1", "sin1"))
            mark(tt(kz[0:64, 0, :], qg[0:64, 4, :], rinv[0:64, 0:T], ALU.mult))
            tt(kz[64:128, 1, :], qg[64:128, 4, :], rinv[64:128, 0:T], ALU.mult).then_inc(S["qn_ready"], 1)
            for j in range(2):
                dve.wait_ge(S["hstd_ready"], j + 2)
                link(dve.reciprocal(rinv[:, :], std[:, :]))
                pair = qg[:, 2 * j:2 * j + 2, :]
                link(rotated(pair, two(2 + j), 2, pair, "cos1", "sin1"))
                tt(pair, pair, rinv[:, :].rearrange("p (a t) -> p a t", a=2), ALU.mult)\
                    .then_inc(S["qn_ready"], 1)

            dve.wait_ge(S["lgsq_ready"], 1)
            lg_, x_ = lgate[:, :, :], gtmp[:, :, :]
            link(tt(sq[:, :, :], rr[:, :, :], rr[:, :, :], ALU.mult))
            stt(th[:, :, :], sq[:, :, :], 1.0, th[:, :, :], ALU.add, ALU.mult).then_inc(S["m_ready"], 1)
            link(ts(x_, x_, 0.044715, 1.0, ALU.mult, ALU.add))
            tt(x_, x_, lg_, ALU.mult).then_inc(S["ginner_ready"], 1)
            bt = ii[:, :, :].rearrange("p (d c) t -> p d c t", d=2)
            link(tt(bt, bt, xc[:, :, :].unsqueeze(1).broadcast_to((P, 2, 4, T)), ALU.mult))
            dve.wait_ge(S["mult_ready"], 1)
            link(tt(ii[:, :, :], ii[:, :, :], th[:, :, :], ALU.mult))

            def lru_tail(a):
                if a < 4:
                    c = a
                    dve.tensor_tensor_scan(th[:, c, :], rr[:, c, :], ii[:, c, :], 0.0, ALU.mult, ALU.add)
                    mark(dve.tensor_tensor_scan(th[:, 4 + c, ::-1], rr[:, 4 + c, ::-1], ii[:, 4 + c, ::-1], 0.0,
                                                ALU.mult, ALU.add))
                if a == 4:
                    dve.wait_ge(S["gsig_ready"], 1)
                    mark(tt(lg_, lg_, x_, ALU.mult))
                    settle()
                    link(tt(xc[:, :, :], th[:, 0:4, :], th[:, 4:8, :], ALU.add))
                    tt(xc[:, :, :], xc[:, :, :], lg_, ALU.mult).then_inc(S["lru_ready"], 1)

            heads(0, 8, 0.125, between=lru_tail)
            dve.wait_ge(S["ostd_ready"], 1)
            link(dve.reciprocal(rinv[:, :], std[:, :]))
            for k in range(C):
                src, g = (at1, "attn_g") if k < 4 else (xc, "lru_g")
                stt(xn[:, k, :], src[:, k % 4, :], V(g, k % 4), rinv[:, T * (k // 4):T * (k // 4) + T],
                    ALU.mult, ALU.mult).then_inc(S["mixed_ready"], 1)
            residual(AT["w_out"])
            norm(1, "norm2", xn)

            dve.wait_ge(S["rout_mm"], 1)
            dve.wait_ge(S["pads_ready"], 6)
            tt(lg[:, :, 0:E], PS[5][:, 0:2 * E].rearrange("p (a e) -> p a e", a=2), over(br[:, :], 2), ALU.add)\
                .then_inc(S["lg_ready"], 1)
            dve.wait_ge(S["lg_ready"], 1)
            for tk in range(2):
                mark(dve.max(m8[:, tk, :], lg[:, tk, 0:E]))
            settle()
            ts(gs[:, 0:2].unsqueeze(2), m8[:, :, 0:1], -1.0, None, ALU.mult).then_inc(S["lg_ready"], 1)
            link(dve.memset(m8[:, :, 4:8], 3.0e38))
            for tk in range(2):
                mark(dve.match_replace(lg2[:, tk, 0:E + 4], m8[:, tk, :], lg[:, tk, 0:E + 4], FAR))
            settle()
            ts(msk[:, :, :], lg2[:, :, 0:E], 0.9 * FAR, None, ALU.is_le).then_inc(S["mask_ready"], 1)
            dve.wait_ge(S["mask_ready"], 1)
            dve.wait_ge(S["gex_ready"], 1)
            link(tt(exr[:, :, :], exr[:, :, :], msk[:, :, :], ALU.mult))
            link(dve.tensor_reduce(gs[:, 2:4], exr[:, :, :], AX, ALU.add))
            link(dve.reciprocal(gs[:, 2:4], gs[:, 2:4]))
            tt(G[:, :, 0:E], exr[:, :, :], along(gs[:, 2:4], E), ALU.mult).then_inc(S["lg_ready"], 1)
            dve.wait_ge(S["cnt_mm"], 1)
            cp = PS[5][:, 64:64 + 3 * E].rearrange("p (a e) -> p a e", a=3)
            link(stt(key[:, :, 0:E], cp[:, 0:2, :], 1.0, msk[:, :, :], ALU.add, ALU.mult))
            link(ts(key[:, :, 0:E], key[:, :, 0:E], -1.0, None, ALU.add))
            nar = exr[:, 0, :]
            link(ts(nar, cp[:, 2, :], float(NARROW), None, ALU.is_le))
            link(tt(msk[:, :, :], msk[:, :, :], over(nar, 2), ALU.mult))
            link(stt(key2[:, :, 0:E], key[:, :, 0:E], float(NARROW + 1), msk[:, :, :], ALU.add, ALU.mult))
            link(ts(key2[:, :, 0:E], key2[:, :, 0:E], -1.0, None, ALU.add))
            mark(dve.tensor_copy(load[:, :], cp[:, 2, :]))
            link(dve.tensor_reduce(cnt[:, 0:1], cp[:, 2, :], AX, ALU.max))
            dve.tensor_copy(flag[:, :], cnt[:, 0:1]).then_inc(S["flag_ready"], 1)

            def select(n, e, b, general, step):
                io = tb("iota")[:, b * WIDE:(b + 1) * WIDE]
                for tk in range(2):
                    o = ts(sel[:, tk, :], io, key[:, tk, bass.ds(e, 1)], None, ALU.is_equal)
                    if general:
                        step.mark(o)
                    else:
                        step.link(o)
                        step.mark(stt(sel[:, tk, :], io, key2[:, tk, bass.ds(e, 1)], sel[:, tk, :],
                                      ALU.is_equal, ALU.add))
                step.settle()
                for tk in range(2):
                    last = ts(selg[:, tk, :], sel[:, tk, :], G[:, tk, bass.ds(e, 1)], None, ALU.mult)
                last.then_inc(M["sel_ready"], 1)

            def swiglu(n, e, w, wide, step):
                r_ = ROUND[w]
                shape = "p (k c h) -> p k c h"
                mb = mbias[:, bass.ds(e * 16, 16)].rearrange(shape, k=2, c=4)
                bias = [mb[:, kind, :, w:w + 1] if wide else mb[:, kind, :, :] for kind in range(2)]

                def cast(v):
                    return v.rearrange("p (c h n) -> p c h n", c=4, h=1 if wide else 2)

                def spread(v):
                    return v.unsqueeze(3).broadcast_to((P, 4, 1, WIDE) if wide else (P, 4, 2, NARROW))

                dve.wait_ge(M["tg_mm" + r_], n + 1)
                step.link(tt(cast(ge), cast(PS[6][:, :]), spread(bias[0]), ALU.add))
                ts(ge, ge, 7.0, None, ALU.min).then_inc(M["sig_in" + r_], 1)
                dve.wait_ge(M["tu_mm" + r_], n + 1)
                step.link(tt(cast(ue), cast(PS[7][:, :]), spread(bias[1]), ALU.add))
                step.link(ts(ue, ue, 7.0, -7.0, ALU.min, ALU.max))
                step.link(stt(ue, ue, 1.0, ge, ALU.add, ALU.mult))
                dve.wait_ge(M["sig_ready" + r_], n + 1)
                tt(hT[w][:, :, :], ue.rearrange("p (c n) -> p c n", c=4),
                   sg.rearrange("p (c n) -> p c n", c=4), ALU.mult).then_inc(M["h_ready" + r_], 1)
                dve.wait_ge(M["h_ready" + r_], n + 1)

            def dve_pass(n, e, nb, ne, wide, general, chain_at, chain2_at):
                step = Chain(dve, M["chain"], chain_at)
                step2 = Chain(dve, M["chain2"], chain2_at)
                dve.wait_ge(M["selT_mm"], n + 1)
                dve.wait_ge(M["xs_mm"], n + 1)
                select(n + 1, ne, nb, general, step)
                swiglu(n, e, 0, wide, step)
                if wide:
                    swiglu(n, e, 1, wide, step2)
                    assert step2.n == STEPS2
                else:
                    dve.sem_inc(M["chain2"], STEPS2)
                    dve.sem_inc(M["sig_in2"], 1)
                    dve.sem_inc(M["h_ready2"], 1)
                dve.sem_inc(M["passed"], 1)
                assert step.n == (STEPS_G if general else STEPS)

            STEPS, STEPS_G, STEPS2 = 8, 6, 4
            dve.wait_ge(S["flag_ready"], 1)
            dve.wait_ge(S["router_loaded"], 48)
            most = dve.value_load(flag[0:1, 0:1], min_val=0, max_val=T)
            with dve.If(most < WIDE + 1):
                first = Chain(dve, M["chain"])
                select(0, 0, 0, False, first)
                with dve.Fori(0, E) as e:
                    at = e * STEPS + first.n
                    with dve.If(dve.value_load(load[0:1, bass.ds(e, 1)], min_val=0, max_val=T) < NARROW + 1):
                        dve_pass(e, e, 0, e + 1, False, False, at, e * STEPS2)
                    with dve.Else():
                        dve_pass(e, e, 0, e + 1, True, False, at, e * STEPS2)
                    dve.nop()
            with dve.Else():
                first = Chain(dve, M["chain"])
                select(0, 0, 0, True, first)
                with dve.Fori(0, E) as e:
                    for b in range(BLOCKS):
                        n = e * BLOCKS + b
                        dve_pass(n, e, (b + 1) % BLOCKS, e + (b + 1) // BLOCKS, True, True,
                                 n * STEPS_G + first.n, n * STEPS2)

            norm(2, "final", xT)
            norm(3, "mix0", xn)

            for j in range(5):
                dve.wait_ge(S["iqrot_mm"], j + 1)
                if j < 4:
                    pair = iqr[:, 2 * j:2 * j + 2, :]
                    cs = iqt
                    if j:
                        dve.wait_ge(S["iqn_ready"], j)
                    link(tt(cs[:, :, :], pair, over(tb("cos3"), 2), ALU.mult))
                    tt(tsq[:, 0, :].rearrange("p (a t) -> p a t", a=2), two(6 + j % 2), over(tb("sin3"), 2),
                       ALU.mult).then_inc(S["iqrot_read"], 1)
                    dve.wait_ge(S["iqrot_read"], j + 1)
                    tt(pair, cs[:, :, :], tsq[:, 0, :].rearrange("p (a t) -> p a t", a=2), ALU.add)\
                        .then_inc(S["iqn_ready"], 1)
                else:
                    dve.wait_ge(S["iqn_ready"], 4)
                    link(tt(iqt[:, 0, :], tv[:, 0, 0:T], tb("cos3"), ALU.mult))
                    tt(iqt[:, 1, :], PS[6][:, 0:T], tb("sin3"), ALU.mult).then_inc(S["iqrot_read"], 1)
                    dve.wait_ge(S["iqrot_read"], 5)
                    dve.wait_ge(S["pads_ready"], 8)
                    tt(iz[0:64, 0, :], iqt[0:64, 0, :], iqt[0:64, 1, :], ALU.add)
                    tt(iz[64:128, 1, :], iqt[64:128, 0, :], iqt[64:128, 1, :], ALU.add)\
                        .then_inc(S["iqn_ready"], 1)
            dve.wait_ge(S["iw_ready"], 1)

            def add_index(h):
                dve.wait_ge(S["relu_ready"], h + 1)
                for b in range(2):
                    if h == 0:
                        last = ts(sc[:, b, :], rl[0][:, b, :], iw[:, b, 0:1], None, ALU.mult)
                    else:
                        if b == 0:
                            dve.wait_ge(S["relu_used"], h)
                        last = stt(sc[:, b, :], rl[h % 2][:, b, :], iw[:, b, h:h + 1], sc[:, b, :],
                                   ALU.mult, ALU.add)
                last.then_inc(S["relu_used"], 1)

            for j in range(4):
                for h in range(4 * j, 4 * j + 4):
                    add_index(h)
                dve.wait_ge(S["drot_mm"], j + 1)
                dve.wait_ge(S["dstd_ready"], j + 1)
                link(dve.reciprocal(rinv[:, :], std[:, :]))
                pair = dqk[:, 2 * j:2 * j + 2, :]
                link(rotated(pair, two(5), 2, pair, "cos2", "sin2"))
                tt(pair, pair, rinv[:, :].rearrange("p (a t) -> p a t", a=2), ALU.mult)\
                    .then_inc(S["dqn_ready"], 1)
            dve.wait_ge(S["relu_used"], 16)
            link(tt(sc[:, :, :], sc[:, :, :], tb("far").rearrange("p (b t) -> p b t", b=2), ALU.add))
            dve.wait_ge(S["u_ready"], 2)
            link(tt(w1[:, :, 1:272], up[:, :, 1:272], up[:, :, 0:271], ALU.add))
            link(tt(w2[:, 1:4, 3:272], w1[:, 1:4, 3:272], w1[:, 1:4, 1:270], ALU.add))
            link(tt(w1[:, 2:4, 7:272], w2[:, 2:4, 7:272], w2[:, 2:4, 3:268], ALU.add))
            link(tt(w2[:, 3:4, 15:272], w1[:, 3:4, 15:272], w1[:, 3:4, 7:264], ALU.add))
            rc = tb("rcount").rearrange("p (g t) -> p g t", g=4)
            for g in range(4):
                w = w2 if g % 2 else w1
                mark(tt(iqt[:, 0, 16 * g:16 * g + 16], w[:, g, 16:32], rc[:, g, :], ALU.mult))
                link(stt(iqt[:, 1, :], w[:, g, 16:272], 0.5 ** (g + 1), up[:, g, 16:272], ALU.mult, ALU.subtract))
                mark(dve.tensor_copy(w1[:, g, 16:256], iqt[:, 1, 16:256]))
                tt(w1[:, g, 0:16], iqt[:, 0, 16 * g:16 * g + 16], up[:, g, 16:32], ALU.subtract)\
                    .then_inc(S["pooled_ready"], 1)
                dve.wait_ge(S["pooled_ready"], g + 1)
            for rnd in range(ROUNDS):
                for b in range(2):
                    mark(dve.max(m8b[:, b, :], sc[:, b, :]))
                settle()
                for b in range(2):
                    mark(dve.match_replace(sc[:, b, :], m8b[:, b, :], sc[:, b, :], TAKEN))
                settle()
            link(ts(pen[:, :, :], sc[:, :, :], 0.5 * (FAR + TAKEN), 1.0e30, ALU.is_le, ALU.mult))
            link(stt(pen[:, :, :], pen[:, :, :], -1.0e30, tb("far").rearrange("p (b t) -> p b t", b=2),
                     ALU.add, ALU.add))
            heads(8, 4, float(P) ** -0.5, sparse=True)
            residual(AT["ab_out"])

            def memory(l):
                if l == 0:
                    dve.wait_ge(S["mstd_ready"], 1)
                    link(dve.reciprocal(rmem, rmem))
                dve.wait_ge(S["mem_loaded"], 16 * (l + 1))
                for k in range(C):
                    stt(memn[:, k, :], memT[l][:, k, :], V(f"mem{l}", k), rmem, ALU.mult, ALU.mult)\
                        .then_inc(S["memn_ready"], 1)

            def cross_norms(l, side, dst):
                for j in range(4):
                    p = 8 * l + 4 * side + j
                    dve.wait_ge(S["ckstd_ready"], p + 1)
                    link(dve.reciprocal(rinv[:, T:2 * T], std[:, T:2 * T]))
                    pair = dst[:, 2 * j:2 * j + 2, :]
                    tt(pair, pair, over(rinv[:, T:2 * T], 2), ALU.mult).then_inc(S["ckn_ready"], 1)

            def cross(l):
                norm(4 + 3 * l, f"cross{l}", xn)
                memory(l)
                cross_norms(l, 0, ckn)
                cross_norms(l, 1, cqn)
                heads(12 + 4 * l, 4, 1.0 / 16)
                residual(AT[f"co{l}"])
                norm(5 + 3 * l, f"ffn{l}", xn)

            def ffn(l):
                for g in range(NG):
                    n = NG * l + g
                    dve.wait_ge(S["f_sig"], n + 1)
                    gb, ub = two(4 + 2 * (g % 2)), two(5 + 2 * (g % 2))
                    link(tt(fs[g % 2][:, :, :], gb, fs[g % 2][:, :, :], ALU.mult))
                    dve.wait_ge(S["units_done"], AT[f"ffn{l}"] + ffn_gate_unit(g) + 2)
                    tt(fh[g % 2][:, :, :], ub, fs[g % 2][:, :, :], ALU.mult).then_inc(S["f_h"], 1)
                dve.wait_ge(S["units_done"], AT[f"ffn{l}"] + 3 * NG)
                for j in range(4):
                    tt(xT[:, 2 * j:2 * j + 2, :], two(j), xT[:, 2 * j:2 * j + 2, :], ALU.add)\
                        .then_inc(S["res_ready"], 1)

            cross(0)
            ffn(0)
            norm(6, "mix1", xn)
            dve.wait_ge(S["pads_ready"], 9)
            for j in range(8):
                dve.wait_ge(S["conv_sig"], j + 1)
                stt(hp[:, j, 30:30 + T], two(j % 4)[:, 0, :], V("cin_b", j), csg[:, j % 2, :], ALU.add, ALU.mult)\
                    .then_inc(S["hp_ready"], 1)
            dve.wait_ge(S["hp_ready"], 8)
            for t in range(TAPS):
                for c in range(4, C):
                    w = V("dw", c * TAPS + t)
                    if t == 0:
                        mark(ts(hc[:, c, :], hp[:, c, 0:T], w, V("dw_b", c), ALU.mult, ALU.add))
                    elif t < TAPS - 1:
                        dve.wait_ge(S["dve_chain"], chain.n - 3)
                        mark(stt(hc[:, c, :], hp[:, c, t:t + T], w, hc[:, c, :], ALU.mult, ALU.add))
                    else:
                        settle()
                        stt(hc[:, c, :], hp[:, c, t:t + T], w, hc[:, c, :], ALU.mult, ALU.add)\
                            .then_inc(S["hc_dve"], 1)
            dve.wait_ge(S["lnsum_mm"], 1)
            dve.wait_ge(S["hc_dve"], 4)
            dve.wait_ge(S["hc_pe"], 4)
            link(ts(rinv[:, 0:T], PS[0][:, 0:T], 1.0 / D, None, ALU.mult))
            for j in range(4):
                pair = hc[:, 2 * j:2 * j + 2, :]
                tt(pair, pair, over(rinv[:, 0:T], 2), ALU.subtract).then_inc(S["lnd_ready"], 1)
            dve.wait_ge(S["lnstd_ready"], 1)
            link(dve.reciprocal(rinv[:, 0:T], std[:, 0:T]))
            for c in range(C):
                stt(hc[:, c, :], hc[:, c, :], V("ln_g", c), rinv[:, 0:T], ALU.mult, ALU.mult)\
                    .then_inc(S["lnz_ready"], 1)
            for c in range(C):
                dve.wait_ge(S["lnsig_ready"], c + 1)
                stt(yc[:, c, :], hc[:, c, :], V("ln_b", c), sq[:, c, :], ALU.add, ALU.mult)\
                    .then_inc(S["yc_ready"], 1)
            residual(AT["conv_out"])
            cross(1)
            ffn(1)



def columns(v):
    return v.reshape(-1, P).T


def stationary_units(w):
    n = w.shape[1] // 256
    return w.reshape(C, P, n, 2, P).transpose(2, 1, 3, 0, 4).reshape(n, P, UNIT)


def row_units(w):
    kk = UNIT // w.shape[1]
    n = w.shape[0] // (P * kk)
    return w.reshape(n, kk, P, w.shape[1]).transpose(0, 2, 1, 3).reshape(n, P, UNIT)


def lay_out_stream(a):
    s = np.zeros((N_UNITS, P, UNIT), np.float32)

    def put(name, units):
        s[AT[name]:AT[name] + len(units)] = units

    w = a["w_in"][0]
    put("lru_x", stationary_units(w[:, 768:1280]))
    put("q", stationary_units(w[:, 0:512].reshape(D, 2, 4, 64).transpose(0, 2, 1, 3).reshape(D, 512)))
    put("kv", stationary_units(w[:, 512:768]))
    put("lru_gate", stationary_units(w[:, 1280:1792]))
    gates = s[AT["lru_w"]].reshape(P, 2, 2, 4, P)
    for kind, name in enumerate(("lru_wa", "lru_wi")):
        for d in range(2):
            for c in range(4):
                for h in range(2):
                    r = slice(64 * h, 64 * h + 64)
                    gates[r, d, kind, c, r] = a[name][0, d, 2 * c + h]
    w = a["w_out"][0]
    w = np.concatenate([w[:512].reshape(2, 4, 64, D).transpose(1, 0, 2, 3).reshape(512, D), w[512:]])
    put("w_out", stationary_units(w))
    moe = s[AT["moe"]:AT["moe"] + 12 * E].reshape(E, 12, P, UNIT)
    for e in range(E):
        for i, name in enumerate(("w_gate", "w_up", "w_down")):
            moe[e, 4 * i:4 * i + 4] = row_units(a[name][0, e])
    w = a["w_in_ab_2"][0]
    put("dq", stationary_units(w[:, 0:512]))
    put("dk", stationary_units(w[:, 512:1024]))
    put("dv", row_units(w[:, 1024:1536]))
    put("u", stationary_units(w[:, 1536:2048]))
    put("iq", stationary_units(w[:, 2048:3072]))
    one = s[AT["ikiw"]]
    ik = w[:, 3088:3152]
    one[:, 0:D] = np.concatenate([ik, ik], 1).reshape(C, P, P).transpose(1, 0, 2).reshape(P, D)
    one[:, D:D + 16 * C] = w[:, 3072:3088].reshape(C, P, 16).transpose(1, 0, 2).reshape(P, 16 * C)
    s[AT["pool"]][:, 0:4 * P] = a["pool_w_2"][0].transpose(1, 0, 2).reshape(P, 4 * P)
    put("ab_out", stationary_units(a["w_out_ab_2"][0]))
    put("conv_in", stationary_units(a["conv_w_in_2"][0].reshape(D, 2, C, P).transpose(0, 2, 1, 3)
                                    .reshape(D, 2 * D)))
    put("conv_out", stationary_units(a["conv_w_out_2"][0]))
    for l in range(2):
        put(f"ck{l}", stationary_units(a["cross_wk_2"][l]))
        put(f"cv{l}", row_units(a["cross_wv_2"][l]))
        put(f"cq{l}", stationary_units(a["cross_wq_2"][l]))
        put(f"co{l}", stationary_units(a["cross_wo_2"][l]))
        f = s[AT[f"ffn{l}"]:AT[f"ffn{l}"] + 3 * NG]
        g, u = (stationary_units(a[n][l]) for n in ("ffn_w_gate_2", "ffn_w_up_2"))
        d = row_units(a["ffn_w_down_2"][l])
        for i in range(NG):
            f[ffn_gate_unit(i)] = g[i]
            f[ffn_gate_unit(i) + 1] = u[i]
            f[min(3 * i + 4, 3 * NG - 1)] = d[i]
    return s


def lay_out_vectors(a):
    v = np.zeros((P, NV), np.float32)

    def put(name, m):
        v[:, VAT[name]:VAT[name] + m.shape[1]] = m

    for name, value in (("norm1", a["norm1_g"][0]), ("norm2", a["norm2_g"][0]), ("final", a["final_g"]),
                        ("mix0", a["norm_mix_2"][0]), ("mix1", a["norm_mix_2"][1]),
                        ("cross0", a["norm_cross_2"][0]), ("cross1", a["norm_cross_2"][1]),
                        ("mem0", a["norm_mem_2"][0]), ("mem1", a["norm_mem_2"][1]),
                        ("ffn0", a["norm_ffn_2"][0]), ("ffn1", a["norm_ffn_2"][1]),
                        ("gq", np.concatenate([a["q_norm_g"][0]] * 2)),
                        ("gk", np.concatenate([a["k_norm_g"][0]] * 2)),
                        ("conv_b", a["conv_b"][0]), ("lam", a["lru_lam"][0]),
                        ("lru_b", np.concatenate([a["lru_ba"][0].ravel(), a["lru_bi"][0].ravel()])),
                        ("attn_g", a["attn_out_g"][0].reshape(2, 4, 64).transpose(1, 0, 2)),
                        ("lru_g", a["lru_out_g"][0]), ("aq", a["a_q_norm_2"][0]), ("ak", a["a_k_norm_2"][0]),
                        ("pool_scale", a["pool_scale_2"][0]), ("cin_b", a["conv_b_in_2"][0]),
                        ("dw_b", a["conv_dw_b_2"][0]), ("ln_g", a["conv_ln_g_2"][0]),
                        ("ln_b", a["conv_ln_b_2"][0]), ("cqg0", a["cross_q_norm_2"][0]),
                        ("cqg1", a["cross_q_norm_2"][1]), ("ckg0", a["cross_k_norm_2"][0]),
                        ("ckg1", a["cross_k_norm_2"][1])):
        put(name, columns(value))
    put("conv_w", a["conv_w"][0].reshape(4, 4, P).transpose(2, 1, 0).reshape(P, 16))
    put("dw", a["conv_dw_w_2"][0].reshape(TAPS, C, P).transpose(2, 1, 0).reshape(P, C * TAPS))
    v[:, VAT["eps5"]] = 1e-5
    v[:, VAT["eps6"]] = 1e-6
    return v


def rotary(heads_at, half, inv, positions):
    cos, sin, rot = np.ones((P, T), np.float32), np.zeros((P, T), np.float32), np.zeros((P, P), np.float32)
    for start, pos in zip(heads_at, positions):
        ang = inv[:, None].astype(np.float32) * pos[None, :].astype(np.float32)
        for i in range(half):
            lo, hi = start + i, start + half + i
            cos[lo] = cos[hi] = np.cos(ang[i])
            sin[lo] = sin[hi] = np.sin(ang[i])
            rot[hi, lo] = -1.0
            rot[lo, hi] = 1.0
    return cos, sin, rot


def lay_out_tables():
    t = np.zeros((P, NT), np.float32)

    def put(name, m):
        t[:, TAT[name]:TAT[name] + m.shape[1]] = m

    tok = np.arange(T)
    f = np.float32
    axial = f(10000.0) ** (-np.arange(16, dtype=f) / f(16))
    inv2 = f(500000.0) ** (-np.arange(16, dtype=f) * f(2.0) / f(32))
    inv3 = f(500000.0) ** (-np.arange(8, dtype=f) * f(2.0) / f(16))
    for n, (cos, sin, rot) in enumerate((rotary((0, 32, 64, 96), 16, axial, (tok // 64, tok % 64) * 2),
                                         rotary((0,), 16, inv2, (tok,)),
                                         rotary((0, 64), 8, inv3, (tok, tok))), 1):
        put(f"cos{n}", cos)
        put(f"sin{n}", sin)
        put(f"rot{n}", rot)
    i = np.arange(P)
    put("ident", np.eye(P, dtype=f))
    put("ones", np.ones((P, P), f))
    put("heads", (i[:, None] // 64 == i[None, :] // 64).astype(f))
    put("before", (i[:, None] < i[None, :]).astype(f))
    put("iota", np.broadcast_to(tok.astype(f), (P, T)))
    q = i[:, None, None] + P * np.arange(2)[None, :, None]
    put("far", np.where(tok[None, None, :] > q, f(FAR), f(0)).reshape(P, 2 * T))
    w = 2 ** np.arange(1, 5)[:, None]
    put("rcount", np.broadcast_to((f(1) / np.minimum(np.arange(16)[None, :] + 1, w).astype(f)).reshape(1, 64),
                                  (P, 64)))
    return t


def token_chunks(m):
    return np.ascontiguousarray(m[0].T.reshape(C, P, T).transpose(1, 0, 2))


def kernel(**inputs):
    import concourse.bacc as _bacc
    from concourse.bass_utils import run_bass_kernel_spmd as _run

    a = {k: np.asarray(v) for k, v in inputs.items()}
    gate, up = (a[n][0].reshape(E, 2, 4, P) for n in ("b_gate", "b_up"))
    arrays = {
        "x": token_chunks(a["x"]),
        "mem": token_chunks(a["mem_2"]),
        "stream": lay_out_stream(a),
        "vecs": lay_out_vectors(a),
        "tables": lay_out_tables(),
        "moe_b": np.ascontiguousarray(np.stack([gate, up], 1).transpose(4, 0, 1, 3, 2).reshape(P, E * 16)),
        "b_down": np.ascontiguousarray(a["b_down"][0]),
        "w_router": np.ascontiguousarray(a["w_router"][0].reshape(C, P, E).transpose(1, 0, 2)),
        "b_router": np.ascontiguousarray(np.broadcast_to(a["b_router"][0], (P, E))),
    }
    nc = _bacc.Bacc("TRN2", target_bir_lowering=False, num_devices=1)
    args = [nc.dram_tensor(f"in_{n}", v.shape, mybir.dt.from_np(v.dtype), kind="ExternalInput").ap()
            for n, v in arrays.items()]
    out = nc.dram_tensor("out_y", (P, C, T), F32, kind="ExternalOutput").ap()
    build(nc, *args, out)
    r = _run(nc, [{f"in_{n}": v for n, v in arrays.items()}], core_ids=[0])
    y = r.results[0]["out_y"]
    return np.ascontiguousarray(y.transpose(1, 0, 2).reshape(D, T).T)[None]
```

```python
from contextlib import ExitStack

import numpy as np

import concourse.bass as bass
from concourse import mybir

F32 = mybir.dt.float32
I32 = mybir.dt.int32
ALU = mybir.AluOpType
ACT = mybir.ActivationFunctionType
AX = mybir.AxisListType.X

P = 128
T = 256
D = 1024
C = D // P
UNIT = 2048
RING = 12
E = 32
NARROW = 64
WIDE = 128
BLOCKS = T // WIDE
FF2 = 2816
NG = FF2 // 256
TAPS = 31
ROUNDS = 64 // 8
FAR = -3.0e38
TAKEN = -3.4e38

PLAN = [("lru_x", 2), ("q", 2), ("lru_w", 1), ("lru_gate", 2), ("kv", 1), ("cv0", 4), ("ck0", 4),
        ("ck1", 4), ("cv1", 4), ("w_out", 4), ("moe", 12 * E),
        ("iq", 4), ("ikiw", 1), ("dq", 2), ("dk", 2), ("u", 2), ("dv", 2), ("pool", 1), ("ab_out", 4),
        ("cq0", 4), ("co0", 4), ("ffn0", 3 * NG),
        ("conv_in", 8), ("conv_out", 4),
        ("cq1", 4), ("co1", 4), ("ffn1", 3 * NG)]
AT = {}
N_UNITS = 0
for _name, _n in PLAN:
    AT[_name] = N_UNITS
    N_UNITS += _n

HELD = 8
EARLY = AT["w_out"]
assert EARLY % HELD == 0 and RING == 12
MOE_AT = AT["moe"] - EARLY


def slot_of(u):
    return u % HELD if u < EARLY else (u - EARLY) % RING


def loads_of(u):
    if u < EARLY:
        return u // HELD + 1
    return (u - EARLY) // RING + 1 + (EARLY // HELD if slot_of(u) < HELD else 0)


def expert_slot(j):
    return (MOE_AT + j) % RING


def expert_loads(j):
    return loads_of(AT["moe"] + j)


VECS = [("norm1", 8), ("norm2", 8), ("final", 8), ("mix0", 8), ("mix1", 8), ("cross0", 8), ("cross1", 8),
        ("mem0", 8), ("mem1", 8), ("ffn0", 8), ("ffn1", 8), ("gq", 1), ("gk", 1), ("conv_w", 16),
        ("conv_b", 4), ("lru_b", 16), ("lam", 8), ("attn_g", 4), ("lru_g", 4), ("aq", 1), ("ak", 1),
        ("pool_scale", 4), ("cin_b", 16), ("dw", 8 * TAPS), ("dw_b", 8), ("ln_g", 8), ("ln_b", 8),
        ("cqg0", 2), ("cqg1", 2), ("ckg0", 2), ("ckg1", 2), ("eps5", 1), ("eps6", 1)]
VAT = {}
NV = 0
for _name, _n in VECS:
    VAT[_name] = NV
    NV += _n

TABLES = [("cos1", T), ("sin1", T), ("cos2", T), ("sin2", T), ("cos3", T), ("sin3", T), ("rot1", P),
          ("rot2", P), ("rot3", P), ("ident", P), ("ones", P), ("heads", P), ("before", P), ("iota", T),
          ("far", 2 * T), ("rcount", 64)]
TAT = {}
NT = 0
for _name, _n in TABLES:
    TAT[_name] = NT
    NT += _n


RES = {1: 0, 4: 1, 5: 2, 6: 3, 7: 4, 8: 5}


def stat_bank(n):
    return 7 if n == 3 else 6


def ffn_gate_unit(g):
    return 3 * g - 1 if g else 0


class Chain:

    def __init__(self, eng, sem, offset=0):
        self.eng, self.sem, self.offset, self.n = eng, sem, offset, 0

    def mark(self, ins):
        ins.then_inc(self.sem, 1)
        self.n += 1

    def settle(self):
        self.eng.wait_ge(self.sem, self.offset + self.n)

    def link(self, ins):
        self.mark(ins)
        self.settle()


def build(nc, x, mem, stream, vecs, tables, moe_b, b_down, w_router, b_router, mem_kv, out):
    with ExitStack() as ctx:
        def sb(name, shape, dt=F32):
            return ctx.enter_context(nc.sbuf_tensor(name, shape, dt))

        def sem(name):
            return ctx.enter_context(nc.semaphore(name))

        ring = sb("ring", [P, RING, UNIT])
        xT = sb("xT", [P, C, T])
        xn = sb("xn", [P, C, T])
        sq = sb("sq", [P, C, T])
        B = sb("B", [P, 12560])
        vec = sb("vec", [P, NV])
        tab = sb("tab", [P, NT])
        mbias = sb("mbias", [P, E * 16])
        wr = sb("wr", [P, C, E])
        br = sb("br", [P, E])
        tsq = sb("tsq", [P, 2, 512])
        tv = sb("tv", [P, 2, 512])
        prob = sb("prob", [P, 2, 2, T])
        pT = sb("pT", [P, 2, 2, T])
        std = sb("std", [P, 512])
        rinv = sb("rinv", [P, 512])
        small = sb("small", [P, 32])
        mx = sb("mx", [P, 2])
        rs = sb("rs", [P, 2])
        lam3 = sb("lam3", [P, 24])
        m8b = sb("m8b", [P, 2, 8])
        nst = sb("nst", [P, 2])
        rq = sb("rq", [P, 8])
        ksum = sb("ksum", [P, 16])
        flag = sb("flag", [P, 1], I32)
        load = sb("load", [P, E], I32)
        PS = [ctx.enter_context(nc.psum_tensor(f"bank{i}", [P, 512], F32)) for i in range(8)]

        def V(name, i=0, n=1):
            return vec[:, VAT[name] + i:VAT[name] + i + n]

        def tb(name):
            return tab[:, TAT[name]:TAT[name] + dict(TABLES)[name]]

        def reg(a, *shape, rows=P):
            n = int(np.prod(shape))
            v = B[0:rows, a:a + n]
            if len(shape) == 2:
                return v.rearrange("p (a b) -> p a b", a=shape[0])
            if len(shape) == 3:
                return v.rearrange("p (a b c) -> p a b c", a=shape[0], b=shape[1])
            return v

        def two(bank):
            return PS[bank][:, :].rearrange("p (a t) -> p a t", a=2)

        def over(ap, n):
            return ap.unsqueeze(1).broadcast_to((P, n, ap.shape[-1]))

        def along(ap, n):
            return ap.unsqueeze(2).broadcast_to((ap.shape[0], ap.shape[1], n))

        lxp = reg(0, 4, 260)
        gtmp = reg(0, 4, T)
        xc = reg(1040, 4, T)
        lgate = reg(2064, 4, T)
        rr = reg(3088, 8, T)
        ii = reg(5136, 8, T)
        th = reg(7184, 8, T)
        qg = reg(9232, 5, T)
        at1 = reg(10512, 4, T)
        vt1 = reg(11536, 2, P)
        kz = reg(11792, 2, T)
        xtok = reg(0, 2, D)
        xs = reg(2048, C, WIDE)
        hT = [reg(3072 + 512 * w, 4, WIDE) for w in range(2)]
        gA = [reg(4096, 512), reg(10320, 512)]
        uA = [reg(4608, 512), reg(10832, 512)]
        ge = reg(5120, 512)
        ue = reg(5632, 512)
        sg = reg(6144, 512)
        yS = reg(6656, D)
        G = reg(7680, 2, E + 1)
        key = reg(7760, 2, E + 1)
        lg = reg(7840, 2, 40)
        lg2 = reg(7920, 2, 40)
        m8 = reg(8000, 2, 8)
        msk = reg(8016, 2, E)
        exr = reg(8080, 2, E)
        gs = reg(8144, 4)
        cnt = reg(8150, 2)
        GT = reg(8192, T, rows=E)
        bd = reg(8448, D, rows=E)
        sel = reg(9472, 2, WIDE)
        selg = reg(9728, 2, WIDE)
        selgT = reg(9984, T)
        key2 = reg(10240, 2, E + 1)
        iqr = reg(0, 8, T)
        iz = reg(2048, 2, T)
        iw = reg(2560, 2, 16)
        dqk = reg(2592, 8, T)
        dv = reg(4640, 2, 512)
        up = reg(5664, 4, 272)
        w1 = reg(6752, 4, 272)
        w2 = reg(7840, 4, 272)
        mix = reg(9680, 8, T)
        iqt = reg(9680, 2, T)
        rl = [reg(9680 + 512 * s, 2, T) for s in range(2)]
        sc = reg(11728, 2, T)
        pen = reg(8928, 2, T)
        ckn = [reg(4096, 8, T), reg(8192, 8, T)]
        cvt = [reg(6144, 2, D), reg(10240, 2, D)]
        cqn = [reg(8192, 8, T), reg(0, 8, T)]
        co = [reg(10240, 8, T), reg(2048, 8, T)]
        rmem = reg(12304, T)

        def held(i, a):
            return ring[:, HELD + i, :].rearrange("p (a b) -> p a b", a=a)

        memT = held(0, 8)
        kst = [held(1, 8), held(0, 8)]
        vst = held(2, 2)
        memn = held(3, 8)
        fh = [reg(512 * s, 2, T) for s in range(2)]
        fs = [reg(1024 + 512 * s, 2, T) for s in range(2)]
        hp = reg(0, 8, 286)
        hc = reg(2304, 8, T)
        yc = reg(4352, 8, T)
        csg = reg(6400, 2, T)
        ON_PE = (6, 7)
        NDIAG = 6
        diag = reg(7000, NDIAG, P)

        GATE_BANKS = (4, 5, 6, 7, 0, 1, 4, 5)
        hstd = [std[:, :], prob[:, 0, :, :].rearrange("p b t -> p (b t)"), prob[:, 1, 0, :]]

        landed = [sem(f"landed{s}") for s in range(RING)]
        names = """x_loaded consts_loaded router_loaded mem_loaded bd_loaded pads_ready units_done
            sq_ready stat_mm std_ready xn_ready res_ready dve_chain act_chain
            lam_exp lx_ready xc_ready qraw_ready qsq_ready vk_ready lgate_ready hstat_mm hstd_ready rot_mm
            rot_read qn_ready lru_mm lru_ev r_ready lgsq_ready ginner_ready gsig_ready m_ready mult_ready lru_ready
            score_mm nmax_ready exp_done probs_ready pT_mm pT_ready o_mm o_ready
            osq_ready ostat_mm ostd_ready mixed_ready cv_mm
            rout_mm lg_ready gex_ready mask_ready cnt_mm flag_ready tok_mm tok_ready acc_mm
            gt_mm gt_ready moe_mm xmoe_ready
            iq_ready iqrot_mm iqrot_read iqn_ready iw_ready iscore_mm relu_ready relu_used
            dqk_ready dsq_ready dstat_mm dstd_ready drot_mm dqn_ready dv_ready u_ready pooled_ready pool_mix
            msq_ready mstat_mm mstd_ready memn_ready ck_raw cksq_ready kstd_ready krec_ready kb_mm kn_ready
            cv_ready k_spilled v_spilled kv_back cq_raw cqsq_ready cqstat_mm cqstd_ready
            f_sig f_h conv_sig hp_ready diag_ready dwc_mm hc_pe hc_dve lnsum_mm lnd_ready lnsq_ready lnvar_mm
            lnstd_ready lnz_ready lnsig_ready yc_ready out_stored""".split()
        S = {n: sem(n) for n in names}
        moe_sem_names = """sel_ready selT_mm selT_ready xs_mm xs_ready y_mm y_ready scat_mm chain chain2 passed
            g_mm g_ready u_mm u_ready tg_mm tu_mm sig_in sig_ready h_ready
            g_mm2 g_ready2 u_mm2 u_ready2 tg_mm2 tu_mm2 sig_in2 sig_ready2 h_ready2""".split()
        M = {n: sem(f"moe_{n}") for n in moe_sem_names}
        ROUND = ("", "2")

        block = ctx.enter_context(nc.Block())

        @block.sync
        def _(sp):
            for dst, src in ((vec, vecs), (xT, x)):
                sp.dma_start(dst[:], src).then_inc(S["x_loaded"], 16)
            sp.dma_start(tab[:, TAT["ident"]:TAT["ones"] + P], tables[:, TAT["ident"]:TAT["ones"] + P])\
                .then_inc(S["x_loaded"], 16)
            for u in range(HELD):
                if u == 2:
                    for lo, hi in ((0, TAT["ident"]), (TAT["ones"] + P, NT)):
                        sp.dma_start(tab[:, lo:hi], tables[:, lo:hi]).then_inc(S["consts_loaded"], 16)
                if u == 4:
                    sp.dma_start(ring[:, HELD, :], mem).then_inc(S["mem_loaded"], 16)
                sp.dma_start(ring[:, u, :], stream[u]).then_inc(landed[u], 16)
            for dst, src in ((wr, w_router), (br, b_router), (mbias, moe_b)):
                sp.dma_start(dst[:], src).then_inc(S["router_loaded"], 16)
            for u in range(HELD, EARLY + RING):
                if slot_of(u) == HELD:
                    sp.wait_ge(S["k_spilled"], 32)
                    sp.wait_ge(S["v_spilled"], 32)
                    sp.wait_ge(S["units_done"], EARLY)
                elif slot_of(u) < HELD:
                    sp.wait_ge(S["units_done"], u - HELD + 1)
                sp.dma_start(ring[:, slot_of(u), :], stream[u]).then_inc(landed[slot_of(u)], 16)
            turns = (N_UNITS - EARLY) // RING
            with sp.Fori(1, turns) as i:
                for s in range(RING):
                    sp.wait_ge(S["units_done"], i * RING + (EARLY + s - RING + 1))
                    sp.dma_start(ring[:, s, :], stream[i * RING + (EARLY + s)]).then_inc(landed[s], 16)
            for u in range(EARLY + turns * RING, N_UNITS):
                sp.wait_ge(S["units_done"], u - RING + 1)
                sp.dma_start(ring[:, slot_of(u), :], stream[u]).then_inc(landed[slot_of(u)], 16)
            for j in range(4):
                sp.wait_ge(S["res_ready"], 4 * 6 + j + 1)
                sp.dma_start(out[:, 2 * j:2 * j + 2, :], xT[:, 2 * j:2 * j + 2, :]).then_inc(S["out_stored"], 16)
            sp.wait_ge(S["out_stored"], 64)

        @block.gpsimd
        def _(pool):
            pool.memset(lxp[:, :, 0:2], 0.0).then_inc(S["pads_ready"], 1)
            pool.memset(lxp[:, :, 258:260], 0.0).then_inc(S["pads_ready"], 1)
            pool.memset(kz[:, :, :], 0.0).then_inc(S["pads_ready"], 1)
            pool.wait_ge(S["cv_ready"], 4)
            pool.dma_start(mem_kv[1], ring[:, HELD + 2, :]).then_inc(S["v_spilled"], 16)
            pool.wait_ge(S["kn_ready"], 2)
            pool.dma_start(mem_kv[0], ring[:, HELD + 1, :]).then_inc(S["k_spilled"], 16)
            pool.wait_ge(S["kn_ready"], 4)
            pool.dma_start(mem_kv[2], ring[:, HELD, :]).then_inc(S["k_spilled"], 16)
            pool.wait_ge(S["cv_ready"], 8)
            pool.dma_start(mem_kv[3], ring[:, HELD + 2, :]).then_inc(S["v_spilled"], 16)
            pool.wait_ge(S["res_ready"], 4)
            pool.dma_start(bd[:, :], b_down).then_inc(S["bd_loaded"], 16)
            pool.memset(G[:, :, E:E + 1], 0.0).then_inc(S["pads_ready"], 1)
            pool.memset(key[:, :, E:E + 1], -1.0)
            pool.memset(key2[:, :, E:E + 1], -1.0).then_inc(S["pads_ready"], 1)
            pool.memset(lg[:, :, E:E + 4], 3.0e38).then_inc(S["pads_ready"], 1)
            pool.wait_ge(S["xmoe_ready"], 4)
            pool.memset(iz[:, :, :], 0.0).then_inc(S["pads_ready"], 1)
            pool.memset(up[:, :, 0:16], 0.0).then_inc(S["pads_ready"], 1)
            pool.wait_ge(S["o_ready"], 12)
            pool.dma_start(ckn[0][:, :, :], mem_kv[0].rearrange("p (a t) -> p a t", a=8)).then_inc(S["kv_back"], 16)
            pool.dma_start(cvt[0][:, :, :], mem_kv[1].rearrange("p (a t) -> p a t", a=2)).then_inc(S["kv_back"], 16)
            pool.wait_ge(S["res_ready"], 4 * 3)
            pool.dma_start(ckn[1][:, :, :], mem_kv[2].rearrange("p (a t) -> p a t", a=8)).then_inc(S["kv_back"], 16)
            pool.dma_start(cvt[1][:, :, :], mem_kv[3].rearrange("p (a t) -> p a t", a=2)).then_inc(S["kv_back"], 16)
            pool.wait_ge(S["res_ready"], 4 * 4)
            pool.memset(hp[:, :, 0:30], 0.0).then_inc(S["pads_ready"], 1)

        @block.tensor
        def _(pe):
            def tile(u, t, n=P):
                return ring[:, slot_of(u), t * P:t * P + n]

            def await_unit(u):
                pe.wait_ge(landed[slot_of(u)], 16 * loads_of(u))

            def stationary(u, dst, rhs, ready=None):
                await_unit(u)
                for m in range(2):
                    for k in range(C):
                        if ready is not None and m == 0:
                            pe.wait_ge(ready[0], ready[1] + k + 1)
                        mm = pe.matmul(dst[:, m, :], tile(u, m * C + k), rhs[:, k, :], start=(k == 0),
                                       stop=(k == C - 1))
                mm.then_inc(S["units_done"], 1)

            def stat_pair(n, j):
                pe.wait_ge(S["sq_ready"], 4 * n + j + 1)
                for c in (2 * j, 2 * j + 1):
                    for b in range(2):
                        mm = pe.matmul(PS[stat_bank(n)][:, b:b + 1], sq[:, c, b * P:(b + 1) * P], tb("ones")[:, 0:1],
                                       start=(c == b == 0), stop=(c == C - 1), skip_group_check=True)
                if j == 3:
                    mm.then_inc(S["stat_mm"], 1)
                    pe.wait_ge(S["std_ready"], 2 * n + 2)
                    for b in range(2):
                        mm = pe.matmul(PS[stat_bank(n)][:, b * P:(b + 1) * P], nst[:, b:b + 1].broadcast_to((P, P)),
                                       tb("ident"), start=True, stop=True)
                    mm.then_inc(S["stat_mm"], 1)

            def output_linear(first, rhs, n, ready=None):
                for j in range(4):
                    stationary(first + j, two(j), rhs, ready if j == 0 else None)
                    if j and n is not None:
                        stat_pair(n, j - 1)
                if n is not None:
                    stat_pair(n, 3)

            def heads(first, count, score, output, fill=None, fill_sum=None):
                def scores(a):
                    if a - first >= 2:
                        pe.wait_ge(S["exp_done"], a - 1)
                    score(a, two(2 + a % 2)).then_inc(S["score_mm"], 1)

                def outputs(a):
                    pe.wait_ge(S["probs_ready"], a + 1)
                    if a >= 2:
                        pe.wait_ge(S["pT_ready"], a - 1)
                    bank = two(6 + a % 2)
                    for kb in range(2):
                        for b in range(2):
                            mm = pe.transpose(bank[:, kb, b * P:(b + 1) * P],
                                              prob[:, a % 2, b, kb * P:(kb + 1) * P], tb("ident"))
                    mm.then_inc(S["pT_mm"], 1)
                    if a + 2 < first + count:
                        scores(a + 2)
                    pe.wait_ge(S["pT_ready"], a + 1)
                    if a >= 2:
                        pe.wait_ge(S["o_ready"], a - 1)
                    if fill_sum:
                        fill_sum(a)
                    output(a, two(4 + a % 2)).then_inc(S["o_mm"], 1)

                scores(first)
                scores(first + 1)
                for a in range(first, first + count):
                    if fill:
                        fill(a)
                    outputs(a)

            pe.wait_ge(S["x_loaded"], 48)
            for j in range(4):
                stat_pair(0, j)
            stationary(AT["lru_x"], two(0), xn, (S["xn_ready"], 0))
            pe.wait_ge(S["consts_loaded"], 32)
            stationary(AT["lru_x"] + 1, two(1), xn)
            for j in range(4):
                pe.wait_ge(S["msq_ready"], j + 1)
                for c in (2 * j, 2 * j + 1):
                    mm = pe.matmul(PS[7][:, 0:T], tb("ones"), kst[0][:, c, :], start=(c == 0), stop=(c == C - 1))
            mm.then_inc(S["mstat_mm"], 1)
            stationary(AT["q"], two(2), xn)
            stationary(AT["q"] + 1, two(3), xn)
            u = AT["lru_w"]
            await_unit(u)
            pe.wait_ge(S["xc_ready"], 4)
            for n in range(8):
                if n == 3:
                    pe.wait_ge(S["mstd_ready"], 1)
                if n >= 6:
                    pe.wait_ge(S["lru_ev"], n - 5)
                for c in range(2):
                    mm = pe.matmul(two(GATE_BANKS[n])[:, c, :], tile(u, 2 * n + c), xc[:, 2 * (n % 2) + c, :],
                                   start=True, stop=True)
                mm.then_inc(S["lru_mm"] if n < 7 else S["units_done"], 1)
            for j in range(2):
                pe.wait_ge(S["qsq_ready"], j + 1)
                pe.wait_ge(S["lru_ev"], j + 3)
                pe.matmul(PS[6 + j][:, :], tb("heads"), tsq[:, j, :], start=True, stop=True)\
                    .then_inc(S["hstat_mm"], 1)
                pe.wait_ge(S["qraw_ready"], j + 1)
                pe.matmul(two(2 + j), tb("rot1"), qg[:, 2 * j:2 * j + 2, :], start=True, stop=True)\
                    .then_inc(S["rot_mm"], 1)
            for j in range(2):
                pe.wait_ge(S["lru_ev"], j + 5)
                stationary(AT["lru_gate"] + j, two(j), xn)
            u = AT["kv"]
            await_unit(u)
            pe.wait_ge(S["lru_ev"], 8)
            for k in range(C):
                pe.matmul(PS[5][:, 0:T], tile(u, k), xn[:, k, :], start=(k == 0), stop=(k == C - 1))
            for b in range(2):
                for k in range(C):
                    mm = pe.matmul(PS[5][:, T + b * P:T + (b + 1) * P], xn[:, k, b * P:(b + 1) * P],
                                   tile(u, C + k), start=(k == 0), stop=(k == C - 1))
            mm.then_inc(S["units_done"], 1)

            def values(l, i, bank):
                b, hf = i // 2, i % 2
                for k in range(C):
                    u = AT[f"cv{l}"] + k // 2
                    if i == 0:
                        await_unit(u)
                        pe.wait_ge(S["memn_ready"], 8 * l + k + 1)
                    at = D * (k % 2) + 512 * hf
                    mm = pe.matmul(PS[bank][:, :], memn[:, k, b * P:(b + 1) * P],
                                   ring[:, slot_of(u), at:at + 512], start=(k == 0), stop=(k == C - 1))
                    if i == 3 and k % 2:
                        mm.then_inc(S["units_done"], 1)
                    elif k == C - 1:
                        mm.then_inc(S["cv_mm"], 1)

            pe.wait_ge(S["qsq_ready"], 3)
            pe.matmul(PS[4][:, 0:T], tb("heads"), tsq[:, 0, 0:T], start=True, stop=True)\
                .then_inc(S["hstat_mm"], 1)
            pe.wait_ge(S["vk_ready"], 1)
            pe.matmul(PS[4][:, T:2 * T], tb("rot1"), qg[:, 4, :], start=True, stop=True)\
                .then_inc(S["rot_mm"], 1)
            for i in range(4):
                if i < 2:
                    pe.wait_ge(S["lgate_ready"], i + 1)
                else:
                    pe.wait_ge(S["cv_ready"], i - 1)
                values(0, i, i % 2)

            def memory_keys(a):
                l, j = a // 4, a % 4
                if a == 0:
                    pe.wait_ge(S["cv_ready"], 4)
                else:
                    pe.wait_ge(S["ck_raw"], a)
                if a in (5, 6):
                    key_scales(0, a - 5, 1)
                stationary(AT[f"ck{l}"] + j, two(0), memn, (S["memn_ready"], 8) if a == 4 else None)

            def key_scales(l, i, bank):
                pe.wait_ge(S["krec_ready"], l + 1)
                if i or l:
                    pe.wait_ge(S["kn_ready"], 2 * l + (i if l == 0 else 0))
                for h in range(2):
                    for b in range(2):
                        at = 8 * l + 4 * i + 2 * h + b
                        mm = pe.matmul(PS[bank][:, h * T + b * P:h * T + (b + 1) * P],
                                       ksum[:, at:at + 1].broadcast_to((P, P)), tb("ident"), start=True, stop=True)
                mm.then_inc(S["kb_mm"], 1)

            def key_sums(a):
                pe.wait_ge(S["cksq_ready"], a + 1)
                for b in range(2):
                    for c in range(2):
                        pe.matmul(PS[4 + a % 2][:, T + b:T + b + 1], tsq[:, a % 2, c * T + b * P:c * T + (b + 1) * P],
                                  tb("ones")[:, 0:1], start=(c == 0), stop=(c == 1))

            def score1(a, bank):
                pe.wait_ge(S["qn_ready"], 3)
                for b in range(2):
                    mm = pe.matmul(bank[:, b, :], qg[:, a % 4, b * P:(b + 1) * P], kz[:, a // 4, :],
                                   start=True, stop=True)
                return mm

            def output1(a, bank):
                for kb in range(2):
                    mm = pe.matmul(bank[:, 0, :], vt1[:, kb, :], pT[:, a % 2, kb, :], start=(kb == 0),
                                   stop=(kb == 1))
                return mm

            heads(0, 8, score1, output1, memory_keys, key_sums)
            pe.wait_ge(S["ck_raw"], 8)
            values(1, 0, 0)
            for g in range(2):
                pe.wait_ge(S["osq_ready"], g + 1)
                for c in range(4):
                    mm = pe.matmul(two(6)[:, g, :], tb("ones"), sq[:, 4 * g + c, :], start=(c == 0),
                                   stop=(c == 3))
                mm.then_inc(S["ostat_mm"], 1)
            key_scales(1, 0, 1)
            key_scales(1, 1, 3)
            pe.wait_ge(S["o_ready"], 8)
            for i, bank in ((1, 2), (2, 5), (3, 7)):
                values(1, i, bank)
            pe.wait_ge(S["cv_ready"], 6)
            pe.wait_ge(S["kn_ready"], 4)
            pe.wait_ge(S["mixed_ready"], 8)
            output_linear(AT["w_out"], xn, 1)

            for tk in range(2):
                for k in range(C):
                    pe.wait_ge(S["xn_ready"], 8 + k + 1)
                    if tk == 0 and k == 0:
                        pe.wait_ge(S["router_loaded"], 48)
                    mm = pe.matmul(PS[5][:, tk * E:(tk + 1) * E], xn[:, k, tk * P:(tk + 1) * P], wr[:, k, :],
                                   start=(k == 0), stop=(k == C - 1))
            mm.then_inc(S["rout_mm"], 1)
            for g in range(4):
                bank = PS[6 + g % 2]
                if g >= 2:
                    pe.wait_ge(S["tok_ready"], g - 1)
                for c in range(4):
                    mm = pe.transpose(bank[:, c * P:(c + 1) * P],
                                      xn[:, 4 * (g % 2) + c, (g // 2) * P:(g // 2 + 1) * P], tb("ident"))
                mm.then_inc(S["tok_mm"], 1)
            for c in range(C):
                mm = pe.matmul(PS[c // 2][:, (c % 2) * T:(c % 2 + 1) * T], tb("ident"), xT[:, c, :],
                               start=(c % 2 == 0), stop=False, skip_group_check=True)
            pe.wait_ge(S["mask_ready"], 1)
            cp = PS[5][:, 64:64 + 3 * E].rearrange("p (a e) -> p a e", a=3)
            pe.matmul(cp[:, 0, :], tb("before"), msk[:, 0, :], start=True, stop=True)
            for g, w in ((1, "before"), (2, "ones")):
                pe.matmul(cp[:, g, :], tb("ones"), msk[:, 0, :], start=True, stop=False)
                mm = pe.matmul(cp[:, g, :], tb(w), msk[:, 1, :], start=False, stop=True)
            mm.then_inc(S["cnt_mm"], 1)
            pe.wait_ge(S["lg_ready"], 3)
            for tk in range(2):
                mm = pe.transpose(PS[4][0:E, tk * P:(tk + 1) * P], G[:, tk, 0:E], tb("ident"))
            mm.then_inc(S["gt_mm"], 1)

            def select_T(n):
                pe.wait_ge(M["sel_ready"], n + 1)
                for tk in range(2):
                    mm = pe.matmul(PS[7][:, tk * P:(tk + 1) * P], selg[:, tk, :], tb("ident"), start=True,
                                   stop=True)
                mm.then_inc(M["selT_mm"], 1)

            def gather(n):
                pe.wait_ge(M["sel_ready"], n + 1)
                for c in range(C):
                    for tk in range(2):
                        mm = pe.matmul(PS[4 + c // 4][:, (c % 4) * WIDE:(c % 4 + 1) * WIDE],
                                       xtok[:, tk, c * P:(c + 1) * P], sel[:, tk, :], start=(tk == 0),
                                       stop=(tk == 1))
                mm.then_inc(M["xs_mm"], 1)

            def await_expert_unit(e, j):
                pe.wait_ge(landed[expert_slot(j)], e * 16 + 16 * expert_loads(j))

            def turn(n, w, kind):
                pe.wait_ge(M[("g_ready", "u_ready")[kind] + ROUND[w]], n + 1)
                for c in range(4):
                    mm = pe.transpose(PS[6 + kind][:, c * P:(c + 1) * P],
                                      (gA, uA)[kind][w][:, c * P:(c + 1) * P], tb("ident"))
                mm.then_inc(M[("tg_mm", "tu_mm")[kind] + ROUND[w]], 1)

            def narrow_pass(n, e):
                mm = None
                for kind in range(2):
                    for j in range(4 * kind, 4 * kind + 4):
                        await_expert_unit(e, j)
                        for kk in range(2):
                            k = 2 * (j % 4) + kk
                            for h in range(2):
                                mm = pe.matmul(PS[4 + kind][NARROW * h:NARROW * (h + 1), :],
                                               xs[:, k, NARROW * h:NARROW * (h + 1)],
                                               ring[:, expert_slot(j), D * kk + 512 * h:D * kk + 512 * (h + 1)],
                                               start=(k == 0), stop=(k == C - 1))
                                if j and kk == h == 0:
                                    mm.then_inc(S["units_done"], 1)
                    mm.then_inc(M[("g_mm", "u_mm")[kind]], 1)
                turn(n, 0, 0)
                pe.wait_ge(M["selT_ready"], n + 1)
                turn(n, 0, 1)
                gather(n + 1)
                pe.wait_ge(M["h_ready"], n + 1)
                for j in range(8, 12):
                    await_expert_unit(e, j)
                    for kk in range(2):
                        f = 2 * (j - 8) + kk
                        for h in range(2):
                            mm = pe.matmul(PS[6][NARROW * h:NARROW * (h + 1), :],
                                           hT[0][:, f % 4, NARROW * (f // 4):NARROW * (f // 4 + 1)],
                                           ring[:, expert_slot(j), D * kk + 512 * h:D * kk + 512 * (h + 1)],
                                           start=(f == 0), stop=(f == C - 1))
                            if kk == h == 0:
                                mm.then_inc(S["units_done"], 1)
                mm.then_inc(M["y_mm"], 1)
                pe.wait_ge(M["y_ready"], n + 1)
                for c in (0, 4, 1, 5, 2, 6, 3, 7):
                    rows = slice(NARROW * (c // 4), NARROW * (c // 4 + 1))
                    mm = pe.matmul(PS[c // 2][:, (c % 2) * T:(c % 2 + 1) * T],
                                   yS[rows, (c % 4) * P:(c % 4 + 1) * P], selgT[rows, :], start=False,
                                   stop=False, skip_group_check=True)
                    if c == 0:
                        mm.then_inc(S["units_done"], 1)
                mm.then_inc(M["scat_mm"], 1)
                select_T(n + 1)
                for name in ("g_mm2", "u_mm2", "tg_mm2", "tu_mm2"):
                    pe.sem_inc(M[name], 1)

            def wide_pass(n, e, frees):
                mm = None
                for w in range(2):
                    for kind in range(2):
                        if w:
                            pe.wait_ge(M[("g_ready", "u_ready")[kind]], n + 1)
                        for j in range(4 * kind, 4 * kind + 4):
                            if w == 0:
                                await_expert_unit(e, j)
                            for kk in range(2):
                                k = 2 * (j % 4) + kk
                                mm = pe.matmul(PS[4 + kind][:, :], xs[:, k, :],
                                               ring[:, expert_slot(j), D * kk + 512 * w:D * kk + 512 * (w + 1)],
                                               start=(k == 0), stop=(k == C - 1))
                                if frees and w and j and kk == 0:
                                    mm.then_inc(S["units_done"], 1)
                        mm.then_inc(M[("g_mm", "u_mm")[kind] + ROUND[w]], 1)
                    if w:
                        pe.wait_ge(M["h_ready"], n + 1)
                    turn(n, w, 0)
                    if w == 0:
                        pe.wait_ge(M["selT_ready"], n + 1)
                    turn(n, w, 1)
                gather(n + 1)
                pe.wait_ge(M["h_ready2"], n + 1)
                for j in range(8, 12):
                    await_expert_unit(e, j)
                    for kk in range(2):
                        f = 2 * (j - 8) + kk
                        for h in range(2):
                            mm = pe.matmul(PS[6 + h][:, :], hT[f // 4][:, f % 4, :],
                                           ring[:, expert_slot(j), D * kk + 512 * h:D * kk + 512 * (h + 1)],
                                           start=(f == 0), stop=(f == C - 1))
                            if frees and kk == h == 0:
                                mm.then_inc(S["units_done"], 1)
                mm.then_inc(M["y_mm"], 1)
                pe.wait_ge(M["y_ready"], n + 1)
                for c in range(C):
                    mm = pe.matmul(PS[c // 2][:, (c % 2) * T:(c % 2 + 1) * T], yS[:, c * P:(c + 1) * P],
                                   selgT[:, :], start=False, stop=False, skip_group_check=True)
                    if frees and c == 0:
                        mm.then_inc(S["units_done"], 1)
                mm.then_inc(M["scat_mm"], 1)
                select_T(n + 1)

            def tokens_of(e):
                return pe.value_load(load[0:1, bass.ds(e, 1)], min_val=0, max_val=T)

            pe.wait_ge(S["flag_ready"], 1)
            pe.wait_ge(S["tok_ready"], 4)
            pe.wait_ge(S["gt_ready"], 1)
            most = pe.value_load(flag[0:1, 0:1], min_val=0, max_val=T)
            select_T(0)
            gather(0)
            with pe.If(most < WIDE + 1):
                with pe.Fori(0, E) as e:
                    pe.wait_ge(M["xs_ready"], e + 1)
                    with pe.If(tokens_of(e) < NARROW + 1):
                        narrow_pass(e, e)
                    with pe.Else():
                        wide_pass(e, e, True)
                    pe.nop()
            with pe.Else():
                with pe.Fori(0, E) as e:
                    for b in range(BLOCKS):
                        pe.wait_ge(M["xs_ready"], e * BLOCKS + b + 1)
                        wide_pass(e * BLOCKS + b, e, b == BLOCKS - 1)
            pe.wait_ge(S["bd_loaded"], 16)
            for c in range(C):
                mm = pe.matmul(PS[c // 2][:, (c % 2) * T:(c % 2 + 1) * T], bd[:, c * P:(c + 1) * P], GT[:, :],
                               start=False, stop=True, skip_group_check=True)
                if c % 2:
                    mm.then_inc(S["moe_mm"], 1)

            for n in (2, 3):
                for j in range(4):
                    stat_pair(n, j)

            for j in range(4):
                stationary(AT["iq"] + j, two(j), xn, (S["xn_ready"], 24) if j == 0 else None)
            u = AT["ikiw"]
            await_unit(u)
            for k in range(C):
                pe.matmul(PS[5][:, 0:T], tile(u, k), xn[:, k, :], start=(k == 0), stop=(k == C - 1))
            for b in range(2):
                for k in range(C):
                    mm = pe.matmul(PS[5][:, T + 16 * b:T + 16 * b + 16], xn[:, k, b * P:(b + 1) * P],
                                   ring[:, slot_of(u), C * P + 16 * k:C * P + 16 * k + 16],
                                   start=(k == 0), stop=(k == C - 1))
            mm.then_inc(S["units_done"], 1)
            for j in range(5):
                pe.wait_ge(S["iq_ready"], j + 1)
                if j >= 2:
                    pe.wait_ge(S["iqrot_read"], j - 1)
                if j < 4:
                    pe.matmul(two(6 + j % 2), tb("rot3"), iqr[:, 2 * j:2 * j + 2, :], start=True, stop=True)\
                        .then_inc(S["iqrot_mm"], 1)
                else:
                    pe.matmul(PS[6][:, 0:T], tb("rot3"), tv[:, 0, 0:T], start=True, stop=True)\
                        .then_inc(S["iqrot_mm"], 1)
            def index_scores(h):
                pe.wait_ge(S["iqn_ready"], 5)
                if h >= 2:
                    pe.wait_ge(S["relu_ready"], h - 1)
                for b in range(2):
                    keys = (b + 1) * P
                    mm = pe.matmul(two(h % 2)[:, b, 0:keys], iqr[:, h // 2, b * P:(b + 1) * P],
                                   iz[:, h % 2, 0:keys], start=True, stop=True)
                mm.then_inc(S["iscore_mm"], 1)

            for j in range(4):
                if j >= 2:
                    pe.wait_ge(S["dqk_ready"], j - 1)
                stationary((AT["dq"] + j), two(2 + j % 2), xn)
                for h in range(4 * j, 4 * j + 4):
                    index_scores(h)
                pe.wait_ge(S["dsq_ready"], j + 1)
                if j:
                    pe.wait_ge(S["dqn_ready"], j)
                pe.matmul(PS[4][:, :], tb("ones"), tsq[:, j % 2, :], start=True, stop=True)\
                    .then_inc(S["dstat_mm"], 1)
                pe.wait_ge(S["dqk_ready"], j + 1)
                pe.matmul(two(5), tb("rot2"), dqk[:, 2 * j:2 * j + 2, :], start=True, stop=True)\
                    .then_inc(S["drot_mm"], 1)
            pe.wait_ge(S["relu_ready"], 16)
            for j in range(2):
                stationary(AT["u"] + j, two(j), xn)
            for w in range(2):
                u = AT["dv"] + w
                await_unit(u)
                for kk in range(4):
                    for b in range(2):
                        k = 4 * w + kk
                        mm = pe.matmul(PS[6 + b][:, :], xn[:, k, b * P:(b + 1) * P],
                                       ring[:, slot_of(u), 512 * kk:512 * kk + 512],
                                       start=(k == 0), stop=(k == C - 1))
                mm.then_inc(S["units_done"], 1)
            u = AT["pool"]
            await_unit(u)
            pe.wait_ge(S["pooled_ready"], 4)
            for g in range(4):
                mm = pe.matmul(two(g // 2)[:, g % 2, :], tile(u, g), w1[:, g, 0:T], start=True, stop=True)
            mm.then_inc(S["units_done"], 1)

            def score2(a, bank):
                pe.wait_ge(S["dqn_ready"], 4)
                h = a - 8
                for b in range(2):
                    mm = pe.matmul(bank[:, b, :], dqk[:, h, b * P:(b + 1) * P], dqk[:, 4 + h, :],
                                   start=True, stop=True)
                return mm

            def output2(a, bank):
                h = a - 8
                for kb in range(2):
                    mm = pe.matmul(bank[:, 0, :], dv[:, kb, h * P:(h + 1) * P], pT[:, a % 2, kb, :],
                                   start=(kb == 0), stop=(kb == 1))
                return mm

            pe.wait_ge(S["dv_ready"], 2)
            heads(8, 4, score2, output2)
            pe.wait_ge(S["pool_mix"], 4)
            pe.wait_ge(S["o_ready"], 12)
            output_linear(AT["ab_out"], mix, 4)

            def cross(l):
                cq, c_o = AT[f"cq{l}"], AT[f"co{l}"]
                for j in range(4):
                    if j >= 2:
                        pe.wait_ge(S["cq_raw"], 4 * l + j - 1)
                    stationary(cq + j, two(2 + j % 2), xn, (S["xn_ready"], 8 * (4 + 3 * l)) if j == 0 else None)
                    if j:
                        head_sum(4 * l + j - 1)
                head_sum(4 * l + 3)
                pe.wait_ge(S["kv_back"], 32 * (l + 1))

                def score(a, bank):
                    h = (a - 12) % 4
                    pe.wait_ge(S["cq_raw"], 4 * l + 4)
                    for b in range(2):
                        for c in range(2):
                            mm = pe.matmul(bank[:, b, :], cqn[l][:, 2 * h + c, b * P:(b + 1) * P],
                                           ckn[l][:, 2 * h + c, :], start=(c == 0), stop=(c == 1))
                    return mm

                def output(a, bank):
                    h = (a - 12) % 4
                    for c in range(2):
                        for kb in range(2):
                            mm = pe.matmul(bank[:, c, :], cvt[l][:, kb, 256 * h + c * P:256 * h + (c + 1) * P],
                                           pT[:, a % 2, kb, :], start=(kb == 0), stop=(kb == 1))
                    return mm

                heads(12 + 4 * l, 4, score, output)
                pe.wait_ge(S["o_ready"], 16 + 4 * l)
                output_linear(c_o, co[l], 5 + 3 * l)

            def head_sum(p):
                pe.wait_ge(S["cqsq_ready"], p + 1)
                for b in range(2):
                    at = T + 2 * (p % 4) + b
                    for c in range(2):
                        mm = pe.matmul(PS[5][:, at:at + 1], tsq[:, p % 2, c * T + b * P:c * T + (b + 1) * P],
                                       tb("ones")[:, 0:1], start=(c == 0), stop=(c == 1))
                mm.then_inc(S["cqstat_mm"], 1)

            def ffn(l):
                first, n = AT[f"ffn{l}"], 8 * (5 + 3 * l)
                at = [first]
                for g in range(NG):
                    for kind in range(2):
                        bank = 4 + 2 * (g % 2) + kind
                        if g >= 2:
                            pe.wait_ge(S["f_h"], NG * l + g - 1)
                        stationary(at[0], two(bank), xn, (S["xn_ready"], n) if g == kind == 0 else None)
                        at[0] += 1
                    if g:
                        down(l, g - 1, at)
                down(l, NG - 1, at)
                if l == 0:
                    for j in range(4):
                        stat_pair(6, j)

            def down(l, g, at):
                u = at[0]
                at[0] += 1
                await_unit(u)
                pe.wait_ge(S["f_h"], NG * l + g + 1)
                for m in range(C):
                    for kk in range(2):
                        mm = pe.matmul(PS[m // 2][:, (m % 2) * T:(m % 2 + 1) * T], tile(u, kk * C + m),
                                       fh[g % 2][:, kk, :], start=(g == 0 and kk == 0 and m % 2 == 0),
                                       stop=(g == NG - 1 and kk == 1), skip_group_check=True)
                mm.then_inc(S["units_done"], 1)

            cross(0)
            ffn(0)
            for j in range(8):
                if j >= 4:
                    pe.wait_ge(S["hp_ready"], j - 3)
                stationary(AT["conv_in"] + j, two(j % 4), xn, (S["xn_ready"], 48) if j == 0 else None)
            for i, c in enumerate(ON_PE):
                pe.wait_ge(S["hp_ready"], c + 1)
                for t in range(TAPS):
                    pe.wait_ge(S["diag_ready"], i * TAPS + t + 1)
                    pe.matmul(PS[4 + i][:, 0:T], diag[:, (i * TAPS + t) % NDIAG, :],
                              hp[:, c, t:t + T], start=(t == 0), stop=(t == TAPS - 1))\
                        .then_inc(S["dwc_mm"], 1)
            for i, c in enumerate((0, 1, 2, 3) + ON_PE + (4, 5)):
                if c in ON_PE:
                    pe.wait_ge(S["hc_pe"], ON_PE.index(c) + 1)
                else:
                    pe.wait_ge(S["hc_dve"], c + 1)
                mm = pe.matmul(PS[0][:, 0:T], tb("ones"), hc[:, c, :], start=(i == 0), stop=(i == C - 1))
            mm.then_inc(S["lnsum_mm"], 1)
            for j in range(4):
                pe.wait_ge(S["lnsq_ready"], j + 1)
                for c in (2 * j, 2 * j + 1):
                    mm = pe.matmul(PS[1][:, 0:T], tb("ones"), sq[:, c, :], start=(c == 0), stop=(c == C - 1))
            mm.then_inc(S["lnvar_mm"], 1)
            output_linear(AT["conv_out"], yc, 7, (S["yc_ready"], 0))
            cross(1)
            ffn(1)
            assert AT["ffn1"] + 3 * NG == N_UNITS

        @block.scalar
        def _(act):
            chain = Chain(act, S["act_chain"])

            def f(out_, in_, fn, **kw):
                return act.activation(out_, in_, fn, **kw)

            def squares(n, j, sem_=None, value=None, src=None):
                if n == 0:
                    act.wait_ge(S["x_loaded"], 48)
                elif n == 3:
                    act.wait_ge(S["xn_ready"], 16 + 2 * j + 2)
                elif n == 2:
                    act.wait_ge(S["xmoe_ready"], j + 1)
                else:
                    act.wait_ge(S["res_ready"], 4 * RES[n] + j + 1)
                f(sq[:, 2 * j:2 * j + 2, :], xT[:, 2 * j:2 * j + 2, :], ACT.Square).then_inc(S["sq_ready"], 1)

            def deviation(n, eps):
                act.wait_ge(S["stat_mm"], 2 * n + 1)
                f(nst[:, :], PS[stat_bank(n)][:, 0:2], ACT.Sqrt, scale=1.0 / D, bias=V(eps)).then_inc(S["std_ready"], 1)

            def norm(n, eps="eps6"):
                for j in range(4):
                    squares(n, j)
                deviation(n, eps)

            def heads(first, count, scale, src, evacuate, fill=None, fill_sum=None):
                def exps(a):
                    act.wait_ge(S["nmax_ready"], a + 1)
                    if a >= 2:
                        act.wait_ge(S["pT_mm"], a - 1)
                        act.wait_ge(S["probs_ready"], a - 1)
                    for b in range(2):
                        at = 2 * (a % 4) + b
                        e_ = f(prob[:, a % 2, b, :], src(a)[:, b, :], ACT.Exp,
                               scale=rq[:, at:at + 1] if scale is rq else scale,
                               bias=small[:, 2 * (a % 2) + b:2 * (a % 2) + b + 1],
                               accum_out=small[:, 4 + 2 * (a % 2) + b:5 + 2 * (a % 2) + b])
                    e_.then_inc(S["exp_done"], 1)

                exps(first)
                for a in range(first, first + count):
                    if a + 1 < first + count:
                        exps(a + 1)
                    if fill:
                        fill(a)
                    act.wait_ge(S["pT_mm"], a + 1)
                    if a >= 2:
                        act.wait_ge(S["o_mm"], a - 1)
                    f(pT[:, a % 2, :, :], two(6 + a % 2), ACT.Copy).then_inc(S["pT_ready"], 1)
                    act.wait_ge(S["o_mm"], a + 1)
                    if fill_sum:
                        fill_sum(a)
                    evacuate(a, two(4 + a % 2)).then_inc(S["o_ready"], 1)

            norm(0, "eps5")
            act.wait_ge(S["pads_ready"], 3)
            act.wait_ge(S["lam_exp"], 1)
            chain.mark(f(small[:, 16:24], small[:, 16:24], ACT.Exp))
            act.wait_ge(S["mem_loaded"], 16)
            for j in range(4):
                f(kst[0][:, 2 * j:2 * j + 2, :], memT[:, 2 * j:2 * j + 2, :], ACT.Square).then_inc(S["msq_ready"], 1)
            for j in range(2):
                act.wait_ge(S["units_done"], j + 1)
                f(lxp[:, 2 * j:2 * j + 2, 2:2 + T], two(j), ACT.Copy).then_inc(S["lx_ready"], 1)
            act.wait_ge(S["mstat_mm"], 1)
            f(rmem, PS[7][:, 0:T], ACT.Sqrt, scale=1.0 / D, bias=V("eps6")).then_inc(S["mstd_ready"], 1)
            for j in range(2):
                act.wait_ge(S["units_done"], AT["q"] + j + 1)
                f(tsq[:, j, :], PS[2 + j][:, :], ACT.Square).then_inc(S["qsq_ready"], 1)
                f(qg[:, 2 * j:2 * j + 2, :], two(2 + j), ACT.Identity, scale=V("gq"))\
                    .then_inc(S["qraw_ready"], 1)
            for n in range(8):
                d, kind, j = n // 4, (n // 2) % 2, n % 2
                if n < 7:
                    act.wait_ge(S["lru_mm"], n + 1)
                else:
                    act.wait_ge(S["units_done"], AT["lru_w"] + 1)
                for c in range(2):
                    ch = 2 * j + c
                    last = f((ii if kind else rr)[:, 4 * d + ch, :], two(GATE_BANKS[n])[:, c, :], ACT.Sigmoid,
                             bias=V("lru_b", 8 * kind + 4 * d + ch))
                last.then_inc(S["lru_ev"], 1)
            for j in range(2):
                act.wait_ge(S["hstat_mm"], j + 1)
                f(hstd[j], PS[6 + j][:, :], ACT.Sqrt, scale=1.0 / 64, bias=V("eps6")).then_inc(S["hstd_ready"], 1)
            for j in range(2):
                act.wait_ge(S["units_done"], AT["lru_gate"] + j + 1)
                f(lgate[:, 2 * j:2 * j + 2, :], two(j), ACT.Copy).then_inc(S["lgate_ready"], 1)
            act.wait_ge(S["units_done"], AT["kv"] + 1)
            f(tsq[:, 0, 0:T], PS[5][:, 0:T], ACT.Square).then_inc(S["qsq_ready"], 1)
            f(vt1[:, :, :], PS[5][:, T:2 * T].rearrange("p (a b) -> p a b", a=2), ACT.Copy)
            f(qg[:, 4, :], PS[5][:, 0:T], ACT.Identity, scale=V("gk")).then_inc(S["vk_ready"], 1)
            act.wait_ge(S["rot_mm"], 3)
            f(hstd[2], PS[4][:, 0:T], ACT.Sqrt, scale=1.0 / 64, bias=V("eps6")).then_inc(S["hstd_ready"], 1)
            act.wait_ge(S["r_ready"], 1)
            act.wait_ge(S["lru_ev"], 8)
            for n in range(8):
                f(th[:, n, :], rr[:, n, :], ACT.Tanh, scale=small[:, 24 + n:25 + n])
            chain.mark(f(gtmp[:, :, :], lgate[:, :, :], ACT.Square))
            chain.settle()
            for n in range(8):
                last = f(rr[:, n, :], rr[:, n, :], ACT.Exp, scale=small[:, 8 + n:9 + n])
            last.then_inc(S["lgsq_ready"], 1)

            def copy_values(l, i, bank):
                if i < 3:
                    act.wait_ge(S["cv_mm"], 3 * l + i + 1)
                else:
                    act.wait_ge(S["units_done"], AT[f"cv{l}"] + 4)
                if l and i == 0:
                    act.wait_ge(S["v_spilled"], 16)
                f(vst[:, i // 2, 512 * (i % 2):512 * (i % 2) + 512], PS[bank][:, :], ACT.Copy)\
                    .then_inc(S["cv_ready"], 1)

            def key_chunks(a):
                l, j = a // 4, a % 4
                act.wait_ge(S["units_done"], AT[f"ck{l}"] + j + 1)
                if a >= 2:
                    act.wait_ge(S["o_mm"], a - 1)
                if a == 4:
                    act.wait_ge(S["memn_ready"], 16)
                f(tsq[:, a % 2, :], PS[0][:, :], ACT.Square).then_inc(S["cksq_ready"], 1)
                for c in range(2):
                    last = f(kst[l][:, 2 * j + c, :], two(0)[:, c, :], ACT.Identity, scale=V(f"ckg{l}", c))
                last.then_inc(S["ck_raw"], 1)

            def key_deviations(a):
                chain.mark(f(ksum[:, 2 * a:2 * a + 2], PS[4 + a % 2][:, T:T + 2], ACT.Copy))
                if a % 4 == 3:
                    chain.settle()
                    part = ksum[:, 2 * a - 6:2 * a + 2]
                    f(part, part, ACT.Sqrt, scale=1.0 / T, bias=V("eps6")).then_inc(S["kstd_ready"], 1)

            for i in range(4):
                copy_values(0, i, i % 2)
            act.wait_ge(S["m_ready"], 1)
            f(th[:, :, :], th[:, :, :], ACT.Sqrt).then_inc(S["mult_ready"], 1)
            act.wait_ge(S["ginner_ready"], 1)
            f(gtmp[:, :, :], gtmp[:, :, :], ACT.Sigmoid, scale=2.0 * float(np.sqrt(2.0 / np.pi)))\
                .then_inc(S["gsig_ready"], 1)
            heads(0, 8, 0.125, lambda a: two(2 + a % 2),
                  lambda a, bank: f(at1[64 * (a // 4):64 * (a // 4) + 64, a % 4, :],
                                    bank[64 * (a // 4):64 * (a // 4) + 64, 0, :], ACT.Copy),
                  key_chunks, key_deviations)
            act.wait_ge(S["o_ready"], 8)
            f(sq[:, 0:4, :], at1[:, :, :], ACT.Square).then_inc(S["osq_ready"], 1)
            act.wait_ge(S["lru_ready"], 1)
            f(sq[:, 4:8, :], xc[:, :, :], ACT.Square).then_inc(S["osq_ready"], 1)
            act.wait_ge(S["ostat_mm"], 2)
            f(std[:, :], PS[6][:, :], ACT.Sqrt, scale=1.0 / 512, bias=V("eps5")).then_inc(S["ostd_ready"], 1)
            for i, bank in enumerate((0, 2, 5, 7)):
                copy_values(1, i, bank)
            norm(1, "eps5")

            for g in range(4):
                act.wait_ge(S["tok_mm"], g + 1)
                f(xtok[:, g // 2, 512 * (g % 2):512 * (g % 2) + 512], PS[6 + g % 2][:, :], ACT.Copy)\
                    .then_inc(S["tok_ready"], 1)
            act.wait_ge(S["lg_ready"], 2)
            for tk in range(2):
                last = f(exr[:, tk, :], lg[:, tk, 0:E], ACT.Exp, bias=gs[:, tk:tk + 1])
            last.then_inc(S["gex_ready"], 1)
            act.wait_ge(S["gt_mm"], 1)
            f(GT[:, :], PS[4][0:E, 0:T], ACT.Copy).then_inc(S["gt_ready"], 1)

            def copy_xs(n):
                act.wait_ge(M["xs_mm"], n + 1)
                for i in range(2):
                    last = f(xs[:, 4 * i:4 * i + 4, :], PS[4 + i][:, :].rearrange("p (c n) -> p c n", c=4),
                             ACT.Copy)
                last.then_inc(M["xs_ready"], 1)

            def selected(n):
                act.wait_ge(M["selT_mm"], n + 1)
                f(selgT, PS[7][:, 0:T], ACT.Copy).then_inc(M["selT_ready"], 1)

            def halves(n, w):
                r_ = ROUND[w]
                for kind in range(2):
                    name, dst = (("g", gA), ("u", uA))[kind]
                    act.wait_ge(M[f"{name}_mm{r_}"], n + 1)
                    f(dst[w], PS[4 + kind][:, :], ACT.Copy).then_inc(M[f"{name}_ready{r_}"], 1)
                act.wait_ge(M["sig_in" + r_], n + 1)
                f(sg, ge, ACT.Sigmoid, scale=1.702).then_inc(M["sig_ready" + r_], 1)

            def act_pass(n, wide):
                selected(n)
                halves(n, 0)
                if wide:
                    halves(n, 1)
                copy_xs(n + 1)
                act.wait_ge(M["y_mm"], n + 1)
                if wide:
                    f(yS[:, 0:512], PS[6][:, :], ACT.Copy)
                    f(yS[:, 512:D], PS[7][:, :], ACT.Copy).then_inc(M["y_ready"], 1)
                else:
                    f(yS[:, 0:512], PS[6][:, :], ACT.Copy).then_inc(M["y_ready"], 1)
                    for name in ("g_ready2", "u_ready2", "sig_ready2"):
                        act.sem_inc(M[name], 1)

            act.wait_ge(S["flag_ready"], 1)
            most = act.value_load(flag[0:1, 0:1], min_val=0, max_val=T)
            copy_xs(0)
            with act.If(most < WIDE + 1):
                with act.Fori(0, E) as e:
                    with act.If(act.value_load(load[0:1, bass.ds(e, 1)], min_val=0, max_val=T) < NARROW + 1):
                        act_pass(e, False)
                    with act.Else():
                        act_pass(e, True)
                    act.nop()
            with act.Else():
                with act.Fori(0, E) as e:
                    for b in range(BLOCKS):
                        act_pass(e * BLOCKS + b, True)
            for j in range(4):
                act.wait_ge(S["moe_mm"], j + 1)
                f(xT[:, 2 * j:2 * j + 2, :], two(j), ACT.Copy).then_inc(S["xmoe_ready"], 1)
            norm(2, "eps5")
            norm(3)

            act.wait_ge(S["pads_ready"], 8)
            for j in range(4):
                act.wait_ge(S["units_done"], AT["iq"] + j + 1)
                f(iqr[:, 2 * j:2 * j + 2, :], two(j), ACT.Copy).then_inc(S["iq_ready"], 1)
            act.wait_ge(S["units_done"], AT["ikiw"] + 1)
            f(tv[:, 0, 0:T], PS[5][:, 0:T], ACT.Copy).then_inc(S["iq_ready"], 1)
            f(iw[:, :, :], PS[5][:, T:T + 32].rearrange("p (a b) -> p a b", a=2), ACT.Copy, scale=1.0 / 32)\
                .then_inc(S["iw_ready"], 1)
            def relu(h):
                act.wait_ge(S["iscore_mm"], h + 1)
                if h >= 2:
                    act.wait_ge(S["relu_used"], h - 1)
                f(rl[h % 2][:, 0, 0:P], two(h % 2)[:, 0, 0:P], ACT.Relu)
                f(rl[h % 2][:, 1, :], two(h % 2)[:, 1, :], ACT.Relu).then_inc(S["relu_ready"], 1)

            for j in range(4):
                act.wait_ge(S["units_done"], AT["dq"] + j + 1)
                if j >= 2:
                    act.wait_ge(S["dstat_mm"], j - 1)
                if j == 0:
                    act.wait_ge(S["iqn_ready"], 4)
                f(tsq[:, j % 2, :], PS[2 + j % 2][:, :], ACT.Square).then_inc(S["dsq_ready"], 1)
                f(dqk[:, 2 * j:2 * j + 2, :], two(2 + j % 2), ACT.Identity, scale=V("aq" if j < 2 else "ak"))\
                    .then_inc(S["dqk_ready"], 1)
                for h in range(4 * j, 4 * j + 4):
                    relu(h)
                act.wait_ge(S["dstat_mm"], j + 1)
                if j:
                    act.wait_ge(S["dqn_ready"], j)
                f(std[:, :], PS[4][:, :], ACT.Sqrt, scale=1.0 / P, bias=V("eps6")).then_inc(S["dstd_ready"], 1)
            for j in range(2):
                act.wait_ge(S["units_done"], AT["u"] + j + 1)
                f(up[:, 2 * j:2 * j + 2, 16:272], two(j), ACT.Copy).then_inc(S["u_ready"], 1)
            act.wait_ge(S["units_done"], AT["dv"] + 2)
            for b in range(2):
                f(dv[:, b, :], PS[6 + b][:, :], ACT.Copy).then_inc(S["dv_ready"], 1)
            act.wait_ge(S["relu_used"], 16)
            act.wait_ge(S["units_done"], AT["pool"] + 1)
            for g in range(4):
                f(mix[:, 4 + g, :], two(g // 2)[:, g % 2, :], ACT.Identity, scale=V("pool_scale", g))\
                    .then_inc(S["pool_mix"], 1)
            heads(8, 4, 1.0, lambda a: tv[:, a % 2, :].rearrange("p (b t) -> p b t", b=2),
                  lambda a, bank: f(mix[:, a - 8, :], bank[:, 0, :], ACT.Copy))

            def cross(l):
                for j in range(4):
                    p = 4 * l + j
                    act.wait_ge(S["units_done"], AT[f"cq{l}"] + j + 1)
                    if p >= 2:
                        act.wait_ge(S["cqstat_mm"], p - 1)
                    f(tsq[:, p % 2, :], PS[2 + j % 2][:, :], ACT.Square).then_inc(S["cqsq_ready"], 1)
                    for c in range(2):
                        last = f(cqn[l][:, 2 * j + c, :], two(2 + j % 2)[:, c, :], ACT.Identity,
                                 scale=V(f"cqg{l}", c))
                    last.then_inc(S["cq_raw"], 1)
                act.wait_ge(S["cqstat_mm"], 4 * l + 4)
                f(rq[:, :], PS[5][:, T:T + 8], ACT.Sqrt, scale=1.0 / T, bias=V("eps6")).then_inc(S["cqstd_ready"], 1)
                heads(12 + 4 * l, 4, rq, lambda a: two(2 + a % 2),
                      lambda a, bank: f(co[l][:, 2 * ((a - 12) % 4):2 * ((a - 12) % 4) + 2, :], bank, ACT.Copy))

            def ffn(l):
                for g in range(NG):
                    act.wait_ge(S["units_done"], AT[f"ffn{l}"] + ffn_gate_unit(g) + 1)
                    f(fs[g % 2][:, :, :], two(4 + 2 * (g % 2)), ACT.Sigmoid).then_inc(S["f_sig"], 1)

            norm(4)
            cross(0)
            norm(5)
            ffn(0)
            norm(6)
            for j in range(8):
                act.wait_ge(S["units_done"], AT["conv_in"] + j + 1)
                if j >= 2:
                    act.wait_ge(S["hp_ready"], j - 1)
                f(csg[:, j % 2, :], two(j % 4)[:, 1, :], ACT.Sigmoid, bias=V("cin_b", 8 + j))\
                    .then_inc(S["conv_sig"], 1)
            for i, c in enumerate(ON_PE):
                for t in range(TAPS):
                    n = i * TAPS + t
                    if n >= NDIAG:
                        act.wait_ge(S["dwc_mm"], n - NDIAG + 1)
                    f(diag[:, n % NDIAG, :], tb("ident"), ACT.Copy, scale=V("dw", c * TAPS + t))\
                        .then_inc(S["diag_ready"], 1)
                act.wait_ge(S["dwc_mm"], (i + 1) * TAPS)
                f(hc[:, c, :], PS[4 + i][:, 0:T], ACT.Identity, bias=V("dw_b", c))\
                    .then_inc(S["hc_pe"], 1)
            for j in range(4):
                act.wait_ge(S["lnd_ready"], j + 1)
                f(sq[:, 2 * j:2 * j + 2, :], hc[:, 2 * j:2 * j + 2, :], ACT.Square).then_inc(S["lnsq_ready"], 1)
            act.wait_ge(S["lnvar_mm"], 1)
            f(std[:, 0:T], PS[1][:, 0:T], ACT.Sqrt, scale=1.0 / D, bias=V("eps6")).then_inc(S["lnstd_ready"], 1)
            for c in range(C):
                act.wait_ge(S["lnz_ready"], c + 1)
                f(sq[:, c, :], hc[:, c, :], ACT.Sigmoid, bias=V("ln_b", c)).then_inc(S["lnsig_ready"], 1)
            norm(7)
            cross(1)
            norm(8)
            ffn(1)

        @block.vector
        def _(dve):
            chain = Chain(dve, S["dve_chain"])
            link, mark, settle = chain.link, chain.mark, chain.settle
            tt, ts, stt = dve.tensor_tensor, dve.tensor_scalar, dve.scalar_tensor_tensor

            def norm(n, gain, dst):
                dve.wait_ge(S["std_ready"], 2 * n + 1)
                dve.reciprocal(nst[:, :], nst[:, :]).then_inc(S["std_ready"], 1)
                dve.wait_ge(S["stat_mm"], 2 * n + 2)
                for k in range(C):
                    stt(dst[:, k, :], xT[:, k, :], V(gain, k), PS[stat_bank(n)][:, 0:T], ALU.mult, ALU.mult)\
                        .then_inc(S["xn_ready"], 1)

            def residual(first):
                for j in range(4):
                    dve.wait_ge(S["units_done"], first + j + 1)
                    tt(xT[:, 2 * j:2 * j + 2, :], two(j), xT[:, 2 * j:2 * j + 2, :], ALU.add)\
                        .then_inc(S["res_ready"], 1)

            def heads(first, count, scale, between=None, sparse=False):
                def maxima(a):
                    dve.wait_ge(S["score_mm"], a + 1)
                    bank = two(2 + a % 2)
                    if a - first >= 2:
                        dve.wait_ge(S["exp_done"], a - 1)
                    if a:
                        dve.wait_ge(S["nmax_ready"], a)
                    if sparse:
                        src = tv[:, a % 2, :].rearrange("p (b t) -> p b t", b=2)
                        link(stt(src, bank, scale, pen[:, :, :], ALU.mult, ALU.add))
                        bank = src
                    link(dve.tensor_reduce(mx[:, :], bank, AX, ALU.max))
                    nmax = small[:, 2 * (a % 2):2 * (a % 2) + 2]
                    if scale is rq:
                        at = 2 * (a % 4)
                        stt(nmax, mx[:, :], -1.0, rq[:, at:at + 2], ALU.mult, ALU.mult).then_inc(S["nmax_ready"], 1)
                    else:
                        ts(nmax, mx[:, :], -1.0 if sparse else -scale, None, ALU.mult).then_inc(S["nmax_ready"], 1)

                def divide(a):
                    dve.wait_ge(S["exp_done"], a + 1)
                    if a:
                        dve.wait_ge(S["probs_ready"], a)
                    o = 4 + 2 * (a % 2)
                    link(dve.reciprocal(rs[:, :], small[:, o:o + 2]))
                    tt(prob[:, a % 2, :, :], prob[:, a % 2, :, :], along(rs[:, :], T), ALU.mult)\
                        .then_inc(S["probs_ready"], 1)

                maxima(first)
                for a in range(first, first + count):
                    if a + 1 < first + count:
                        maxima(a + 1)
                    divide(a)
                    if between:
                        between(a)

            dve.wait_ge(S["x_loaded"], 48)
            ea, rate_n, rate_p = small[:, 16:24], small[:, 8:16], small[:, 24:32]
            link(ts(rate_n, V("lam", 0, 8), -1.0, None, ALU.mult))
            ts(ea, V("lam", 0, 8), 0.0, None, ALU.max)
            link(ts(rate_p, rate_n, 0.0, None, ALU.max))
            link(tt(ea, ea, rate_p, ALU.add))
            ts(ea, ea, -1.0, None, ALU.mult).then_inc(S["lam_exp"], 1)
            norm(0, "norm1", xn)
            dve.wait_ge(S["act_chain"], 1)
            z, z2, ser = lam3[:, 0:8], lam3[:, 8:16], lam3[:, 16:24]
            link(ts(z, ea, 2.0, None, ALU.add))
            link(dve.reciprocal(z, z))
            link(tt(z, z, ea, ALU.mult))
            link(tt(z2, z, z, ALU.mult))
            link(ts(ser, z2, 1.0 / 19, 1.0 / 17, ALU.mult, ALU.add))
            for k in range(15, 0, -2):
                link(tt(ser, ser, z2, ALU.mult))
                link(ts(ser, ser, 1.0 / k, None, ALU.add))
            link(stt(ser, ser, 2.0, z, ALU.mult, ALU.mult))
            link(tt(ser, ser, rate_p, ALU.add))
            ts(rate_n, ser, -8.0, None, ALU.mult)
            ts(rate_p, ser, 8.0, None, ALU.mult).then_inc(S["r_ready"], 1)
            dve.wait_ge(S["pads_ready"], 3)
            for c in range(4):
                dve.wait_ge(S["lx_ready"], c // 2 + 1)
                link(ts(xc[:, c, :], lxp[:, c, 0:T], V("conv_w", 4 * c), V("conv_b", c), ALU.mult, ALU.add))
                for t in range(1, 4):
                    o = stt(xc[:, c, :], lxp[:, c, t:t + T], V("conv_w", 4 * c + t), xc[:, c, :],
                            ALU.mult, ALU.add)
                    if t < 3:
                        link(o)
                o.then_inc(S["xc_ready"], 1)

            def rotated(src, rot, n, dst, cos, sin):
                link(tt(tv[:, 0, 0:n * T].rearrange("p (a t) -> p a t", a=n), src, over(tb(cos), n), ALU.mult))
                link(tt(tv[:, 1, 0:n * T].rearrange("p (a t) -> p a t", a=n), rot, over(tb(sin), n), ALU.mult))
                return tt(dst, tv[:, 0, 0:n * T].rearrange("p (a t) -> p a t", a=n),
                          tv[:, 1, 0:n * T].rearrange("p (a t) -> p a t", a=n), ALU.add)

            dve.wait_ge(S["mstd_ready"], 1)
            link(dve.reciprocal(rmem, rmem))
            dve.wait_ge(S["consts_loaded"], 32)

            def memory(l):
                for k in range(C):
                    stt(memn[:, k, :], memT[:, k, :], V(f"mem{l}", k), rmem, ALU.mult, ALU.mult)\
                        .then_inc(S["memn_ready"], 1)

            dve.wait_ge(S["mem_loaded"], 16)
            memory(0)
            for j in range(2):
                dve.wait_ge(S["rot_mm"], j + 1)
                dve.wait_ge(S["hstd_ready"], j + 1)
                link(dve.reciprocal(rinv[:, :], hstd[j]))
                pair = qg[:, 2 * j:2 * j + 2, :]
                link(rotated(pair, two(2 + j), 2, pair, "cos1", "sin1"))
                tt(pair, pair, rinv[:, :].rearrange("p (a t) -> p a t", a=2), ALU.mult)\
                    .then_inc(S["qn_ready"], 1)
                dve.wait_ge(S["qn_ready"], j + 1)
            dve.wait_ge(S["rot_mm"], 3)
            dve.wait_ge(S["hstd_ready"], 3)
            link(dve.reciprocal(rinv[:, 0:T], hstd[2]))
            link(rotated(qg[:, 4:5, :], PS[4][:, T:2 * T].unsqueeze(1), 1, qg[:, 4:5, :], "cos1", "sin1"))
            mark(tt(kz[0:64, 0, :], qg[0:64, 4, :], rinv[0:64, 0:T], ALU.mult))
            tt(kz[64:128, 1, :], qg[64:128, 4, :], rinv[64:128, 0:T], ALU.mult).then_inc(S["qn_ready"], 1)

            dve.wait_ge(S["lgsq_ready"], 1)
            lg_, x_ = lgate[:, :, :], gtmp[:, :, :]
            link(tt(sq[:, :, :], rr[:, :, :], rr[:, :, :], ALU.mult))
            stt(th[:, :, :], sq[:, :, :], 1.0, th[:, :, :], ALU.add, ALU.mult).then_inc(S["m_ready"], 1)
            link(ts(x_, x_, 0.044715, 1.0, ALU.mult, ALU.add))
            tt(x_, x_, lg_, ALU.mult).then_inc(S["ginner_ready"], 1)
            bt = ii[:, :, :].rearrange("p (d c) t -> p d c t", d=2)
            link(tt(bt, bt, xc[:, :, :].unsqueeze(1).broadcast_to((P, 2, 4, T)), ALU.mult))
            dve.wait_ge(S["mult_ready"], 1)
            link(tt(ii[:, :, :], ii[:, :, :], th[:, :, :], ALU.mult))

            def lru_tail(a):
                if a < 4:
                    c = a
                    dve.tensor_tensor_scan(th[:, c, :], rr[:, c, :], ii[:, c, :], 0.0, ALU.mult, ALU.add)
                    mark(dve.tensor_tensor_scan(th[:, 4 + c, ::-1], rr[:, 4 + c, ::-1], ii[:, 4 + c, ::-1], 0.0,
                                                ALU.mult, ALU.add))
                if a == 4:
                    dve.wait_ge(S["gsig_ready"], 1)
                    mark(tt(lg_, lg_, x_, ALU.mult))
                    settle()
                    link(tt(xc[:, :, :], th[:, 0:4, :], th[:, 4:8, :], ALU.add))
                    tt(xc[:, :, :], xc[:, :, :], lg_, ALU.mult).then_inc(S["lru_ready"], 1)

                if a == 3:
                    dve.wait_ge(S["units_done"], AT["ck0"] + 4)
                    memory(1)
                if a == 4:
                    key_reciprocals(0)
                if a in (5, 6):
                    scale_keys(0, a - 5, 1)

            def key_reciprocals(l):
                dve.wait_ge(S["kstd_ready"], l + 1)
                part = ksum[:, 8 * l:8 * l + 8]
                dve.reciprocal(part, part).then_inc(S["krec_ready"], 1)

            def scale_keys(l, i, bank):
                dve.wait_ge(S["kb_mm"], 2 * l + i + 1)
                for h in range(2):
                    c = 4 * i + 2 * h
                    o = tt(kst[l][:, c:c + 2, :], kst[l][:, c:c + 2, :], over(PS[bank][:, h * T:(h + 1) * T], 2),
                           ALU.mult)
                o.then_inc(S["kn_ready"], 1)

            heads(0, 8, 0.125, between=lru_tail)
            key_reciprocals(1)
            scale_keys(1, 0, 1)
            scale_keys(1, 1, 3)
            dve.wait_ge(S["ostd_ready"], 1)
            link(dve.reciprocal(rinv[:, :], std[:, :]))
            for k in range(C):
                src, g = (at1, "attn_g") if k < 4 else (xc, "lru_g")
                stt(xn[:, k, :], src[:, k % 4, :], V(g, k % 4), rinv[:, T * (k // 4):T * (k // 4) + T],
                    ALU.mult, ALU.mult).then_inc(S["mixed_ready"], 1)
            residual(AT["w_out"])
            norm(1, "norm2", xn)

            dve.wait_ge(S["rout_mm"], 1)
            dve.wait_ge(S["pads_ready"], 6)
            tt(lg[:, :, 0:E], PS[5][:, 0:2 * E].rearrange("p (a e) -> p a e", a=2), over(br[:, :], 2), ALU.add)\
                .then_inc(S["lg_ready"], 1)
            dve.wait_ge(S["lg_ready"], 1)
            for tk in range(2):
                mark(dve.max(m8[:, tk, :], lg[:, tk, 0:E]))
            settle()
            ts(gs[:, 0:2].unsqueeze(2), m8[:, :, 0:1], -1.0, None, ALU.mult).then_inc(S["lg_ready"], 1)
            link(dve.memset(m8[:, :, 4:8], 3.0e38))
            for tk in range(2):
                mark(dve.match_replace(lg2[:, tk, 0:E + 4], m8[:, tk, :], lg[:, tk, 0:E + 4], FAR))
            settle()
            ts(msk[:, :, :], lg2[:, :, 0:E], 0.9 * FAR, None, ALU.is_le).then_inc(S["mask_ready"], 1)
            dve.wait_ge(S["mask_ready"], 1)
            dve.wait_ge(S["gex_ready"], 1)
            link(tt(exr[:, :, :], exr[:, :, :], msk[:, :, :], ALU.mult))
            link(dve.tensor_reduce(gs[:, 2:4], exr[:, :, :], AX, ALU.add))
            link(dve.reciprocal(gs[:, 2:4], gs[:, 2:4]))
            tt(G[:, :, 0:E], exr[:, :, :], along(gs[:, 2:4], E), ALU.mult).then_inc(S["lg_ready"], 1)
            dve.wait_ge(S["cnt_mm"], 1)
            cp = PS[5][:, 64:64 + 3 * E].rearrange("p (a e) -> p a e", a=3)
            link(stt(key[:, :, 0:E], cp[:, 0:2, :], 1.0, msk[:, :, :], ALU.add, ALU.mult))
            link(ts(key[:, :, 0:E], key[:, :, 0:E], -1.0, None, ALU.add))
            nar = exr[:, 0, :]
            link(ts(nar, cp[:, 2, :], float(NARROW), None, ALU.is_le))
            link(tt(msk[:, :, :], msk[:, :, :], over(nar, 2), ALU.mult))
            link(stt(key2[:, :, 0:E], key[:, :, 0:E], float(NARROW + 1), msk[:, :, :], ALU.add, ALU.mult))
            link(ts(key2[:, :, 0:E], key2[:, :, 0:E], -1.0, None, ALU.add))
            mark(dve.tensor_copy(load[:, :], cp[:, 2, :]))
            link(dve.tensor_reduce(cnt[:, 0:1], cp[:, 2, :], AX, ALU.max))
            dve.tensor_copy(flag[:, :], cnt[:, 0:1]).then_inc(S["flag_ready"], 1)

            def select(n, e, b, general, step):
                io = tb("iota")[:, b * WIDE:(b + 1) * WIDE]
                for tk in range(2):
                    o = ts(sel[:, tk, :], io, key[:, tk, bass.ds(e, 1)], None, ALU.is_equal)
                    if general:
                        step.mark(o)
                    else:
                        step.link(o)
                        step.mark(stt(sel[:, tk, :], io, key2[:, tk, bass.ds(e, 1)], sel[:, tk, :],
                                      ALU.is_equal, ALU.add))
                step.settle()
                for tk in range(2):
                    last = ts(selg[:, tk, :], sel[:, tk, :], G[:, tk, bass.ds(e, 1)], None, ALU.mult)
                last.then_inc(M["sel_ready"], 1)

            def swiglu(n, e, w, wide, step):
                r_ = ROUND[w]
                shape = "p (k c h) -> p k c h"
                mb = mbias[:, bass.ds(e * 16, 16)].rearrange(shape, k=2, c=4)
                bias = [mb[:, kind, :, w:w + 1] if wide else mb[:, kind, :, :] for kind in range(2)]

                def cast(v):
                    return v.rearrange("p (c h n) -> p c h n", c=4, h=1 if wide else 2)

                def spread(v):
                    return v.unsqueeze(3).broadcast_to((P, 4, 1, WIDE) if wide else (P, 4, 2, NARROW))

                dve.wait_ge(M["tg_mm" + r_], n + 1)
                step.link(tt(cast(ge), cast(PS[6][:, :]), spread(bias[0]), ALU.add))
                ts(ge, ge, 7.0, None, ALU.min).then_inc(M["sig_in" + r_], 1)
                dve.wait_ge(M["tu_mm" + r_], n + 1)
                step.link(tt(cast(ue), cast(PS[7][:, :]), spread(bias[1]), ALU.add))
                step.link(ts(ue, ue, 7.0, -7.0, ALU.min, ALU.max))
                step.link(stt(ue, ue, 1.0, ge, ALU.add, ALU.mult))
                dve.wait_ge(M["sig_ready" + r_], n + 1)
                tt(hT[w][:, :, :], ue.rearrange("p (c n) -> p c n", c=4),
                   sg.rearrange("p (c n) -> p c n", c=4), ALU.mult).then_inc(M["h_ready" + r_], 1)
                dve.wait_ge(M["h_ready" + r_], n + 1)

            def dve_pass(n, e, nb, ne, wide, general, chain_at, chain2_at):
                step = Chain(dve, M["chain"], chain_at)
                step2 = Chain(dve, M["chain2"], chain2_at)
                dve.wait_ge(M["selT_mm"], n + 1)
                dve.wait_ge(M["xs_mm"], n + 1)
                select(n + 1, ne, nb, general, step)
                swiglu(n, e, 0, wide, step)
                if wide:
                    swiglu(n, e, 1, wide, step2)
                    assert step2.n == STEPS2
                else:
                    dve.sem_inc(M["chain2"], STEPS2)
                    dve.sem_inc(M["sig_in2"], 1)
                    dve.sem_inc(M["h_ready2"], 1)
                dve.sem_inc(M["passed"], 1)
                assert step.n == (STEPS_G if general else STEPS)

            STEPS, STEPS_G, STEPS2 = 8, 6, 4
            dve.wait_ge(S["flag_ready"], 1)
            dve.wait_ge(S["router_loaded"], 48)
            most = dve.value_load(flag[0:1, 0:1], min_val=0, max_val=T)
            with dve.If(most < WIDE + 1):
                first = Chain(dve, M["chain"])
                select(0, 0, 0, False, first)
                with dve.Fori(0, E) as e:
                    at = e * STEPS + first.n
                    with dve.If(dve.value_load(load[0:1, bass.ds(e, 1)], min_val=0, max_val=T) < NARROW + 1):
                        dve_pass(e, e, 0, e + 1, False, False, at, e * STEPS2)
                    with dve.Else():
                        dve_pass(e, e, 0, e + 1, True, False, at, e * STEPS2)
                    dve.nop()
            with dve.Else():
                first = Chain(dve, M["chain"])
                select(0, 0, 0, True, first)
                with dve.Fori(0, E) as e:
                    for b in range(BLOCKS):
                        n = e * BLOCKS + b
                        dve_pass(n, e, (b + 1) % BLOCKS, e + (b + 1) // BLOCKS, True, True,
                                 n * STEPS_G + first.n, n * STEPS2)

            norm(2, "final", xT)
            norm(3, "mix0", xn)

            for j in range(5):
                dve.wait_ge(S["iqrot_mm"], j + 1)
                if j < 4:
                    pair = iqr[:, 2 * j:2 * j + 2, :]
                    cs = iqt
                    if j:
                        dve.wait_ge(S["iqn_ready"], j)
                    link(tt(cs[:, :, :], pair, over(tb("cos3"), 2), ALU.mult))
                    tt(tsq[:, 0, :].rearrange("p (a t) -> p a t", a=2), two(6 + j % 2), over(tb("sin3"), 2),
                       ALU.mult).then_inc(S["iqrot_read"], 1)
                    dve.wait_ge(S["iqrot_read"], j + 1)
                    tt(pair, cs[:, :, :], tsq[:, 0, :].rearrange("p (a t) -> p a t", a=2), ALU.add)\
                        .then_inc(S["iqn_ready"], 1)
                else:
                    dve.wait_ge(S["iqn_ready"], 4)
                    link(tt(iqt[:, 0, :], tv[:, 0, 0:T], tb("cos3"), ALU.mult))
                    tt(iqt[:, 1, :], PS[6][:, 0:T], tb("sin3"), ALU.mult).then_inc(S["iqrot_read"], 1)
                    dve.wait_ge(S["iqrot_read"], 5)
                    dve.wait_ge(S["pads_ready"], 8)
                    tt(iz[0:64, 0, :], iqt[0:64, 0, :], iqt[0:64, 1, :], ALU.add)
                    tt(iz[64:128, 1, :], iqt[64:128, 0, :], iqt[64:128, 1, :], ALU.add)\
                        .then_inc(S["iqn_ready"], 1)
            dve.wait_ge(S["iw_ready"], 1)

            def add_index(h):
                dve.wait_ge(S["relu_ready"], h + 1)
                for b in range(2):
                    to, src = sc[:, b, 0:(b + 1) * P], rl[h % 2][:, b, 0:(b + 1) * P]
                    if h == 0:
                        last = ts(to, src, iw[:, b, 0:1], None, ALU.mult)
                    else:
                        if b == 0:
                            dve.wait_ge(S["relu_used"], h)
                        last = stt(to, src, iw[:, b, h:h + 1], to, ALU.mult, ALU.add)
                last.then_inc(S["relu_used"], 1)

            for j in range(4):
                for h in range(4 * j, 4 * j + 4):
                    add_index(h)
                dve.wait_ge(S["drot_mm"], j + 1)
                dve.wait_ge(S["dstd_ready"], j + 1)
                link(dve.reciprocal(rinv[:, :], std[:, :]))
                pair = dqk[:, 2 * j:2 * j + 2, :]
                link(rotated(pair, two(5), 2, pair, "cos2", "sin2"))
                tt(pair, pair, rinv[:, :].rearrange("p (a t) -> p a t", a=2), ALU.mult)\
                    .then_inc(S["dqn_ready"], 1)
            dve.wait_ge(S["relu_used"], 16)
            far = tb("far").rearrange("p (b t) -> p b t", b=2)
            mark(dve.memset(sc[:, 0, P:T], FAR))
            for b in range(2):
                keys = (b + 1) * P
                mark(tt(sc[:, b, 0:keys], sc[:, b, 0:keys], far[:, b, 0:keys], ALU.add))
            settle()
            for rnd in range(ROUNDS):
                for b in range(2):
                    mark(dve.max(m8b[:, b, :], sc[:, b, 0:(b + 1) * P]))
                settle()
                for b in range(2):
                    seen = sc[:, b, 0:(b + 1) * P]
                    mark(dve.match_replace(seen, m8b[:, b, :], seen, TAKEN))
                settle()
            link(ts(pen[:, :, :], sc[:, :, :], 0.5 * (FAR + TAKEN), 1.0e30, ALU.is_le, ALU.mult))
            link(stt(pen[:, :, :], pen[:, :, :], -1.0e30, tb("far").rearrange("p (b t) -> p b t", b=2),
                     ALU.add, ALU.add))
            dve.wait_ge(S["u_ready"], 2)
            link(tt(w1[:, :, 1:272], up[:, :, 1:272], up[:, :, 0:271], ALU.add))
            link(tt(w2[:, 1:4, 3:272], w1[:, 1:4, 3:272], w1[:, 1:4, 1:270], ALU.add))
            link(tt(w1[:, 2:4, 7:272], w2[:, 2:4, 7:272], w2[:, 2:4, 3:268], ALU.add))
            link(tt(w2[:, 3:4, 15:272], w1[:, 3:4, 15:272], w1[:, 3:4, 7:264], ALU.add))
            rc = tb("rcount").rearrange("p (g t) -> p g t", g=4)
            for g in range(4):
                w = w2 if g % 2 else w1
                mark(tt(iqt[:, 0, 16 * g:16 * g + 16], w[:, g, 16:32], rc[:, g, :], ALU.mult))
                link(stt(iqt[:, 1, :], w[:, g, 16:272], 0.5 ** (g + 1), up[:, g, 16:272], ALU.mult, ALU.subtract))
                mark(dve.tensor_copy(w1[:, g, 16:256], iqt[:, 1, 16:256]))
                tt(w1[:, g, 0:16], iqt[:, 0, 16 * g:16 * g + 16], up[:, g, 16:32], ALU.subtract)\
                    .then_inc(S["pooled_ready"], 1)
                dve.wait_ge(S["pooled_ready"], g + 1)
            heads(8, 4, float(P) ** -0.5, sparse=True)
            residual(AT["ab_out"])

            def cross(l):
                norm(4 + 3 * l, f"cross{l}", xn)
                dve.wait_ge(S["cqstd_ready"], l + 1)
                link(dve.reciprocal(rq[:, :], rq[:, :]))
                link(ts(rq[:, :], rq[:, :], 1.0 / 16, None, ALU.mult))
                heads(12 + 4 * l, 4, rq)
                residual(AT[f"co{l}"])
                norm(5 + 3 * l, f"ffn{l}", xn)

            def ffn(l):
                for g in range(NG):
                    n = NG * l + g
                    dve.wait_ge(S["f_sig"], n + 1)
                    gb, ub = two(4 + 2 * (g % 2)), two(5 + 2 * (g % 2))
                    link(tt(fs[g % 2][:, :, :], gb, fs[g % 2][:, :, :], ALU.mult))
                    dve.wait_ge(S["units_done"], AT[f"ffn{l}"] + ffn_gate_unit(g) + 2)
                    tt(fh[g % 2][:, :, :], ub, fs[g % 2][:, :, :], ALU.mult).then_inc(S["f_h"], 1)
                dve.wait_ge(S["units_done"], AT[f"ffn{l}"] + 3 * NG)
                for j in range(4):
                    tt(xT[:, 2 * j:2 * j + 2, :], two(j), xT[:, 2 * j:2 * j + 2, :], ALU.add)\
                        .then_inc(S["res_ready"], 1)

            cross(0)
            ffn(0)
            norm(6, "mix1", xn)
            dve.wait_ge(S["pads_ready"], 9)
            def gated(j):
                dve.wait_ge(S["conv_sig"], j + 1)
                stt(hp[:, j, 30:30 + T], two(j % 4)[:, 0, :], V("cin_b", j), csg[:, j % 2, :], ALU.add, ALU.mult)\
                    .then_inc(S["hp_ready"], 1)

            gated(0)
            gated(1)
            steps, gates = 0, 2
            last = {}
            for first in (0, 2, 4):
                for t in range(TAPS):
                    for c in (first, first + 1):
                        w = V("dw", c * TAPS + t)
                        if t == 0:
                            dve.wait_ge(S["hp_ready"], c + 1)
                            mark(ts(hc[:, c, :], hp[:, c, 0:T], w, V("dw_b", c), ALU.mult, ALU.add))
                        else:
                            dve.wait_ge(S["dve_chain"], last[c])
                            o = stt(hc[:, c, :], hp[:, c, t:t + T], w, hc[:, c, :], ALU.mult, ALU.add)
                            if t < TAPS - 1:
                                mark(o)
                            else:
                                o.then_inc(S["hc_dve"], 1)
                        last[c] = chain.n
                        steps += 1
                        if steps % 18 == 0 and gates < C:
                            gated(gates)
                            gates += 1
            assert gates == C
            dve.wait_ge(S["lnsum_mm"], 1)
            dve.wait_ge(S["hc_dve"], 6)
            dve.wait_ge(S["hc_pe"], 2)
            link(ts(rinv[:, 0:T], PS[0][:, 0:T], 1.0 / D, None, ALU.mult))
            for j in range(4):
                pair = hc[:, 2 * j:2 * j + 2, :]
                tt(pair, pair, over(rinv[:, 0:T], 2), ALU.subtract).then_inc(S["lnd_ready"], 1)
            dve.wait_ge(S["lnstd_ready"], 1)
            link(dve.reciprocal(rinv[:, 0:T], std[:, 0:T]))
            for c in range(C):
                stt(hc[:, c, :], hc[:, c, :], V("ln_g", c), rinv[:, 0:T], ALU.mult, ALU.mult)\
                    .then_inc(S["lnz_ready"], 1)
            for c in range(C):
                dve.wait_ge(S["lnsig_ready"], c + 1)
                stt(yc[:, c, :], hc[:, c, :], V("ln_b", c), sq[:, c, :], ALU.add, ALU.mult)\
                    .then_inc(S["yc_ready"], 1)
            residual(AT["conv_out"])
            cross(1)
            ffn(1)



def columns(v):
    return v.reshape(-1, P).T


def stationary_units(w):
    n = w.shape[1] // 256
    return w.reshape(C, P, n, 2, P).transpose(2, 1, 3, 0, 4).reshape(n, P, UNIT)


def row_units(w):
    kk = UNIT // w.shape[1]
    n = w.shape[0] // (P * kk)
    return w.reshape(n, kk, P, w.shape[1]).transpose(0, 2, 1, 3).reshape(n, P, UNIT)


def lay_out_stream(a):
    s = np.zeros((N_UNITS, P, UNIT), np.float32)

    def put(name, units):
        s[AT[name]:AT[name] + len(units)] = units

    w = a["w_in"][0]
    put("lru_x", stationary_units(w[:, 768:1280]))
    put("q", stationary_units(w[:, 0:512].reshape(D, 2, 4, 64).transpose(0, 2, 1, 3).reshape(D, 512)))
    put("kv", stationary_units(w[:, 512:768]))
    put("lru_gate", stationary_units(w[:, 1280:1792]))
    gates = s[AT["lru_w"]].reshape(P, 2, 2, 4, P)
    for kind, name in enumerate(("lru_wa", "lru_wi")):
        for d in range(2):
            for c in range(4):
                for h in range(2):
                    r = slice(64 * h, 64 * h + 64)
                    gates[r, d, kind, c, r] = a[name][0, d, 2 * c + h]
    w = a["w_out"][0]
    w = np.concatenate([w[:512].reshape(2, 4, 64, D).transpose(1, 0, 2, 3).reshape(512, D), w[512:]])
    put("w_out", stationary_units(w))
    moe = s[AT["moe"]:AT["moe"] + 12 * E].reshape(E, 12, P, UNIT)
    for e in range(E):
        for i, name in enumerate(("w_gate", "w_up", "w_down")):
            moe[e, 4 * i:4 * i + 4] = row_units(a[name][0, e])
    w = a["w_in_ab_2"][0]
    put("dq", stationary_units(w[:, 0:512]))
    put("dk", stationary_units(w[:, 512:1024]))
    put("dv", row_units(w[:, 1024:1536]))
    put("u", stationary_units(w[:, 1536:2048]))
    put("iq", stationary_units(w[:, 2048:3072]))
    one = s[AT["ikiw"]]
    ik = w[:, 3088:3152]
    one[:, 0:D] = np.concatenate([ik, ik], 1).reshape(C, P, P).transpose(1, 0, 2).reshape(P, D)
    one[:, D:D + 16 * C] = w[:, 3072:3088].reshape(C, P, 16).transpose(1, 0, 2).reshape(P, 16 * C)
    s[AT["pool"]][:, 0:4 * P] = a["pool_w_2"][0].transpose(1, 0, 2).reshape(P, 4 * P)
    put("ab_out", stationary_units(a["w_out_ab_2"][0]))
    put("conv_in", stationary_units(a["conv_w_in_2"][0].reshape(D, 2, C, P).transpose(0, 2, 1, 3)
                                    .reshape(D, 2 * D)))
    put("conv_out", stationary_units(a["conv_w_out_2"][0]))
    for l in range(2):
        put(f"ck{l}", stationary_units(a["cross_wk_2"][l]))
        put(f"cv{l}", row_units(a["cross_wv_2"][l]))
        put(f"cq{l}", stationary_units(a["cross_wq_2"][l]))
        put(f"co{l}", stationary_units(a["cross_wo_2"][l]))
        f = s[AT[f"ffn{l}"]:AT[f"ffn{l}"] + 3 * NG]
        g, u = (stationary_units(a[n][l]) for n in ("ffn_w_gate_2", "ffn_w_up_2"))
        d = row_units(a["ffn_w_down_2"][l])
        for i in range(NG):
            f[ffn_gate_unit(i)] = g[i]
            f[ffn_gate_unit(i) + 1] = u[i]
            f[min(3 * i + 4, 3 * NG - 1)] = d[i]
    return s


def lay_out_vectors(a):
    v = np.zeros((P, NV), np.float32)

    def put(name, m):
        v[:, VAT[name]:VAT[name] + m.shape[1]] = m

    for name, value in (("norm1", a["norm1_g"][0]), ("norm2", a["norm2_g"][0]), ("final", a["final_g"]),
                        ("mix0", a["norm_mix_2"][0]), ("mix1", a["norm_mix_2"][1]),
                        ("cross0", a["norm_cross_2"][0]), ("cross1", a["norm_cross_2"][1]),
                        ("mem0", a["norm_mem_2"][0]), ("mem1", a["norm_mem_2"][1]),
                        ("ffn0", a["norm_ffn_2"][0]), ("ffn1", a["norm_ffn_2"][1]),
                        ("gq", np.concatenate([a["q_norm_g"][0]] * 2)),
                        ("gk", np.concatenate([a["k_norm_g"][0]] * 2)),
                        ("conv_b", a["conv_b"][0]), ("lam", a["lru_lam"][0]),
                        ("lru_b", np.concatenate([a["lru_ba"][0].ravel(), a["lru_bi"][0].ravel()])),
                        ("attn_g", a["attn_out_g"][0].reshape(2, 4, 64).transpose(1, 0, 2)),
                        ("lru_g", a["lru_out_g"][0]), ("aq", a["a_q_norm_2"][0]), ("ak", a["a_k_norm_2"][0]),
                        ("pool_scale", a["pool_scale_2"][0]), ("cin_b", a["conv_b_in_2"][0]),
                        ("dw_b", a["conv_dw_b_2"][0]), ("ln_g", a["conv_ln_g_2"][0]),
                        ("ln_b", a["conv_ln_b_2"][0]), ("cqg0", a["cross_q_norm_2"][0]),
                        ("cqg1", a["cross_q_norm_2"][1]), ("ckg0", a["cross_k_norm_2"][0]),
                        ("ckg1", a["cross_k_norm_2"][1])):
        put(name, columns(value))
    put("conv_w", a["conv_w"][0].reshape(4, 4, P).transpose(2, 1, 0).reshape(P, 16))
    put("dw", a["conv_dw_w_2"][0].reshape(TAPS, C, P).transpose(2, 1, 0).reshape(P, C * TAPS))
    v[:, VAT["eps5"]] = 1e-5
    v[:, VAT["eps6"]] = 1e-6
    return v


def rotary(heads_at, half, inv, positions):
    cos, sin, rot = np.ones((P, T), np.float32), np.zeros((P, T), np.float32), np.zeros((P, P), np.float32)
    for start, pos in zip(heads_at, positions):
        ang = inv[:, None].astype(np.float32) * pos[None, :].astype(np.float32)
        for i in range(half):
            lo, hi = start + i, start + half + i
            cos[lo] = cos[hi] = np.cos(ang[i])
            sin[lo] = sin[hi] = np.sin(ang[i])
            rot[hi, lo] = -1.0
            rot[lo, hi] = 1.0
    return cos, sin, rot


def lay_out_tables():
    t = np.zeros((P, NT), np.float32)

    def put(name, m):
        t[:, TAT[name]:TAT[name] + m.shape[1]] = m

    tok = np.arange(T)
    f = np.float32
    axial = f(10000.0) ** (-np.arange(16, dtype=f) / f(16))
    inv2 = f(500000.0) ** (-np.arange(16, dtype=f) * f(2.0) / f(32))
    inv3 = f(500000.0) ** (-np.arange(8, dtype=f) * f(2.0) / f(16))
    for n, (cos, sin, rot) in enumerate((rotary((0, 32, 64, 96), 16, axial, (tok // 64, tok % 64) * 2),
                                         rotary((0,), 16, inv2, (tok,)),
                                         rotary((0, 64), 8, inv3, (tok, tok))), 1):
        put(f"cos{n}", cos)
        put(f"sin{n}", sin)
        put(f"rot{n}", rot)
    i = np.arange(P)
    put("ident", np.eye(P, dtype=f))
    put("ones", np.ones((P, P), f))
    put("heads", (i[:, None] // 64 == i[None, :] // 64).astype(f))
    put("before", (i[:, None] < i[None, :]).astype(f))
    put("iota", np.broadcast_to(tok.astype(f), (P, T)))
    q = i[:, None, None] + P * np.arange(2)[None, :, None]
    put("far", np.where(tok[None, None, :] > q, f(FAR), f(0)).reshape(P, 2 * T))
    w = 2 ** np.arange(1, 5)[:, None]
    put("rcount", np.broadcast_to((f(1) / np.minimum(np.arange(16)[None, :] + 1, w).astype(f)).reshape(1, 64),
                                  (P, 64)))
    return t


def token_chunks(m):
    return np.ascontiguousarray(m[0].T.reshape(C, P, T).transpose(1, 0, 2))


def kernel(**inputs):
    import concourse.bacc as _bacc
    from concourse.bass_utils import run_bass_kernel_spmd as _run

    a = {k: np.asarray(v) for k, v in inputs.items()}
    gate, up = (a[n][0].reshape(E, 2, 4, P) for n in ("b_gate", "b_up"))
    arrays = {
        "x": token_chunks(a["x"]),
        "mem": token_chunks(a["mem_2"]).reshape(P, UNIT),
        "stream": lay_out_stream(a),
        "vecs": lay_out_vectors(a),
        "tables": lay_out_tables(),
        "moe_b": np.ascontiguousarray(np.stack([gate, up], 1).transpose(4, 0, 1, 3, 2).reshape(P, E * 16)),
        "b_down": np.ascontiguousarray(a["b_down"][0]),
        "w_router": np.ascontiguousarray(a["w_router"][0].reshape(C, P, E).transpose(1, 0, 2)),
        "b_router": np.ascontiguousarray(np.broadcast_to(a["b_router"][0], (P, E))),
    }
    nc = _bacc.Bacc("TRN2", target_bir_lowering=False, num_devices=1)
    args = [nc.dram_tensor(f"in_{n}", v.shape, mybir.dt.from_np(v.dtype), kind="ExternalInput").ap()
            for n, v in arrays.items()]
    out = nc.dram_tensor("out_y", (P, C, T), F32, kind="ExternalOutput").ap()
    mem_kv = nc.dram_tensor("mem_kv", (4, P, UNIT), F32, kind="Internal").ap()
    build(nc, *args, mem_kv, out)
    r = _run(nc, [{f"in_{n}": v for n, v in arrays.items()}], core_ids=[0])
    y = r.results[0]["out_y"]
    return np.ascontiguousarray(y.transpose(1, 0, 2).reshape(D, T).T)[None]
```
